# Optimizing a Trainium2 kernel written in Bass

```python
import jax
import jax.numpy as jnp
from jax import lax
import numpy as np

D_MODEL = 1024
BATCH = 1
SEQ = 256
DEPTH = 1
DEC_BATCH = 8
DEC_SEQ = 8
PAST_LEN = 1024
PAGE_SIZE = 128

HEAD_DIM = 64
N_HEADS = D_MODEL // HEAD_DIM
A_HEADS = N_HEADS // 2
B_HEADS = N_HEADS - A_HEADS
B_KV_HEADS = 2
B_GROUP = B_HEADS // B_KV_HEADS
A_PATTERNS = ((128, 1), (512, 4), (2048, 16))
A_BUF_MAX = 2048
CMP_LEN = 32
CMP_STRIDE = 16
CMP_HID = 256
SEL_BLOCK = 64
SEL_TOPN = 16
WIN = 512
BAND_BLOCK = 128
SEL_QBLOCK = 16
ROPE_THETA = 500000.0
ROT_DIM = HEAD_DIM // 4
ATTN_SCALE = HEAD_DIM ** -0.5
PEER_HEADS = 8
PEER_KEYS = 128
PEER_EXPERTS = PEER_KEYS * PEER_KEYS
PEER_DK = 256
PEER_TOPK = 16
PEER_CHUNK = 256
LN_EPS = 1e-5
DN_ALPHA = (2 * DEPTH) ** 0.25
DN_BETA = (8 * DEPTH) ** -0.25
PROJ_SIZES = (A_HEADS * HEAD_DIM,) * 3 + (B_HEADS * HEAD_DIM,) + (B_KV_HEADS * HEAD_DIM,) * 6 + (3 * B_HEADS,)
PROJ_DIM = sum(PROJ_SIZES)

kernel_name = 'hymba_longnet_nsa_peer'

def split_columns(h):
    parts = []
    start = 0
    for size in PROJ_SIZES:
        parts.append(h[..., start:start + size])
        start += size
    return parts

def rope(x, pos):
    half = ROT_DIM // 2
    inv = jnp.power(ROPE_THETA, -jnp.arange(half, dtype=jnp.float32) / half)
    ang = pos.astype(jnp.float32)[:, None] * inv[None, :]
    cos = jnp.cos(ang)[:, None, :]
    sin = jnp.sin(ang)[:, None, :]
    xf = x.astype(jnp.float32)
    x1 = xf[..., :half]
    x2 = xf[..., half:ROT_DIM]
    out = jnp.concatenate([x1 * cos - x2 * sin, x2 * cos + x1 * sin, xf[..., ROT_DIM:]], axis=-1)
    return out.astype(x.dtype)

def layer_norm(x, g, b):
    xf = x.astype(jnp.float32)
    mu = jnp.mean(xf, axis=-1, keepdims=True)
    var = jnp.mean(jnp.square(xf - mu), axis=-1, keepdims=True)
    return ((xf - mu) * lax.rsqrt(var + LN_EPS) * g + b).astype(x.dtype)

def project(x, pos, w_in):
    b, t, _ = x.shape
    h = jnp.einsum('btd,de->bte', x, w_in)
    qa, ka, va, qb, kc, vc, ks, vs, kw, vw, gl = split_columns(h)

    def heads(z, n):
        return z.reshape(b, t, n, HEAD_DIM)

    qa = rope(heads(qa, A_HEADS), pos)
    ka = rope(heads(ka, A_HEADS), pos)
    va = heads(va, A_HEADS)
    qb = heads(qb, B_HEADS)
    qb_rot = rope(qb, pos).reshape(b, t, B_KV_HEADS, B_GROUP, HEAD_DIM)
    qb_raw = qb.reshape(b, t, B_KV_HEADS, B_GROUP, HEAD_DIM)
    kc = heads(kc, B_KV_HEADS)
    vc = heads(vc, B_KV_HEADS)
    ks = rope(heads(ks, B_KV_HEADS), pos)
    vs = heads(vs, B_KV_HEADS)
    kw = rope(heads(kw, B_KV_HEADS), pos)
    vw = heads(vw, B_KV_HEADS)
    return qa, ka, va, qb_raw, qb_rot, kc, vc, ks, vs, kw, vw, gl

def banded_attention(q, k, v, window):
    n, l, kvh, g, hd = q.shape
    nb = l // BAND_BLOCK
    nprev = window // BAND_BLOCK
    span = (nprev + 1) * BAND_BLOCK
    pad = ((0, 0), (nprev * BAND_BLOCK, 0), (0, 0), (0, 0))
    kp = jnp.pad(k, pad)
    vp = jnp.pad(v, pad)
    qi = jnp.arange(BAND_BLOCK)[:, None]
    kj = jnp.arange(span)[None, :]
    dist = nprev * BAND_BLOCK + qi - kj
    in_band = (dist >= 0) & (dist <= window)

    def block(bi):
        qb = lax.dynamic_slice_in_dim(q, bi * BAND_BLOCK, BAND_BLOCK, axis=1)
        kb = lax.dynamic_slice_in_dim(kp, bi * BAND_BLOCK, span, axis=1)
        vb = lax.dynamic_slice_in_dim(vp, bi * BAND_BLOCK, span, axis=1)
        kpos = (bi - nprev) * BAND_BLOCK + kj
        mask = in_band & (kpos >= 0)
        s = jnp.einsum('nqhgd,nkhd->nhgqk', qb, kb, preferred_element_type=jnp.float32) * ATTN_SCALE
        s = jnp.where(mask, s, -jnp.inf)
        lse = jax.nn.logsumexp(s, axis=-1)
        p = jnp.exp(s - lse[..., None])
        o = jnp.einsum('nhgqk,nkhd->nqhgd', p, vb.astype(jnp.float32))
        return o, jnp.moveaxis(lse, 3, 1)

    o, lse = lax.map(block, jnp.arange(nb))
    o = jnp.moveaxis(o, 0, 1).reshape(n, l, kvh, g, hd)
    lse = jnp.moveaxis(lse, 0, 1).reshape(n, l, kvh, g)
    return o, lse

def combine_patterns(outs, lses):
    w = jax.nn.softmax(jnp.stack(lses, 0), axis=0)
    return jnp.einsum('pbth,pbthd->bthd', w, jnp.stack(outs, 0))

def dilated_attention_prompt(q, k, v):
    bsz, s, h, hd = q.shape
    outs, lses = [], []
    for window, dil in A_PATTERNS:
        span = window // dil
        s_pad = -(-s // (dil * BAND_BLOCK)) * dil * BAND_BLOCK
        ls = s_pad // dil

        def to_strided(z):
            z = jnp.pad(z, ((0, 0), (0, s_pad - s), (0, 0), (0, 0)))
            z = z.reshape(bsz, ls, dil, h, hd)
            return jnp.swapaxes(z, 1, 2).reshape(bsz * dil, ls, h, hd)

        o, lse = banded_attention(to_strided(q)[:, :, :, None], to_strided(k), to_strided(v), span)
        o = jnp.swapaxes(o[:, :, :, 0].reshape(bsz, dil, ls, h, hd), 1, 2).reshape(bsz, s_pad, h, hd)[:, :s]
        lse = jnp.swapaxes(lse[..., 0].reshape(bsz, dil, ls, h), 1, 2).reshape(bsz, s_pad, h)[:, :s]
        outs.append(o)
        lses.append(lse)
    return combine_patterns(outs, lses)

def dilated_attention_sample(q, k_buf, v_buf):
    t = q.shape[1]
    nbuf = k_buf.shape[1] - t
    outs, lses = [], []
    for window, dil in A_PATTERNS:
        j = jnp.arange(window // dil + 1)
        idx = nbuf + jnp.arange(t)[:, None] - dil * j[None, :]
        valid = idx >= 0
        idx = jnp.maximum(idx, 0)
        kg = k_buf[:, idx]
        vg = v_buf[:, idx]
        s = jnp.einsum('bthd,btjhd->bhtj', q, kg, preferred_element_type=jnp.float32) * ATTN_SCALE
        s = jnp.where(valid, s, -jnp.inf)
        lse = jax.nn.logsumexp(s, axis=-1)
        p = jnp.exp(s - lse[..., None])
        outs.append(jnp.einsum('bhtj,btjhd->bthd', p, vg.astype(jnp.float32)))
        lses.append(jnp.swapaxes(lse, 1, 2))
    return combine_patterns(outs, lses)

def gather_pages(pool, page_table):
    rows = pool[page_table]
    db, n_pages = page_table.shape
    return rows.reshape(db, n_pages * pool.shape[1], pool.shape[2], pool.shape[3])

def compress_rows(rows, pe, w1, w2):
    b, l, kvh, hd = rows.shape
    nc = (l - CMP_LEN) // CMP_STRIDE + 1
    idx = CMP_STRIDE * jnp.arange(nc)[:, None] + jnp.arange(CMP_LEN)[None, :]
    blk = rows[:, idx] + pe[:, None, :]
    blk = jnp.swapaxes(blk, 2, 3).reshape(b, nc, kvh, CMP_LEN * hd)
    return jax.nn.gelu(blk @ w1) @ w2

def compressed_attention(q, qpos, kc, vc):
    nc = kc.shape[1]
    blk_end = CMP_STRIDE * jnp.arange(nc) + (CMP_LEN - 1)
    mask = blk_end[None, :] <= qpos[:, None]
    s = jnp.einsum('bthgd,bchd->bhgtc', q, kc, preferred_element_type=jnp.float32) * ATTN_SCALE
    s = jnp.where(mask, s, -jnp.inf)
    m = jnp.max(s, axis=-1, keepdims=True)
    m = jnp.where(jnp.isfinite(m), m, 0.0)
    e = jnp.exp(s - m)
    p = e / jnp.maximum(jnp.sum(e, axis=-1, keepdims=True), jnp.finfo(jnp.float32).tiny)
    o = jnp.einsum('bhgtc,bchd->bthgd', p, vc.astype(jnp.float32))
    return o, p

def select_blocks(p_cmp, qpos, n_sel):
    nc = p_cmp.shape[-1]
    cstart = CMP_STRIDE * jnp.arange(nc)
    sstart = SEL_BLOCK * jnp.arange(n_sel)
    overlap = ((cstart[:, None] < sstart[None, :] + SEL_BLOCK)
               & (cstart[:, None] + CMP_LEN > sstart[None, :])).astype(jnp.float32)
    imp = jnp.einsum('bhgtc,cj->bhtj', p_cmp, overlap)
    qblk = qpos // SEL_BLOCK
    jj = jnp.arange(n_sel)[None, :]
    visible = jj <= qblk[:, None]
    forced = (jj == 0) | (jj == qblk[:, None]) | (jj == qblk[:, None] - 1)
    score = jnp.where(forced, jnp.inf, jnp.where(visible, imp, -jnp.inf))
    _, idx = lax.top_k(score, min(SEL_TOPN, n_sel))
    valid = idx <= qblk[None, None, :, None]
    return idx, valid

def to_blocks(rows, n_sel):
    b, l, kvh, hd = rows.shape
    rows = jnp.pad(rows, ((0, 0), (0, n_sel * SEL_BLOCK - l), (0, 0), (0, 0)))
    return jnp.transpose(rows.reshape(b, n_sel, SEL_BLOCK, kvh, hd), (0, 3, 1, 2, 4))

def selected_attention(q, qpos, k_blocks, v_blocks, idx, valid):
    b, t, kvh, g, hd = q.shape
    k_top = idx.shape[-1]
    bi = jnp.arange(b)[:, None, None, None]
    hi = jnp.arange(kvh)[None, :, None, None]
    kg = k_blocks[bi, hi, idx]
    vg = v_blocks[bi, hi, idx]
    kpos = idx[..., None] * SEL_BLOCK + jnp.arange(SEL_BLOCK)
    mask = valid[..., None] & (kpos <= qpos[None, None, :, None, None])
    s = jnp.einsum('bthgd,bhtksd->bhgtks', q, kg, preferred_element_type=jnp.float32) * ATTN_SCALE
    s = jnp.where(mask[:, :, None], s, -jnp.inf).reshape(b, kvh, g, t, k_top * SEL_BLOCK)
    p = jax.nn.softmax(s, axis=-1)
    vg = vg.reshape(b, kvh, t, k_top * SEL_BLOCK, hd).astype(jnp.float32)
    return jnp.einsum('bhgtn,bhtnd->bthgd', p, vg)

def selected_attention_chunked(q, qpos, k_blocks, v_blocks, idx, valid):
    b, t, kvh, g, hd = q.shape
    nq = t // SEL_QBLOCK
    k_top = idx.shape[-1]
    q_c = jnp.moveaxis(q.reshape(b, nq, SEL_QBLOCK, kvh, g, hd), 1, 0)
    pos_c = qpos.reshape(nq, SEL_QBLOCK)
    idx_c = jnp.moveaxis(idx.reshape(b, kvh, nq, SEL_QBLOCK, k_top), 2, 0)
    val_c = jnp.moveaxis(valid.reshape(b, kvh, nq, SEL_QBLOCK, k_top), 2, 0)

    def step(args):
        qc, pc, ic, vc = args
        return selected_attention(qc, pc, k_blocks, v_blocks, ic, vc)

    o = lax.map(step, (q_c, pos_c, idx_c, val_c))
    return jnp.moveaxis(o, 0, 1).reshape(b, t, kvh, g, hd)

def nsa_cmp_sel(q_raw, q_rot, qpos, kc_rows, vc_rows, ks_rows, vs_rows,
                pe_k, w1_k, w2_k, pe_v, w1_v, w2_v, chunked):
    kc = compress_rows(kc_rows, pe_k, w1_k, w2_k)
    vc = compress_rows(vc_rows, pe_v, w1_v, w2_v)
    o_cmp, p_cmp = compressed_attention(q_raw, qpos, kc, vc)
    n_sel = -(-ks_rows.shape[1] // SEL_BLOCK)
    idx, valid = select_blocks(p_cmp, qpos, n_sel)
    kb = to_blocks(ks_rows, n_sel)
    vb = to_blocks(vs_rows, n_sel)
    if chunked:
        o_sel = selected_attention_chunked(q_rot, qpos, kb, vb, idx, valid)
    else:
        o_sel = selected_attention(q_rot, qpos, kb, vb, idx, valid)
    return o_cmp, o_sel

def window_attention_sample(q, k_buf, v_buf):
    t = q.shape[1]
    nbuf = k_buf.shape[1] - t
    dist = (nbuf + jnp.arange(t))[:, None] - jnp.arange(nbuf + t)[None, :]
    mask = (dist >= 0) & (dist <= WIN)
    s = jnp.einsum('bthgd,bnhd->bhgtn', q, k_buf, preferred_element_type=jnp.float32) * ATTN_SCALE
    p = jax.nn.softmax(jnp.where(mask, s, -jnp.inf), axis=-1)
    return jnp.einsum('bhgtn,bnhd->bthgd', p, v_buf.astype(jnp.float32))

def gate_branches(gl, o_cmp, o_sel, o_win):
    b, t = gl.shape[:2]
    g = jax.nn.sigmoid(gl.astype(jnp.float32)).reshape(b, t, 3, B_KV_HEADS, B_GROUP, 1)
    return g[:, :, 0] * o_cmp + g[:, :, 1] * o_sel + g[:, :, 2] * o_win

def peer_ffn(x2d, wq, k1, k2, u_tab, v_tab):
    t, d = x2d.shape
    nchunk = -(-t // PEER_CHUNK)
    xp = jnp.pad(x2d, ((0, nchunk * PEER_CHUNK - t), (0, 0))).reshape(nchunk, PEER_CHUNK, d)
    half = PEER_DK // 2

    def chunk(xc):
        q = (xc @ wq).reshape(PEER_CHUNK, PEER_HEADS, PEER_DK)
        s1 = jnp.einsum('chd,hnd->chn', q[..., :half], k1, preferred_element_type=jnp.float32)
        s2 = jnp.einsum('chd,hnd->chn', q[..., half:], k2, preferred_element_type=jnp.float32)
        v1, i1 = lax.top_k(s1, PEER_TOPK)
        v2, i2 = lax.top_k(s2, PEER_TOPK)
        cand = (v1[..., :, None] + v2[..., None, :]).reshape(PEER_CHUNK, PEER_HEADS, PEER_TOPK * PEER_TOPK)
        cidx = (i1[..., :, None] * PEER_KEYS + i2[..., None, :]).reshape(PEER_CHUNK, PEER_HEADS, PEER_TOPK * PEER_TOPK)
        sc, sel = lax.top_k(cand, PEER_TOPK)
        experts = jnp.take_along_axis(cidx, sel, axis=-1).reshape(PEER_CHUNK, PEER_HEADS * PEER_TOPK)
        g = jax.nn.softmax(sc, axis=-1).reshape(PEER_CHUNK, PEER_HEADS * PEER_TOPK)
        hid = jax.nn.gelu(jnp.einsum('ced,cd->ce', u_tab[experts], xc, preferred_element_type=jnp.float32))
        y = jnp.einsum('ce,ced->cd', g * hid, v_tab[experts].astype(jnp.float32))
        return y.astype(xc.dtype)

    y = lax.map(chunk, xp)
    return y.reshape(nchunk * PEER_CHUNK, d)[:t]

def finish_layer(x, o_a, o_b, w_o, ln1_g, ln1_b, ln2_g, ln2_b, peer_wq, peer_k1, peer_k2, peer_u, peer_v):
    b, t, d = x.shape
    o = jnp.concatenate([o_a.reshape(b, t, A_HEADS * HEAD_DIM), o_b.reshape(b, t, B_HEADS * HEAD_DIM)],
                        axis=-1).astype(x.dtype)
    x = layer_norm(DN_ALPHA * x + o @ w_o, ln1_g, ln1_b)
    y = peer_ffn(x.reshape(b * t, d), peer_wq, peer_k1, peer_k2, peer_u, peer_v).reshape(b, t, d)
    return layer_norm(DN_ALPHA * x + y, ln2_g, ln2_b)

def setup_inputs(seed: int = 0) -> dict:
    key = jax.random.key(seed)
    ks = jax.random.split(key, 28)
    n_pages = PAST_LEN // PAGE_SIZE
    n_used = DEC_BATCH * n_pages
    n_pool = n_used + n_used // 4
    a_buf = min(A_BUF_MAX, PAST_LEN)
    w_buf = min(WIN, PAST_LEN)

    def nrm(k, shape, scale=1.0):
        return jax.random.normal(k, shape, jnp.float32) * scale

    page_table = jax.random.permutation(ks[0], n_pool)[:n_used].reshape(DEC_BATCH, n_pages).astype(jnp.int32)
    pool_shape = (DEPTH, n_pool, PAGE_SIZE, B_KV_HEADS, HEAD_DIM)
    a_shape = (DEPTH, DEC_BATCH, a_buf, A_HEADS, HEAD_DIM)
    w_shape = (DEPTH, DEC_BATCH, w_buf, B_KV_HEADS, HEAD_DIM)
    cmp_in = CMP_LEN * HEAD_DIM
    return {
        'x_prompt': nrm(ks[1], (BATCH, SEQ, D_MODEL)),
        'x_sample': nrm(ks[2], (DEC_BATCH, DEC_SEQ, D_MODEL)),
        'cache_a_k': nrm(ks[3], a_shape),
        'cache_a_v': nrm(ks[4], a_shape),
        'cache_cmp_k': nrm(ks[5], pool_shape),
        'cache_cmp_v': nrm(ks[6], pool_shape),
        'cache_sel_k': nrm(ks[7], pool_shape),
        'cache_sel_v': nrm(ks[8], pool_shape),
        'cache_win_k': nrm(ks[9], w_shape),
        'cache_win_v': nrm(ks[10], w_shape),
        'page_table': page_table,
        'w_in': nrm(ks[11], (DEPTH, D_MODEL, PROJ_DIM), D_MODEL ** -0.5),
        'w_o': nrm(ks[12], (DEPTH, D_MODEL, D_MODEL), DN_BETA * D_MODEL ** -0.5),
        'cmp_pe_k': nrm(ks[13], (DEPTH, CMP_LEN, HEAD_DIM), 0.1),
        'cmp_w1_k': nrm(ks[14], (DEPTH, cmp_in, CMP_HID), cmp_in ** -0.5),
        'cmp_w2_k': nrm(ks[15], (DEPTH, CMP_HID, HEAD_DIM), CMP_HID ** -0.5),
        'cmp_pe_v': nrm(ks[16], (DEPTH, CMP_LEN, HEAD_DIM), 0.1),
        'cmp_w1_v': nrm(ks[17], (DEPTH, cmp_in, CMP_HID), cmp_in ** -0.5),
        'cmp_w2_v': nrm(ks[18], (DEPTH, CMP_HID, HEAD_DIM), CMP_HID ** -0.5),
        'ln1_g': 1.0 + nrm(ks[19], (DEPTH, D_MODEL), 0.02),
        'ln1_b': nrm(ks[20], (DEPTH, D_MODEL), 0.02),
        'ln2_g': 1.0 + nrm(ks[21], (DEPTH, D_MODEL), 0.02),
        'ln2_b': nrm(ks[22], (DEPTH, D_MODEL), 0.02),
        'peer_wq': nrm(ks[23], (DEPTH, D_MODEL, PEER_HEADS * PEER_DK), D_MODEL ** -0.5),
        'peer_k1': nrm(ks[24], (DEPTH, PEER_HEADS, PEER_KEYS, PEER_DK // 2), (PEER_DK // 2) ** -0.5),
        'peer_k2': nrm(ks[25], (DEPTH, PEER_HEADS, PEER_KEYS, PEER_DK // 2), (PEER_DK // 2) ** -0.5),
        'peer_u': nrm(ks[26], (DEPTH, PEER_EXPERTS, D_MODEL), D_MODEL ** -0.5),
        'peer_v': nrm(ks[27], (DEPTH, PEER_EXPERTS, D_MODEL), DN_BETA),
    }

def reference(x_prompt, x_sample, cache_a_k, cache_a_v, cache_cmp_k, cache_cmp_v, cache_sel_k, cache_sel_v,
              cache_win_k, cache_win_v, page_table, w_in, w_o, cmp_pe_k, cmp_w1_k, cmp_w2_k, cmp_pe_v,
              cmp_w1_v, cmp_w2_v, ln1_g, ln1_b, ln2_g, ln2_b, peer_wq, peer_k1, peer_k2, peer_u, peer_v):
    seq = x_prompt.shape[1]
    dec_seq = x_sample.shape[1]
    past_len = page_table.shape[1] * PAGE_SIZE
    pos_p = jnp.arange(seq, dtype=jnp.int32)
    pos_s = past_len + jnp.arange(dec_seq, dtype=jnp.int32)
    a_keep = min(A_BUF_MAX, seq)
    w_keep = min(WIN, seq)
    xp, xs = x_prompt, x_sample
    pa_k, pa_v, pc_k, pc_v, ps_k, ps_v, pw_k, pw_v = [], [], [], [], [], [], [], []
    sa_k, sa_v, sc_k, sc_v, ss_k, ss_v, sw_k, sw_v = [], [], [], [], [], [], [], []
    for l in range(DEPTH):
        cmp_p = (cmp_pe_k[l], cmp_w1_k[l], cmp_w2_k[l], cmp_pe_v[l], cmp_w1_v[l], cmp_w2_v[l])
        ffn_p = (ln1_g[l], ln1_b[l], ln2_g[l], ln2_b[l], peer_wq[l], peer_k1[l], peer_k2[l], peer_u[l], peer_v[l])

        qa, ka, va, qb_raw, qb_rot, kc, vc, ks, vs, kw, vw, gl = project(xp, pos_p, w_in[l])
        o_a = dilated_attention_prompt(qa, ka, va)
        o_cmp, o_sel = nsa_cmp_sel(qb_raw, qb_rot, pos_p, kc, vc, ks, vs, *cmp_p, chunked=True)
        o_win, _ = banded_attention(qb_rot, kw, vw, WIN)
        o_b = gate_branches(gl, o_cmp, o_sel, o_win)
        xp = finish_layer(xp, o_a, o_b, w_o[l], *ffn_p)
        pa_k.append(ka[:, seq - a_keep:])
        pa_v.append(va[:, seq - a_keep:])
        pc_k.append(kc)
        pc_v.append(vc)
        ps_k.append(ks)
        ps_v.append(vs)
        pw_k.append(kw[:, seq - w_keep:])
        pw_v.append(vw[:, seq - w_keep:])

        qa, ka, va, qb_raw, qb_rot, kc, vc, ks, vs, kw, vw, gl = project(xs, pos_s, w_in[l])
        ka_buf = jnp.concatenate([cache_a_k[l], ka], axis=1)
        va_buf = jnp.concatenate([cache_a_v[l], va], axis=1)
        o_a = dilated_attention_sample(qa, ka_buf, va_buf)
        kc_rows = jnp.concatenate([gather_pages(cache_cmp_k[l], page_table), kc], axis=1)
        vc_rows = jnp.concatenate([gather_pages(cache_cmp_v[l], page_table), vc], axis=1)
        ks_rows = jnp.concatenate([gather_pages(cache_sel_k[l], page_table), ks], axis=1)
        vs_rows = jnp.concatenate([gather_pages(cache_sel_v[l], page_table), vs], axis=1)
        o_cmp, o_sel = nsa_cmp_sel(qb_raw, qb_rot, pos_s, kc_rows, vc_rows, ks_rows, vs_rows, *cmp_p, chunked=False)
        kw_buf = jnp.concatenate([cache_win_k[l], kw], axis=1)
        vw_buf = jnp.concatenate([cache_win_v[l], vw], axis=1)
        o_win = window_attention_sample(qb_rot, kw_buf, vw_buf)
        o_b = gate_branches(gl, o_cmp, o_sel, o_win)
        xs = finish_layer(xs, o_a, o_b, w_o[l], *ffn_p)
        sa_k.append(ka_buf[:, dec_seq:])
        sa_v.append(va_buf[:, dec_seq:])
        sc_k.append(kc)
        sc_v.append(vc)
        ss_k.append(ks)
        ss_v.append(vs)
        sw_k.append(kw_buf[:, dec_seq:])
        sw_v.append(vw_buf[:, dec_seq:])

    y_prompt = xp
    y_sample = xs
    return (y_prompt, y_sample,
            jnp.stack(pa_k), jnp.stack(pa_v), jnp.stack(pc_k), jnp.stack(pc_v),
            jnp.stack(ps_k), jnp.stack(ps_v), jnp.stack(pw_k), jnp.stack(pw_v),
            jnp.stack(sa_k), jnp.stack(sa_v), jnp.stack(sc_k), jnp.stack(sc_v),
            jnp.stack(ss_k), jnp.stack(ss_v), jnp.stack(sw_k), jnp.stack(sw_v))


_drawn_inputs = setup_inputs


def setup_inputs(seed=0):
    import zlib

    import numpy as np

    out = dict(_drawn_inputs(seed))
    spreads = {}
    factors = {'cmp_pe_k': 5.791, 'ln2_g': 2.737, 'ln2_b': 2.828}
    for name, (base, spread) in spreads.items():
        noise = np.random.default_rng([zlib.crc32(name.encode()), seed]).standard_normal(out[name].shape)
        drawn = base * np.exp(spread * noise) if base else spread * noise
        out[name] = jnp.asarray(drawn.astype(out[name].dtype))
    for name, factor in factors.items():
        out[name] = (out[name] * factor).astype(out[name].dtype)
    return out
```

```python
from contextlib import ExitStack

import numpy as np
import concourse.bass as bass
from concourse import mybir

F32 = mybir.dt.float32
F32R = mybir.dt.float32r
BF16 = mybir.dt.bfloat16
I32 = mybir.dt.int32
U32 = mybir.dt.uint32
ALU = mybir.AluOpType
ACT = mybir.ActivationFunctionType
AX = mybir.AxisListType

class Names:
    pass


P = 128
D = 1024
KD = D // P
SEQ = 256
NB = 8
NT = 8
ROWS = SEQ + NB * NT
TILES = 3
RT = [P, P, NB * NT]
PAST = 1024
HD = 64
HEADS = 8
KVH = 2
G = HEADS // KVH
SCALE = HD ** -0.5
NEG = -1e30
ROT = HD // 4
HALF = ROT // 2
ALPHA = 2.0 ** 0.25
EPS = 1e-5
TINY = float(np.finfo(np.float32).tiny)

HK_VA, HK_KC, HK_VC, HK_VS, HK_VW, HK_GL, HK_W = 0, 512, 640, 768, 896, 1024, 1048
HR_QB, HR_QR, HR_QA, HR_KA, HR_KS, HR_W = 0, 512, 1024, 1536, 2048, 2304
ROPED = (HR_W - HR_QR) // HD
WCOLS = [512, 512, 512, 280, 512, 512]
WOFF = [KD * c for c in np.cumsum([0] + WCOLS).tolist()]
QB0, QR0, QA0, KA0, KS0, KW0, NTT = 0, 4, 8, 12, 16, 17, 18

PAGES = PAST // P
CMP_W1 = 16
NC_S = 63
NC_P = 15
C0_W = P + 2 * TILES * HALF
GELU_BANKS = 2


def project_block(nc, d, t, s):
    with ExitStack() as ctx:
        sb = lambda n, sh, dt=F32: ctx.enter_context(nc.sbuf_tensor(n, sh, dt))
        xT = sb("xT", [P, KD, ROWS])
        w = sb("w_in_ring", [P, 2, KD * 512])
        hr = sb("h_rope", [P, TILES, HR_W])
        rt = sb("rope_tmp", [P, 4, ROPED, HALF])
        ps = [t.psum[:, i] for i in range(6)]
        pt = [t.psum[:, 6 + i].rearrange("p (c n) -> p c n", n=P) for i in range(2)]
        block = ctx.enter_context(nc.Block())
        hk, TT, c0 = t.hk, t.TT, t.c0
        ident = c0[:, 0:P]
        nblk = len(WCOLS)
        turns = [(i, g) for i in range(TILES) for g in range(5)]

        @block.sync
        def _(sp):
            sp.dma_start(xT[:], d.xT).then_inc(s["x_in"], 16)
            for n in range(nblk):
                if n >= 2:
                    sp.wait_ge(s["proj"], 3 * (n - 1))
                c = WCOLS[n]
                sp.dma_start(w[:, n % 2, 0:KD * c], d.w_in[:, WOFF[n]:WOFF[n] + KD * c]).then_inc(s[f"w_in{n % 2}"], 16)
                if n == 1:
                    sp.dma_start(c0[:], d.c0).then_inc(s["c0"], 16)
                    sp.dma_start(t.w1k[:], d.w1k).then_inc(s["w1"], 16)
                    sp.dma_start(t.w1v[:], d.w1v).then_inc(s["w1"], 16)
                    sp.dma_start(t.w2k[:], d.w2k).then_inc(s["w1"], 16)
                    sp.dma_start(t.w2v[:], d.w2v).then_inc(s["w1"], 16)
                    sp.dma_start(t.pe[:], d.pe).then_inc(s["w1"], 16)
            sp.wait_ge(s["evac"], 3 * nblk)
            for i in range(TILES):
                r, o = RT[i], P * i
                sp.dma_start(d.o_av[o:o + r, :], hk[0:r, i, 0:512]).then_inc(s["out0"], 16)
                sp.dma_start(d.o_kv[o:o + r, :], hk[0:r, i, 512:1024]).then_inc(s["out_kv"], 16)
                sp.wait_ge(s["roped"], i + 1)
                sp.dma_start(d.o_ak[o:o + r, :], hr[0:r, i, HR_KA:HR_KS]).then_inc(s["out0"], 16)
                sp.dma_start(d.o_ksw[o:o + r, :], hr[0:r, i, HR_KS:HR_W]).then_inc(s["out0"], 16)
            sp.wait_ge(s["gate"], 2)
            sp.dma_start(d.gate_rows, t.gates[0:RT[2], 2, :]).then_inc(s["gate_out"], 16)
            sp.wait_ge(s["out_kv"], 48)
            sp.wait_ge(s["out0"], 16 * 9)
            sp.wait_ge(s["gate_out"], 16)

        @block.tensor
        def _(pe):
            pe.wait_ge(s["x_in"], 16)
            for n in range(nblk):
                pe.wait_ge(s[f"w_in{n % 2}"], 16 * (n // 2 + 1))
                c = WCOLS[n]
                for i in range(TILES):
                    if n >= 2:
                        pe.wait_ge(s["evac"], 3 * (n - 2) + i + 1)
                    out = ps[3 * (n % 2) + i]
                    for k in range(KD):
                        mm = pe.matmul(out[0:RT[i], 0:c], xT[:, k, P * i:P * i + RT[i]],
                                       w[:, n % 2, k * c:(k + 1) * c], start=(k == 0), stop=(k == KD - 1))
                    mm.then_inc(s["proj"], 1)
            pe.wait_ge(s["c0"], 16)
            for u, (i, g) in enumerate(turns):
                pe.wait_ge(s["roped"], i + 1)
                if u >= 2:
                    pe.wait_ge(s["turned_out"], u - 1)
                for c in range(4 if g < 4 else 2):
                    mm = pe.transpose(pt[u % 2][:, c, 0:RT[i]], hr[0:RT[i], i, (4 * g + c) * P:(4 * g + c + 1) * P],
                                      ident[0:RT[i], 0:RT[i]])
                mm.then_inc(s["turned"], 1)

        @block.scalar
        def _(act):
            for n in range(nblk):
                for i in range(TILES):
                    act.wait_ge(s["proj"], 3 * n + i + 1)
                    r, src = RT[i], ps[3 * (n % 2) + i]
                    if n == 0:
                        ins = act.activation(hr[0:r, i, HR_QB:HR_QB + 512], src[0:r, :], ACT.Copy)
                    elif n in (1, 2):
                        ins = act.activation(hr[0:r, i, 512 * (n + 1):512 * (n + 2)], src[0:r, :], ACT.Copy)
                    elif n == 3:
                        act.activation(hr[0:r, i, HR_KS:HR_W], src[0:r, 0:256], ACT.Copy)
                        ins = act.activation(hk[0:r, i, HK_GL:HK_W], src[0:r, 256:280], ACT.Copy)
                    else:
                        ins = act.activation(hk[0:r, i, 512 * (n - 4):512 * (n - 3)], src[0:r, :], ACT.Copy)
                    ins.then_inc(s["evac"], 1)
            act.wait_ge(s["evac"], 12)
            act.activation(t.gates[:, 0:2, :], hk[:, 0:2, HK_GL:HK_W], ACT.Exp, scale=-1.0).then_inc(s["gate_e"], 1)
            act.activation(t.gates[0:RT[2], 2, :], hk[0:RT[2], 2, HK_GL:HK_W], ACT.Exp, scale=-1.0).then_inc(s["gate_e"], 1)

        @block.vector
        def _(ve):
            cos = lambda i: c0[:, P + HALF * i:P + HALF * (i + 1)]
            sin = lambda i: c0[:, P + HALF * (TILES + i):P + HALF * (TILES + i + 1)]
            ve.wait_ge(s["c0"], 16)
            for i in range(TILES):
                r = RT[i]
                ve.wait_ge(s["evac"], 9 + i + 1)
                ve.tensor_copy(hr[0:r, i, HR_QR:HR_QA], hr[0:r, i, HR_QB:HR_QR]).then_inc(s["rope_c"], 1)
                ve.wait_ge(s["rope_c"], 3 * i + 1)
                z = hr[0:r, i, HR_QR:HR_W].rearrange("p (g d) -> p g d", d=HD)
                x1, x2 = z[:, :, 0:HALF], z[:, :, HALF:ROT]
                cb = cos(i)[0:r].unsqueeze(1).broadcast_to([r, ROPED, HALF])
                sn = sin(i)[0:r].unsqueeze(1).broadcast_to([r, ROPED, HALF])
                if i:
                    ve.wait_ge(s["roped"], i)
                for j, (a, b) in enumerate([(x1, cb), (x2, sn), (x2, cb), (x1, sn)]):
                    ins = ve.tensor_tensor(rt[0:r, j], a, b, ALU.mult)
                ins.then_inc(s["rope_c"], 1)
                ve.wait_ge(s["rope_c"], 3 * i + 2)
                ve.tensor_tensor(x1, rt[0:r, 0], rt[0:r, 1], ALU.subtract).then_inc(s["rope_c"], 1)
                ve.tensor_tensor(x2, rt[0:r, 2], rt[0:r, 3], ALU.add).then_inc(s["roped"], 1)
            for u, (i, g) in enumerate(turns):
                ve.wait_ge(s["turned"], u + 1)
                n = 4 if g < 4 else 2
                ve.tensor_copy(TT[:, 4 * g:4 * g + n, P * i:P * i + RT[i]], pt[u % 2][:, 0:n, 0:RT[i]]).then_inc(s["turned_out"], 1)
            ve.wait_ge(s["gate_e"], 2)
            g2 = [t.gates[:, 0:2, :], t.gates[0:RT[2], 2, :]]
            for a in g2:
                ve.tensor_scalar(a, a, 1.0, None, ALU.add).then_inc(s["gate_a"], 1)
            ve.wait_ge(s["gate_a"], 2)
            for a in g2:
                ve.reciprocal(a, a).then_inc(s["gate"], 1)


def compress_block(nc, d, t, s):
    with ExitStack() as ctx:
        sb = lambda n, sh, dt=F32: ctx.enter_context(nc.sbuf_tensor(n, sh, dt))
        pages = sb("cmp_pages", [P, 2, PAGES, 2, KVH, 8, 8])
        c16 = sb("cmp_prompt_rows", [16, 2, KVH, 16, HD])
        rp = sb("cmp_prompt_turned", [P, 2, KVH, 8, 16])
        hid = sb("cmp_hidden", [P, 2, 2, KVH, NC_S])
        bias = sb("cmp_bias", [P, 2, 2])
        ph = [t.psum[:, i, 0:264].rearrange("p (h k n) -> p h k n", h=2, k=KVH) for i in range(2)]
        po = [t.psum[:, 2 + i] for i in range(2)]
        pb = t.psum[:, 4, 0:4]
        pr = t.psum[:, 5].rearrange("p (x g) -> p x g", g=16)
        block = ctx.enter_context(nc.Block())
        w1, w2 = [t.w1k, t.w1v], [t.w2k, t.w2v]
        units = [(b, a) for b in range(NB + 1) for a in range(2)]
        ident = t.c0[:, 0:P]

        @block.sync
        def _(sp):
            sp.dma_start(t.ptab[:], d.page_table).then_inc(s["ptab"], 16)
            for x in range(2 * KVH):
                sp.dma_start(c16[:, x // KVH, x % KVH], d.o_kv.rearrange("(j r) c -> j r c", r=16)[0:16, :, x * HD:(x + 1) * HD])\
                  .then_inc(s["c16"], 16)
            sp.wait_ge(s["ptab"], 16)
            with sp.Fori(0, NB // 2) as i:
                for b in range(2):
                    sp.wait_ge(s["cmp_slot_free"], i * 4 + (2 * b + 2))
                    for p in range(PAGES):
                        r = sp.value_load(t.ptab[0:1, bass.ds((i * 2 + b) * PAGES + p, 1)], min_val=0, max_val=79)
                        sp.dma_start(pages[:, b, p].rearrange("p a k r g -> p (a k r g)"),
                                     d.cmp_pool[bass.ds(r, 1)].rearrange("a p n -> p (a n)")).then_inc(s[f"cmp_pg{b}"], 16)

        @block.tensor
        def _(pe):
            pe.wait_ge(s["w1"], 80)
            for a in range(2):
                for h in range(2):
                    for c in range(CMP_W1):
                        mm = pe.matmul(pb[:, 2 * a + h:2 * a + h + 1], w1[a][:, c, h * P:(h + 1) * P], t.pe[:, a, c:c + 1],
                                       start=(c == 0), stop=(c == CMP_W1 - 1))
            mm.then_inc(s["cmp_b"], 1)
            pe.wait_ge(s["c16"], 64)
            for a in range(2):
                for k in range(KVH):
                    for r in range(8):
                        mm = pe.transpose(pr[:, (a * KVH + k) * 8 + r, :], c16[0:16, a, k, 2 * r:2 * r + 2, :].rearrange("j r e -> j (r e)"), ident[0:16, 0:16])
            mm.then_inc(s["cmp_turn"], 1)

            def hidden(u):
                b, a = units[u]
                if b < NB:
                    pe.wait_ge(s[f"cmp_pg{b % 2}"], 16 * PAGES * (b // 2 + 1))
                else:
                    pe.wait_ge(s["cmp_rp"], 1)
                if u >= 2:
                    pe.wait_ge(s["cmp_gelu"], 2 * (u - 1))
                n = 64 if b < NB else 16
                for h in range(2):
                    for c in range(CMP_W1):
                        first = c < 8
                        if b < NB:
                            rhs = pages[:, b % 2, :, a, :, c % 8, :].rearrange("p g k b -> p k g b")
                        else:
                            rhs = rp[:, a, :, c % 8, :]
                        o = ph[u % 2][:, h, :, 1:1 + n] if first else ph[u % 2][:, h, :, 0:n]
                        if b < NB:
                            o = o.rearrange("p k (g b) -> p k g b", b=8)
                        mm = pe.matmul(o, w1[a][:, c, h * P:(h + 1) * P], rhs, start=(c == 0), stop=(c == CMP_W1 - 1),
                                       skip_group_check=True)
                mm.then_inc(s["cmp_hid"], 1)

            def second(u):
                b, a = units[u]
                n = NC_S if b < NB else NC_P
                pe.wait_ge(s["cmp_gelu"], 2 * (u + 1))
                if u >= 2:
                    pe.wait_ge(s["cmp_done"], u - 1)
                for k in range(KVH):
                    for h in range(2):
                        hk = hid[:, u % 2, h, k, 0:n]
                        if a == 0:
                            mm = pe.matmul(po[u % 2][k * HD:(k + 1) * HD, 0:n], w2[0][:, h, :], hk, start=(h == 0), stop=(h == 1))
                        else:
                            mm = pe.matmul(po[u % 2][0:n, k * HD:(k + 1) * HD], hk, w2[1][:, h, :], start=(h == 0), stop=(h == 1))
                mm.then_inc(s["cmp_second"], 1)

            for u in range(len(units)):
                hidden(u)
                if u >= 1:
                    second(u - 1)
            second(len(units) - 1)

        @block.scalar
        def _(act):
            act.wait_ge(s["cmp_bias"], 1)
            for u, (b, a) in enumerate(units):
                n = NC_S if b < NB else NC_P
                act.wait_ge(s["cmp_hid"], u + 1)
                if u >= 2:
                    act.wait_ge(s["cmp_second"], u - 1)
                for h in range(2):
                    act.activation(hid[:, u % 2, h, :, 0:n], ph[u % 2][:, h, :, 1:1 + n], ACT.Gelu_apprx_tanh,
                                   bias=bias[:, a, h:h + 1]).then_inc(s["cmp_gelu"], 1)

        @block.vector
        def _(ve):
            ve.sem_inc(s["cmp_slot_free"], 4)
            ve.wait_ge(s["cmp_b"], 1)
            ve.tensor_copy(bias[:].rearrange("p a h -> p (a h)"), pb).then_inc(s["cmp_bias"], 1)
            ve.wait_ge(s["cmp_turn"], 1)
            ve.tensor_copy(rp[:].rearrange("p a k r g -> p (a k r) g"), pr).then_inc(s["cmp_rp"], 1)
            for u, (b, a) in enumerate(units):
                n = NC_S if b < NB else NC_P
                ve.wait_ge(s["cmp_hid"], u + 1)
                ve.sem_inc(s["cmp_slot_free"], 1)
                ve.wait_ge(s["cmp_second"], u + 1)
                if a == 0:
                    ve.tensor_copy(t.kc[:, b, 0:n], po[u % 2][:, 0:n]).then_inc(s["cmp_done"], 1)
                else:
                    ve.tensor_copy(t.vc[0:n, b, :], po[u % 2][0:n, 0:P]).then_inc(s["cmp_done"], 1)


NKA, NKW = PAST + NT, 512 + NT
SA, SS, SW, SC = 0, NKA, 2 * NKA, 2 * NKA + NKW
SCOLS = SC + NC_S
CA_PA = 0
CA_PC = CA_PA + 2 * SEQ
CA_PB = CA_PC + 2 * SEQ
CA_SA = CA_PB + 2 * NC_P
CA_SW = CA_SA + NKA
CA_SN = CA_SW + NKW
CA_OV = CA_SN + NT
CA_GS = CA_OV + 17
CA_RV = CA_GS + 64
CA_W = CA_RV + 14
NSEL = 17


def attention_block(nc, d, t, s):
    with ExitStack() as ctx:
        sb = lambda n, sh, dt=F32: ctx.enter_context(nc.sbuf_tensor(n, sh, dt))
        ca = sb("att_consts", [P, CA_W])
        wk = sb("att_work", [P, 2 * SCOLS])
        pp = wk[:, 0:2048].rearrange("p (s e n) -> p s e n", s=4, e=2)
        pT = wk[:, 2048:3072].rearrange("p (s x q) -> p s x q", s=2, x=4)
        nm = sb("att_negmax", [P, 64])
        sm = sb("att_sum", [P, 64])
        rs = sb("att_rsum", [P, 64])
        O = wk[:, 3072:5120].rearrange("p (i n) -> p i n", i=2)
        ka = sb("a_keys", [P, 2, 4, PAST])
        va = sb("a_vals", [P, 2, 8, 512])
        pg = sb("sel_pages", [P, 2, PAGES, 2, P])
        kw = sb("win_keys", [P, 2, 512])
        vw = sb("win_vals", [P, 2, 4, P])
        vn = sb("new_vals", [NT, 2, 768])
        qa = sb("qa_diag", [P, NB, 4, 64])
        qn = sb("qn_diag", [P, 2, NB, 64])
        gs = sb("gates_ht", [64, NB, 3])
        sp_ = wk[0:64].rearrange("p (s n) -> p s n", s=2)
        sT = sb("smp_pT", [P, 2, 24, 64])
        pcn = sb("smp_pc", [64, NC_S])
        pcT = sb("smp_pcT", [NC_S, 64])
        x1 = sb("smp_imp", [64, NSEL])
        imp = sb("smp_negimp", [64, 14])
        top = sb("smp_top", [64, 8])
        tix = sb("smp_topi", [64, 8], U32)
        tif = sb("smp_topf", [64, 1])
        pen = sb("smp_pen", [64, 16])
        st = sb("smp_stats", [64, NB, 4, 4])
        block = ctx.enter_context(nc.Block())
        hk, TT, OT, ident = t.hk, t.TT, t.OT, t.c0[:, 0:P]
        bank = lambda i: t.psum[:, i]
        KINDS = ["A", "cmp", "sel", "win"]
        units = [(i, c, k) for i in range(2) for c in range(4) for k in KINDS]
        NU = len(units)

        def shape(u):
            i, _, k = units[u]
            return (NC_P, 1, NC_P) if k == "cmp" else (P * (i + 1), i + 1, P)

        chunk = lambda b, n: 6 * b + n

        @block.sync
        def _(sp):
            sp.dma_start(ca[:], d.ca).then_inc(s["ca"], 16)
            for br in range(3):
                rows = d.gate_rows.rearrange("(b t) (r h) -> r h t b", t=NT, r=3)[br]
                for h in range(HEADS):
                    sp.dma_start(gs[h * NT:(h + 1) * NT, :, br], rows[h], allow_slow_non_contiguous=True).then_inc(s["gs"], 16)
            for b in range(NB):
                q = b % 2
                if b >= 2:
                    sp.wait_ge(s["s_scores"], chunk(b - 2, 5) + 1)
                    sp.wait_ge(s[f"st_k{q}"], 32 * (b // 2))
                sp.dma_start(ka[:, q], d.a_k[b]).then_inc(s[f"ld_ka{q}"], 16)
                sp.dma_start(kw[:, q], d.w_k[b]).then_inc(s[f"ld_kw{q}"], 16)
                if b >= 2:
                    sp.wait_ge(s["s_pv"], b - 1)
                    sp.wait_ge(s[f"st_v{q}"], 64 * (b // 2))
                for p in range(PAGES):
                    r = sp.value_load(t.ptab[0:1, b * PAGES + p:b * PAGES + p + 1], min_val=0, max_val=79)
                    sp.dma_start(pg[:, q, p].rearrange("p a n -> p (a n)"),
                                 d.sel_pool[bass.ds(r, 1)].rearrange("a p n -> p (a n)")).then_inc(s[f"ld_pg{q}"], 16)
                sp.dma_start(va[:, q].rearrange("p j n -> p (j n)"), d.a_v[b]).then_inc(s[f"ld_v{q}"], 16)
                sp.dma_start(vw[:, q].rearrange("p j n -> p (j n)"), d.w_v[b]).then_inc(s[f"ld_v{q}"], 16)
                o = SEQ + NT * b
                sp.dma_start(vn[:, q, 0:512], d.o_av[o:o + NT, :]).then_inc(s[f"ld_v{q}"], 16)
                sp.dma_start(vn[:, q, 512:768], d.o_kv[o:o + NT, 256:512]).then_inc(s[f"ld_v{q}"], 16)
            for q in range(2):
                sp.wait_ge(s[f"st_k{q}"], 32 * (NB // 2))
                sp.wait_ge(s[f"st_v{q}"], 64 * (NB // 2))

        @block.gpsimd
        def _(gp):
            gp.memset(qa[:], 0.0).then_inc(s["diag0"], 1)
            gp.memset(qn[:], 0.0).then_inc(s["diag0"], 1)
            gp.memset(pen[:], 0.0).then_inc(s["diag0"], 1)
            for b in range(NB):
                q = b % 2
                gp.wait_ge(s[f"ld_ka{q}"], 16 * (b // 2 + 1))
                gp.dma_start(d.keep_ak[b], ka[:, q, :, NT:PAST]).then_inc(s[f"st_k{q}"], 16)
                gp.wait_ge(s[f"ld_kw{q}"], 16 * (b // 2 + 1))
                gp.dma_start(d.keep_wk[b], kw[:, q, NT:512]).then_inc(s[f"st_k{q}"], 16)
                gp.wait_ge(s[f"ld_v{q}"], 64 * (b // 2 + 1))
                av = va[:, q].rearrange("p j n -> p (j n)")
                wv = vw[:, q].rearrange("p j n -> p (j n)")
                gp.dma_start(d.keep_av[b, 7:127], av[8:128]).then_inc(s[f"st_v{q}"], 16)
                gp.dma_start(d.keep_av[b, 0:7], av[1:8]).then_inc(s[f"st_v{q}"], 16)
                gp.dma_start(d.keep_wv[b, 14:126], wv[16:128]).then_inc(s[f"st_v{q}"], 16)
                gp.dma_start(d.keep_wv[b, 0:14], wv[2:16]).then_inc(s[f"st_v{q}"], 16)

        @block.tensor
        def _(pe):
            def p_scores(u):
                i, c, k = units[u]
                n = shape(u)[0]
                if u >= 2:
                    pe.wait_ge(s["p_masked"], u - 1)
                qc = {"A": QA0, "cmp": QB0, "sel": QR0, "win": QR0}[k] + c
                for e in range(2):
                    h = slice(e * HD, (e + 1) * HD)
                    keys = {"A": TT[h, KA0 + c, 0:n], "cmp": t.kc[h, NB, 0:min(n, NC_P)], "sel": TT[h, KS0, 0:n], "win": TT[h, KW0, 0:n]}[k]
                    mm = pe.matmul(bank(2 * (u % 2) + e)[:, 0:n], TT[h, qc, P * i:P * i + P], keys, start=True, stop=True)
                mm.then_inc(s["p_scores"], 1)

            def p_turn(u):
                n, nk, kr = shape(u)
                pe.wait_ge(s["p_exp"], u + 1)
                if u >= 2:
                    pe.wait_ge(s["p_turned_out"], u - 1)
                for e in range(2):
                    for x in range(nk):
                        mm = pe.transpose(bank(4 + u % 2)[0:kr, (2 * e + x) * P:(2 * e + x + 1) * P], pp[:, u % 4, e, x * P:x * P + kr], ident)
                mm.then_inc(s["p_turned"], 1)

            def p_pv(u):
                i, c, k = units[u]
                n, nk, kr = shape(u)
                pe.wait_ge(s["p_turned_out"], u + 1)
                if u >= 2:
                    pe.wait_ge(s["p_normed"], u - 1)
                for e in range(2):
                    for x in range(nk):
                        v = {"A": hk[:, x, (2 * c + e) * HD:(2 * c + e + 1) * HD], "cmp": t.vc[0:min(kr, NC_P), NB, e * HD:(e + 1) * HD],
                             "sel": hk[:, x, HK_VS + e * HD:HK_VS + (e + 1) * HD],
                             "win": hk[:, x, HK_VW + e * HD:HK_VW + (e + 1) * HD]}[k]
                        mm = pe.matmul(bank(6 + u % 2)[:, e * HD:(e + 1) * HD], pT[0:kr, u % 2, 2 * e + x, :], v,
                                       start=(x == 0), stop=(x == nk - 1))
                mm.then_inc(s["p_pv"], 1)

            for u in range(NU + 3):
                if u < NU:
                    p_scores(u)
                if 2 <= u < NU + 2:
                    p_turn(u - 2)
                if u >= 3:
                    p_pv(u - 3)
            pe.wait_ge(s["p_normed"], NU)
            for x in range(4):
                if x >= 2:
                    pe.wait_ge(s["p_OT"], x - 1)
                for y in range(4):
                    c = 4 * (x % 2) + y
                    mm = pe.transpose(bank(6 + x % 2)[:, y * P:(y + 1) * P], O[:, x // 2, c * P:(c + 1) * P], ident)
                mm.then_inc(s["p_O_turned"], 1)

            pe.wait_ge(s["diag"], 12)
            pe.wait_ge(s["p_OT"], 4)

            def chunk_begin(b, n):
                q = chunk(b, n)
                if q >= 3:
                    pe.wait_ge(s["s_read"], q - 2)
                return bank(q % 3)[0:64, :]

            def new_keys(b):
                q = b % 2
                o = chunk_begin(b, 0)
                r = slice(SEQ + NT * b, SEQ + NT * (b + 1))
                for c in range(4):
                    pe.matmul(o[:, 0:NT], qa[:, b, c, :], TT[:, KA0 + c, r], start=(c == 0), stop=(c == 3))
                pe.matmul(o[:, 8:16], qn[:, 1, b, :], TT[:, KS0, r], start=True, stop=True)
                pe.matmul(o[:, 16:24], qn[:, 1, b, :], TT[:, KW0, r], start=True, stop=True)
                pe.matmul(o[:, 24:24 + NC_S], qn[:, 0, b, :], t.kc[:, b, :], start=True, stop=True).then_inc(s["s_scores"], 1)

            def a_scores(b):
                pe.wait_ge(s[f"ld_ka{b % 2}"], 16 * (b // 2 + 1))
                for x in range(2):
                    o = chunk_begin(b, 1 + x)
                    for c in range(4):
                        mm = pe.matmul(o, qa[:, b, c, :], ka[:, b % 2, c, x * 512:(x + 1) * 512], start=(c == 0), stop=(c == 3))
                    mm.then_inc(s["s_scores"], 1)

            def sel_scores(b):
                pe.wait_ge(s[f"ld_pg{b % 2}"], 16 * PAGES * (b // 2 + 1))
                for x in range(2):
                    o = chunk_begin(b, 3 + x)
                    pe.matmul(o, qn[:, 1, b, :], pg[:, b % 2, 4 * x:4 * x + 4, 0, :], start=True, stop=True).then_inc(s["s_scores"], 1)

            def win_scores(b):
                pe.wait_ge(s[f"ld_kw{b % 2}"], 16 * (b // 2 + 1))
                o = chunk_begin(b, 5)
                pe.matmul(o, qn[:, 1, b, :], kw[:, b % 2, :], start=True, stop=True).then_inc(s["s_scores"], 1)

            def turn(b, n):
                w = 3 * b + n
                src = sp_[:, b % 2, :]
                pe.wait_ge(s["s_weights"], 3 * b + n + 1)
                if w >= 2:
                    pe.wait_ge(s["s_turned_out"], w - 1)
                o = bank(3 + w % 2)
                id64 = ident[0:64, 0:64]
                if n == 0:
                    for j in range(8):
                        mm = pe.transpose(o[:, j * 64:(j + 1) * 64], src[:, SA + j:SA + PAST:8], id64)
                elif n == 1:
                    for j in range(8):
                        mm = pe.transpose(o[:, j * 64:(j + 1) * 64], src[:, SS + j * P:SS + (j + 1) * P], id64)
                else:
                    for j in range(4):
                        pe.transpose(o[:, j * 64:(j + 1) * 64], src[:, SW + j:SW + 512:4], id64)
                    for j, c in enumerate((SA + PAST, SS + PAST, SW + 512)):
                        pe.transpose(o[0:NT, (4 + j) * 64:(5 + j) * 64], src[:, c:c + NT], id64)
                    mm = pe.transpose(o[0:NC_S, 7 * 64:8 * 64], src[:, SC:SC + NC_S], id64)
                mm.then_inc(s["s_turned"], 1)

            def values(b):
                q = b % 2
                w = sT[:, q]
                pe.wait_ge(s["s_turned_out"], 3 * b + 3)
                pe.wait_ge(s[f"ld_v{q}"], 64 * (b // 2 + 1))
                if b >= 2:
                    pe.wait_ge(s["s_OT"], b - 1)
                o = bank(5 + q)
                for c in range(4):
                    hc = slice(c * P, (c + 1) * P)
                    for j in range(8):
                        pe.matmul(o[:, c * 16:(c + 1) * 16], va[:, q, j, hc], w[:, j, c * 16:(c + 1) * 16], start=(j == 0), stop=False)
                    pe.matmul(o[:, c * 16:(c + 1) * 16], vn[:, q, hc], w[0:NT, 20, c * 16:(c + 1) * 16], start=False, stop=True)
                o2 = o[:, 64:128]
                for j in range(8):
                    pe.matmul(o2, pg[:, q, j, 1, :], w[:, 8 + j, :], start=(j == 0), stop=False)
                for j in range(4):
                    pe.matmul(o2, vw[:, q, j, :], w[:, 16 + j, :], start=False, stop=False)
                pe.matmul(o2, vn[:, q, 512:640], w[0:NT, 21, :], start=False, stop=False)
                pe.matmul(o2, vn[:, q, 640:768], w[0:NT, 22, :], start=False, stop=False)
                pe.matmul(o2, t.vc[:, b, :], w[0:NC_S, 23, :], start=False, stop=True).then_inc(s["s_pv"], 1)

            def importance(b, n):
                o = bank(7)
                if n == 0:
                    pe.wait_ge(s["i_pc"], b + 1)
                    if b:
                        pe.wait_ge(s["i_pen"], b)
                    pe.transpose(o[0:NC_S, 0:64], pcn[:], ident[0:64, 0:64]).then_inc(s["i_mm"], 1)
                elif n == 1:
                    pe.wait_ge(s["i_cp"], 2 * b + 1)
                    pe.matmul(o[0:64, 64:64 + NSEL], pcT[:], ca[0:NC_S, CA_OV:CA_OV + NSEL], start=True, stop=True).then_inc(s["i_mm"], 1)
                else:
                    pe.wait_ge(s["i_cp"], 2 * b + 2)
                    pe.matmul(o[0:64, 96:96 + NSEL], ca[0:64, CA_GS:CA_GS + 64], x1[:], start=True, stop=True).then_inc(s["i_mm"], 1)

            for b in range(NB + 1):
                if b < NB:
                    new_keys(b)
                    a_scores(b)
                    importance(b, 0)
                if b:
                    turn(b - 1, 0)
                if b < NB:
                    importance(b, 1)
                if b:
                    turn(b - 1, 1)
                    turn(b - 1, 2)
                if b < NB:
                    importance(b, 2)
                if b:
                    values(b - 1)
                if b < NB:
                    sel_scores(b)
                    win_scores(b)

        @block.scalar
        def _(act):
            def p_exp(u):
                n = shape(u)[0]
                act.wait_ge(s["p_max"], u + 1)
                for e in range(2):
                    v = pp[:, u % 4, e, 0:n]
                    ins = act.activation(v, v, ACT.Exp, bias=nm[:, 2 * u + e:2 * u + e + 1], accum_out=sm[:, 2 * u + e:2 * u + e + 1])
                ins.then_inc(s["p_exp"], 1)

            def p_out(u):
                n, nk, kr = shape(u)
                act.wait_ge(s["p_turned"], u + 1)
                if u >= 2:
                    act.wait_ge(s["p_pv"], u - 1)
                src = bank(4 + u % 2)[0:kr, :].rearrange("p (e x q) -> p e x q", e=2, x=2)[:, :, 0:nk, :]
                dst = pT[0:kr, u % 2].rearrange("p (e x) q -> p e x q", e=2)[:, :, 0:nk, :]
                act.activation(dst, src, ACT.Copy).then_inc(s["p_turned_out"], 1)

            for u in range(NU + 2):
                if u < NU:
                    p_exp(u)
                if u >= 2:
                    p_out(u - 2)
            for x in range(4):
                act.wait_ge(s["p_O_turned"], x + 1)
                c = 4 * (x % 2)
                act.activation(OT[:, c:c + 4, P * (x // 2):P * (x // 2) + P], bank(6 + x % 2).rearrange("p (c q) -> p c q", q=P),
                               ACT.Copy).then_inc(s["p_OT"], 1)

            def s_exp(b, n):
                a, w = [(SC, NC_S), (SA, NKA), (SS, NKA), (SW, NKW)][n]
                act.wait_ge(s["s_max"], 4 * b + n + 1)
                v = sp_[:, b % 2, a:a + w]
                act.activation(v, v, ACT.Exp, bias=st[:, b, n, 0:1], accum_out=st[:, b, n, 1:2]).then_inc(s["s_exp"], 1)

            def s_out(b, n):
                w = 3 * b + n
                act.wait_ge(s["s_turned"], w + 1)
                if n == 0 and b >= 2:
                    act.wait_ge(s["s_pv"], b - 1)
                o = bank(3 + w % 2).rearrange("p (j r) -> p j r", r=64)
                z = sT[:, b % 2]
                if n < 2:
                    act.activation(z[:, 8 * n:8 * n + 8, :], o, ACT.Copy).then_inc(s["s_turned_out"], 1)
                else:
                    act.activation(z[:, 16:20, :], o[:, 0:4, :], ACT.Copy)
                    act.activation(z[0:NT, 20:23, :], o[0:NT, 4:7, :], ACT.Copy)
                    act.activation(z[0:NC_S, 23, :], o[0:NC_S, 7, :], ACT.Copy).then_inc(s["s_turned_out"], 1)

            def s_OT(b):
                act.wait_ge(s["s_pv"], b + 1)
                r = slice(SEQ + NT * b, SEQ + NT * (b + 1))
                o = bank(5 + b % 2)
                for e in range(2):
                    h = slice(e * HD, (e + 1) * HD)
                    act.activation(OT[h, 0:4, r], o[h, 0:64].rearrange("p (c e q) -> p c e q", c=4, e=2)[:, :, e, :], ACT.Copy)
                    ins = act.activation(OT[h, 4:8, r], o[h, 64:128].rearrange("p (k g q) -> p k g q", k=KVH, g=G)[:, e], ACT.Copy)
                ins.then_inc(s["s_OT"], 1)

            for b in range(NB + 1):
                if b < NB:
                    s_exp(b, 0)
                    s_exp(b, 1)
                if b:
                    for n in range(3):
                        s_out(b - 1, n)
                    s_OT(b - 1)
                if b < NB:
                    s_exp(b, 2)
                    s_exp(b, 3)

        @block.vector
        def _(ve):
            ve.wait_ge(s["diag0"], 3)
            for c in range(4):
                for e in range(2):
                    h = slice(e * HD, (e + 1) * HD)
                    n = (2 * c + e) * NT
                    ve.tensor_copy(qa[h, :, c, n:n + NT], TT[h, QA0 + c, SEQ:ROWS].rearrange("p (b t) -> p b t", t=NT)).then_inc(s["diag"], 1)
            for x, q0 in enumerate((QB0, QR0)):
                for e in range(2):
                    h = slice(e * HD, (e + 1) * HD)
                    ve.tensor_copy(qn[h, x, :, e * 32:(e + 1) * 32].rearrange("p b (g t) -> p b g t", t=NT),
                                   TT[h, q0:q0 + G, SEQ:ROWS].rearrange("p g (b t) -> p b g t", t=NT)).then_inc(s["diag"], 1)
            ve.wait_ge(s["ca"], 16)
            ve.wait_ge(s["gs"], 16 * 3 * HEADS)

            def p_mask(u):
                i, c, k = units[u]
                n = shape(u)[0]
                ve.wait_ge(s["p_scores"], u + 1)
                if u >= 4:
                    ve.wait_ge(s["p_turned"], u - 3)
                base, w = {"A": (CA_PA, SEQ), "cmp": (CA_PB, NC_P)}.get(k, (CA_PC, SEQ))
                mask = ca[:, base + w * i:base + w * i + n].unsqueeze(1).broadcast_to([P, 2, n])
                v = pp[:, u % 4, :, 0:n]
                ve.scalar_tensor_tensor(v, t.psum[:, 2 * (u % 2):2 * (u % 2) + 2, 0:n], SCALE, mask, ALU.mult, ALU.add)\
                  .then_inc(s["p_masked"], 1)
                ve.wait_ge(s["p_masked"], u + 1)
                z = nm[:, 2 * u:2 * u + 2]
                if k != "cmp":
                    ve.tensor_reduce(z, v, AX.X, ALU.max, negate=True).then_inc(s["p_max"], 1)
                else:
                    j = (u // 4) + 1
                    ve.tensor_reduce(z, v, AX.X, ALU.max, negate=True).then_inc(s["p_cmax"], 1)
                    ve.wait_ge(s["p_cmax"], j)
                    ve.tensor_scalar(z, z, -NEG * 0.1, None, ALU.min).then_inc(s["p_max"], 1)

            def p_sum(u):
                i, c, k = units[u]
                ve.wait_ge(s["p_exp"], u + 1)
                zs, z = sm[:, 2 * u:2 * u + 2], rs[:, 2 * u:2 * u + 2]
                if k == "cmp":
                    ve.tensor_scalar(zs, zs, TINY, None, ALU.max).then_inc(s["p_csum"], 1)
                    ve.wait_ge(s["p_csum"], u // 4 + 1)
                ve.reciprocal(z, zs).then_inc(s["p_rec"], 1)
                if k != "A":
                    br = KINDS.index(k) - 1
                    gate = t.gates[:, i, br * HEADS:(br + 1) * HEADS].rearrange("p (k g) -> p k g", k=KVH)[:, :, c]
                    ve.wait_ge(s["p_rec"], u + 1)
                    ve.tensor_tensor(z, z, gate, ALU.mult).then_inc(s["p_fac"], 1)
                else:
                    ve.sem_inc(s["p_fac"], 1)

            def p_norm(u):
                i, c, k = units[u]
                ve.wait_ge(s["p_pv"], u + 1)
                ve.wait_ge(s["p_rec"], u + 1)
                ve.wait_ge(s["p_fac"], u + 1)
                if k in ("sel", "win"):
                    ve.wait_ge(s["p_normed"], u)
                for e in range(2):
                    col = (2 * c + e) * HD + (0 if k == "A" else 512)
                    dst, src, f = O[:, i, col:col + HD], bank(6 + u % 2)[:, e * HD:(e + 1) * HD], rs[:, 2 * u + e:2 * u + e + 1]
                    if k in ("A", "cmp"):
                        ins = ve.tensor_scalar(dst, src, f, None, ALU.mult)
                    else:
                        ins = ve.scalar_tensor_tensor(dst, src, f, dst, ALU.mult, ALU.add)
                ins.then_inc(s["p_normed"], 1)

            for u in range(NU + 3):
                if u < NU:
                    p_mask(u)
                if 1 <= u < NU + 1:
                    p_sum(u - 1)
                if u >= 3:
                    p_norm(u - 3)

            read = lambda ins: ins.then_inc(s["s_read"], 1)

            def stt(b, n, bk0, w, col, mask):
                return ve.scalar_tensor_tensor(sp_[:, b % 2, col:col + w], bank(chunk(b, n) % 3)[0:64, bk0:bk0 + w], SCALE, mask, ALU.mult, ALU.add)

            def negmax(b, n):
                a, w = [(SC, NC_S), (SA, NKA), (SS, NKA), (SW, NKW)][n]
                ve.wait_ge(s["s_read"], chunk(b, [0, 2, 4, 5][n]) + 1)
                ve.tensor_reduce(st[:, b, n, 0:1], sp_[:, b % 2, a:a + w], AX.X, ALU.max, negate=True).then_inc(s["s_max"], 1)

            def recip(b, n):
                ve.wait_ge(s["s_exp"], 4 * b + n + 1)
                ve.reciprocal(st[:, b, n, 2:3], st[:, b, n, 1:2]).then_inc(s["s_rec"], 1)

            def weigh(b, n):
                a, w = [(SC, NC_S), (SA, NKA), (SS, NKA), (SW, NKW)][n]
                f = st[:, b, n, 2:3]
                ve.wait_ge(s["s_rec"], 4 * b + n + 1)
                if n != 1:
                    gate = gs[:, b, [0, 0, 1, 2][n]:[0, 0, 1, 2][n] + 1]
                    ve.tensor_tensor(st[:, b, n, 3:4], f, gate, ALU.mult).then_inc(s["s_fac"], 1)
                    ve.wait_ge(s["s_fac"], 3 * b + [1, 0, 2, 3][n])
                    f = st[:, b, n, 3:4]
                v = sp_[:, b % 2, a:a + w]
                return ve.tensor_scalar(v, v, f, None, ALU.mult)

            for b in range(NB):
                q = b % 2
                ve.wait_ge(s["s_scores"], chunk(b, 0) + 1)
                if b >= 2:
                    ve.wait_ge(s["s_turned"], 3 * (b - 1))
                stt(b, 0, 0, NT, SA + PAST, ca[0:64, CA_SA + PAST:CA_SA + NKA])
                stt(b, 0, 8, NT, SS + PAST, ca[0:64, CA_SN:CA_SN + NT])
                stt(b, 0, 16, NT, SW + 512, ca[0:64, CA_SW + 512:CA_SW + NKW])
                read(ve.tensor_scalar(sp_[:, q, SC:SCOLS], bank(chunk(b, 0) % 3)[0:64, 24:24 + NC_S], SCALE, None, ALU.mult))
                negmax(b, 0)
                ve.wait_ge(s["s_scores"], chunk(b, 1) + 1)
                read(stt(b, 1, 0, 512, SA, ca[0:64, CA_SA:CA_SA + 512]))
                recip(b, 0)
                ve.wait_ge(s["s_rec"], 4 * b + 1)
                if b:
                    ve.wait_ge(s["i_mm"], 3 * b - 2)
                ve.tensor_scalar(pcn[:], sp_[:, q, SC:SCOLS], st[:, b, 0, 2:3], None, ALU.mult).then_inc(s["i_pc"], 1)
                ve.wait_ge(s["s_scores"], chunk(b, 2) + 1)
                read(stt(b, 2, 0, 512, SA + 512, ca[0:64, CA_SA + 512:CA_SA + PAST]))
                negmax(b, 1)
                ve.wait_ge(s["i_mm"], 3 * b + 1)
                ve.tensor_copy(pcT[:], bank(7)[0:NC_S, 0:64]).then_inc(s["i_cp"], 1)
                recip(b, 1)
                ve.wait_ge(s["i_mm"], 3 * b + 2)
                ve.tensor_copy(x1[:], bank(7)[0:64, 64:64 + NSEL]).then_inc(s["i_cp"], 1)
                weigh(b, 1).then_inc(s["s_w1"], 1)
                ve.wait_ge(s["i_mm"], 3 * b + 3)
                ve.tensor_scalar(imp[:], bank(7)[0:64, 96 + 14:96:-1], -1.0, None, ALU.mult).then_inc(s["i_sel"], 1)
                ve.wait_ge(s["i_sel"], 4 * b + 1)
                ve.max(top[:], imp[:]).then_inc(s["i_sel"], 1)
                ve.wait_ge(s["i_sel"], 4 * b + 2)
                ve.max_index(tix[:], top[:], imp[:]).then_inc(s["i_sel"], 1)
                ve.wait_ge(s["i_sel"], 4 * b + 3)
                ve.tensor_copy(tif[:], tix[:, 0:1]).then_inc(s["i_sel"], 1)
                ve.wait_ge(s["i_sel"], 4 * b + 4)
                ve.tensor_scalar(pen[:, 1:15], ca[0:64, CA_RV:CA_RV + 14], tif[:, 0:1], NEG, ALU.is_equal, ALU.mult).then_inc(s["i_pen"], 1)
                ve.wait_ge(s["i_pen"], b + 1)
                for x in range(2):
                    ve.wait_ge(s["s_scores"], chunk(b, 3 + x) + 1)
                    m = pen[:, 8 * x:8 * x + 8].unsqueeze(2).broadcast_to([64, 8, 64])
                    read(ve.scalar_tensor_tensor(sp_[:, q, SS + 512 * x:SS + 512 * (x + 1)].rearrange("p (j n) -> p j n", n=64),
                                                 bank(chunk(b, 3 + x) % 3)[0:64].rearrange("p (j n) -> p j n", n=64), SCALE, m, ALU.mult, ALU.add))
                negmax(b, 2)
                ve.wait_ge(s["s_scores"], chunk(b, 5) + 1)
                read(stt(b, 5, 0, 512, SW, ca[0:64, CA_SW:CA_SW + 512]))
                negmax(b, 3)
                ve.wait_ge(s["i_pc"], b + 1)
                weigh(b, 0).then_inc(s["s_w1"], 1)
                ve.wait_ge(s["s_w1"], 2 * b + 2)
                ve.sem_inc(s["s_weights"], 1)
                recip(b, 2)
                weigh(b, 2).then_inc(s["s_weights"], 1)
                recip(b, 3)
                weigh(b, 3).then_inc(s["s_weights"], 1)


NH = 8
HH = 2 * NH
TOPK = 16
PAIRS = [TOPK // (a + 1) for a in range(8)]
POFF = [sum(PAIRS[:a]) for a in range(9)]
NPAIR = POFF[8] + 8
LOW = -3e38


def norm_rows(ve, s, key, i, r, x, psum, y, lnp, bn, mv):
    for h in range(2):
        c = slice(512 * h, 512 * (h + 1))
        ve.scalar_tensor_tensor(y[:, c], x[:, c], ALPHA, psum[h], ALU.mult, ALU.add).then_inc(s[key + "_sum"], 1)
    ve.wait_ge(s[key + "_sum"], 2 * i + 2)
    for h in range(2):
        ve.bn_stats(bn[0:r, 6 * h:6 * h + 6], y[:, 512 * h:512 * (h + 1)]).then_inc(s[key + "_st"], 1)
    ve.wait_ge(s[key + "_st"], 5 * i + 2)
    ve.bn_aggr(mv[0:r, 0:2], bn[0:r, :]).then_inc(s[key + "_st"], 1)
    ve.wait_ge(s[key + "_st"], 5 * i + 3)
    ve.tensor_scalar(mv[0:r, 2:3], mv[0:r, 1:2], EPS, None, ALU.add).then_inc(s[key + "_var"], 1)
    ve.wait_ge(s[key + "_root"], i + 1)
    ve.reciprocal(mv[0:r, 2:3], mv[0:r, 2:3]).then_inc(s[key + "_st"], 1)
    ve.wait_ge(s[key + "_st"], 5 * i + 4)
    ve.tensor_scalar(y, y, mv[0:r, 0:1], mv[0:r, 2:3], ALU.subtract, ALU.mult).then_inc(s[key + "_st"], 1)
    ve.wait_ge(s[key + "_st"], 5 * i + 5)
    ve.tensor_tensor(y, y, lnp[0:r, 0, :], ALU.mult).then_inc(s[key + "_g"], 1)
    ve.wait_ge(s[key + "_g"], i + 1)
    ve.tensor_tensor(y, y, lnp[0:r, 1, :], ALU.add).then_inc(s[key + "_ln"], 1)


def route_block(nc, d, t, s):
    with ExitStack() as ctx:
        sb = lambda n, sh, dt=F32: ctx.enter_context(nc.sbuf_tensor(n, sh, dt))
        wo = sb("w_o", [P, KD, D])
        xr = sb("x_rows", [P, TILES, D])
        ln = sb("ln1", [P, 2, D])
        wq = sb("wq_ring", [P, 4, KD, P])
        ky = sb("peer_keys", [P, HH, P])
        qT = sb("peer_q", [P, HH, ROWS])
        xT = sb("x1T", [P, KD, ROWS])
        sc = sb("peer_scores", [P, 3, 4, P])
        sc2 = sb("peer_scores2", [P, 4, P])
        v = sb("top_vals", [P, TILES, HH, TOPK])
        ix = sb("top_idx", [P, TILES, HH, TOPK], U32)
        ixf = sb("top_idxf", [P, TILES, HH, TOPK])
        i128 = sb("top_idx128", [P, NH, TOPK])
        cv = sb("pair_vals", [P, NH, NPAIR])
        cv2 = sb("pair_vals2", [P, NH, NPAIR])
        ci = sb("pair_ids", [P, NH, NPAIR])
        bv = sb("best_vals", [P, NH, TOPK])
        bi = sb("best_idx", [P, NH, TOPK], U32)
        bf = sb("best_idxf", [P, NH, TOPK])
        eq = sb("best_onehot", [P, 2, TOPK, NPAIR])
        ids = sb("expert_ids", [P, NH, TOPK])
        den = sb("gate_sum", [P, 2, NH])
        cT = sb("ids_turned", [P, ROWS])
        gT = sb("gates_turned", [P, ROWS])
        ii = sb("ids_int", [P, 2, ROWS], I32)
        gr = sb("gate_rest", [P, 2, ROWS])
        bn = sb("ln1_bn", [P, 12])
        mv = sb("ln1_mv", [P, 3])
        io = sb("iota_pairs", [P, NPAIR])
        block = ctx.enter_context(nc.Block())
        OT, x1, ident = t.OT, t.x1, t.c0[:, 0:P]
        bank = lambda i: t.psum[:, i]
        sunits = [(g, i) for g in range(4) for i in range(TILES)]

        @block.sync
        def _(sp):
            for k in range(0, KD, 2):
                sp.dma_start(wo[:, k:k + 2], d.w_o[:, k:k + 2]).then_inc(s[f"ld_wo{k // 2}"], 16)
            for i in range(TILES):
                sp.dma_start(xr[0:RT[i], i, :], d.x_rows[P * i:P * i + RT[i], :]).then_inc(s["ld_xr"], 16)
            sp.dma_start(ln[:, 0, :], d.ln1_g.partition_broadcast(P)).then_inc(s["ld_xr"], 16)
            sp.dma_start(ln[:, 1, :], d.ln1_b.partition_broadcast(P)).then_inc(s["ld_xr"], 16)
            sp.dma_start(io[:], d.iota_pairs).then_inc(s["ld_ky"], 16)
            sp.dma_start(ky[:], d.peer_keys).then_inc(s["ld_ky"], 16)
            for j in range(HH):
                if j >= 4:
                    sp.wait_ge(s["q_mm"], j - 3)
                sp.dma_start(wq[:, j % 4], d.peer_wq[j]).then_inc(s[f"ld_wq{j % 4}"], 16)

        @block.tensor
        def _(pe):
            for i in range(TILES):
                r = slice(P * i, P * i + RT[i])
                for h in range(2):
                    for k in range(KD):
                        if i == 0 and h == 0 and k % 2 == 0:
                            pe.wait_ge(s[f"ld_wo{k // 2}"], 16)
                        mm = pe.matmul(bank(2 * i + h)[0:RT[i], :], OT[:, k, r], wo[:, k, 512 * h:512 * (h + 1)],
                                       start=(k == 0), stop=(k == KD - 1))
                mm.then_inc(s["o_mm"], 1)
            for x in range(2 * TILES):
                i = x // 2
                pe.wait_ge(s["l1_ln"], i + 1)
                if x >= 2:
                    pe.wait_ge(s["x_out"], x - 1)
                for y in range(4):
                    k = 4 * (x % 2) + y
                    mm = pe.transpose(bank(6 + x % 2)[:, y * P:y * P + RT[i]], x1[0:RT[i], i, k * P:(k + 1) * P], ident[0:RT[i], 0:RT[i]])
                mm.then_inc(s["x_turn"], 1)
            pe.wait_ge(s["x_out"], 6)
            pe.wait_ge(s["ld_ky"], 32)
            for g in range(4):
                for j in range(4 * g, 4 * g + 4):
                    pe.wait_ge(s[f"ld_wq{j % 4}"], 16 * (j // 4 + 1))
                    if j >= 2:
                        pe.wait_ge(s["q_out"], j - 1)
                    for k in range(KD):
                        mm = pe.matmul(bank(j % 2)[:, 0:ROWS], wq[:, j % 4, k, :], xT[:, k, :], start=(k == 0), stop=(k == KD - 1))
                    mm.then_inc(s["q_mm"], 1)
                pe.wait_ge(s["q_out"], 4 * g + 4)
                for i in range(TILES):
                    u = 3 * g + i
                    if u >= 2:
                        pe.wait_ge(s["sc_out"], u - 1)
                    for j in range(4):
                        mm = pe.matmul(bank(2 + u % 2)[0:RT[i], j * P:(j + 1) * P], qT[:, 4 * g + j, P * i:P * i + RT[i]], ky[:, 4 * g + j, :],
                                       start=True, stop=True)
                    mm.then_inc(s["sc_mm"], 1)
            for i in range(TILES):
                r = RT[i]
                pe.wait_ge(s["ids"], i + 1)
                pe.transpose(bank(4 + i)[:, 0:r], ids[0:r].rearrange("p h k -> p (h k)"), ident[0:r, 0:r])
                pe.transpose(bank(4 + i)[:, P:P + r], bv[0:r].rearrange("p h k -> p (h k)"), ident[0:r, 0:r]).then_inc(s["id_turn"], 1)

        @block.scalar
        def _(act):
            for i in range(TILES):
                act.wait_ge(s["l1_var"], i + 1)
                act.activation(mv[0:RT[i], 2:3], mv[0:RT[i], 2:3], ACT.Sqrt).then_inc(s["l1_root"], 1)
            for x in range(2 * TILES):
                i, c = x // 2, 4 * (x % 2)
                act.wait_ge(s["x_turn"], x + 1)
                act.activation(xT[:, c:c + 4, P * i:P * i + RT[i]], bank(6 + x % 2).rearrange("p (c q) -> p c q", q=P)[:, :, 0:RT[i]],
                               ACT.Copy).then_inc(s["x_out"], 1)
            for g in range(4):
                for j in range(4 * g, 4 * g + 4):
                    act.wait_ge(s["q_mm"], j + 1)
                    act.activation(qT[:, j, :], bank(j % 2)[:, 0:ROWS], ACT.Copy).then_inc(s["q_out"], 1)
                for i in range(TILES):
                    u = 3 * g + i
                    act.wait_ge(s["sc_mm"], u + 1)
                    if u >= 3:
                        act.wait_ge(s["top2"], 4 * (u - 2))
                    act.activation(sc[0:RT[i], u % 3], bank(2 + u % 2)[0:RT[i]].rearrange("p (j n) -> p j n", n=P), ACT.Copy).then_inc(s["sc_out"], 1)
            for i in range(TILES):
                act.wait_ge(s["g_sub"], i + 1)
                act.activation(bv[0:RT[i]], bv[0:RT[i]], ACT.Exp).then_inc(s["g_exp"], 1)

        @block.vector
        def _(ve):
            ve.wait_ge(s["ld_xr"], 80)
            for i in range(TILES):
                r = RT[i]
                ve.wait_ge(s["o_mm"], i + 1)
                norm_rows(ve, s, "l1", i, r, xr[0:r, i, :], [bank(2 * i + h)[0:r, :] for h in range(2)], x1[0:r, i, :], ln, bn, mv)
            ve.wait_ge(s["x_out"], 6)
            ve.tensor_copy(t.x1h[:], xT[:]).then_inc(s["x_hi"], 1)
            ve.wait_ge(s["x_hi"], 1)
            ve.tensor_tensor(t.x1l[:], xT[:], t.x1h[:].bitcast(F32), ALU.subtract).then_inc(s["x_lo"], 1)

            def top16(n, base, r, src, src2, vals, idxs, names):
                a, b, c = names
                for j in range(n):
                    ve.max(vals(j)[:, 0:8], src(j)).then_inc(s[a], 1)
                ve.wait_ge(s[a], base + n)
                for j in range(n):
                    ve.max_index(idxs(j)[:, 0:8], vals(j)[:, 0:8], src(j))
                    ve.match_replace(src2(j), vals(j)[:, 0:8], src(j), LOW).then_inc(s[b], 1)
                ve.wait_ge(s[b], base + n)
                for j in range(n):
                    ve.max(vals(j)[:, 8:16], src2(j)).then_inc(s[a + "b"], 1)
                ve.wait_ge(s[a + "b"], base + n)
                for j in range(n):
                    ve.max_index(idxs(j)[:, 8:16], vals(j)[:, 8:16], src2(j)).then_inc(s[c], 1)

            def pairs(i):
                r = RT[i]
                z = v[0:r, i].rearrange("p (h e) k -> p h e k", e=2)
                w = ixf[0:r, i].rearrange("p (h e) k -> p h e k", e=2)
                ve.tensor_scalar(i128[0:r], w[:, :, 0, :], float(P), None, ALU.mult).then_inc(s["pr128"], 1)
                ve.wait_ge(s["pr128"], i + 1)
                for a in range(8):
                    n, o = PAIRS[a], POFF[a]
                    bc = lambda q: q.unsqueeze(2).broadcast_to([r, NH, n])
                    ve.tensor_tensor(cv[0:r, :, o:o + n], z[:, :, 1, 0:n], bc(z[:, :, 0, a]), ALU.add)
                    ve.tensor_tensor(ci[0:r, :, o:o + n], w[:, :, 1, 0:n], bc(i128[0:r, :, a]), ALU.add)
                o = POFF[8]
                bc = lambda q: q.unsqueeze(2).broadcast_to([r, NH, 8])
                ve.tensor_tensor(cv[0:r, :, o:NPAIR], z[:, :, 0, 8:16], bc(z[:, :, 1, 0]), ALU.add)
                ve.tensor_tensor(ci[0:r, :, o:NPAIR], i128[0:r, :, 8:16], bc(w[:, :, 1, 0]), ALU.add).then_inc(s["pair"], 1)

            def best(i):
                r = RT[i]
                if i:
                    ve.wait_ge(s["id_turn"], i)
                ve.wait_ge(s["pair"], i + 1)
                top16(NH, NH * i, r, lambda j: cv[0:r, j], lambda j: cv2[0:r, j], lambda j: bv[0:r, j], lambda j: bi[0:r, j], ("be", "ber", "bei"))
                ve.wait_ge(s["bei"], NH * (i + 1))
                ve.tensor_copy(bf[0:r], bi[0:r]).then_inc(s["bf"], 1)
                ve.tensor_copy(den[0:r, 1], bv[0:r, :, 0]).then_inc(s["g_max"], 1)
                ve.wait_ge(s["g_max"], i + 1)
                ve.tensor_tensor(bv[0:r], bv[0:r], den[0:r, 1].unsqueeze(2).broadcast_to([r, NH, TOPK]), ALU.subtract).then_inc(s["g_sub"], 1)
                ve.wait_ge(s["bf"], i + 1)
                for h in range(0, NH, 2):
                    sel = bf[0:r, h:h + 2].unsqueeze(3).broadcast_to([r, 2, TOPK, NPAIR])
                    iot = io[0:r].unsqueeze(1).unsqueeze(1).broadcast_to([r, 2, TOPK, NPAIR])
                    n = 4 * i + h // 2
                    if n:
                        ve.wait_ge(s["id_sum"], n)
                    ve.tensor_tensor(eq[0:r], iot, sel, ALU.is_equal).then_inc(s["id_eq"], 1)
                    ve.wait_ge(s["id_eq"], n + 1)
                    ve.tensor_tensor(eq[0:r], eq[0:r], ci[0:r, h:h + 2].unsqueeze(2).broadcast_to([r, 2, TOPK, NPAIR]), ALU.mult).then_inc(s["id_mul"], 1)
                    ve.wait_ge(s["id_mul"], n + 1)
                    ve.tensor_reduce(ids[0:r, h:h + 2], eq[0:r], AX.X, ALU.add).then_inc(s["id_sum"], 1)
                ve.wait_ge(s["g_exp"], i + 1)
                ve.tensor_reduce(den[0:r, 0], bv[0:r], AX.X, ALU.add).then_inc(s["g_den"], 1)
                ve.wait_ge(s["g_den"], 2 * i + 1)
                ve.reciprocal(den[0:r, 0], den[0:r, 0]).then_inc(s["g_den"], 1)
                ve.wait_ge(s["g_den"], 2 * i + 2)
                ve.tensor_tensor(bv[0:r], bv[0:r], den[0:r, 0].unsqueeze(2).broadcast_to([r, NH, TOPK]), ALU.mult).then_inc(s["g_fin"], 1)
                ve.wait_ge(s["g_fin"], i + 1)
                ve.wait_ge(s["id_sum"], 4 * i + 4)
                ve.sem_inc(s["ids"], 1)

            for u, (g, i) in enumerate(sunits):
                r = RT[i]
                ve.wait_ge(s["sc_out"], u + 1)
                if u:
                    ve.wait_ge(s["top2"], 4 * u)
                top16(4, 4 * u, r, lambda j: sc[0:r, u % 3, j], lambda j: sc2[0:r, j], lambda j: v[0:r, i, 4 * g + j],
                      lambda j: ix[0:r, i, 4 * g + j], ("top", "topr", "top2"))
                ve.wait_ge(s["top2"], 4 * (u + 1))
                ve.tensor_copy(ixf[0:r, i, 4 * g:4 * g + 4], ix[0:r, i, 4 * g:4 * g + 4]).then_inc(s["ixf"], 1)
                if g == 3:
                    ve.wait_ge(s["ixf"], u + 1)
                    if i:
                        ve.wait_ge(s["id_mul"], 4 * i)
                    pairs(i)
                    best(i)
            for i in range(TILES):
                r = slice(P * i, P * i + RT[i])
                ve.wait_ge(s["id_turn"], i + 1)
                ve.tensor_copy(cT[:, r], bank(4 + i)[:, 0:RT[i]])
                ve.tensor_copy(gT[:, r], bank(4 + i)[:, P:P + RT[i]]).then_inc(s["id_out"], 1)
            step = [0]

            def after(ins):
                step[0] += 1
                ins.then_inc(s["split"], 1)
                ve.wait_ge(s["split"], step[0])

            ve.wait_ge(s["id_out"], 3)
            after(ve.tensor_copy(ii[:, 0, :], cT[:]))
            after(ve.tensor_scalar(ii[:, 1, :], ii[:, 0, :], 7, None, ALU.logical_shift_right))
            after(ve.tensor_copy(t.i1[:], ii[:, 1, :]))
            after(ve.tensor_scalar(ii[:, 1, :], ii[:, 0, :], P - 1, None, ALU.bitwise_and))
            for g in range(SEGS):
                ve.tensor_scalar(t.i2[:, g, :], ii[:, 1, :], float(-g * SEGW), None, ALU.add)
            after(ve.tensor_copy(t.gp[:, 0, :], gT[:]))
            after(ve.tensor_tensor(gr[:, 0, :], gT[:], t.gp[:, 0, :], ALU.subtract))
            after(ve.tensor_copy(t.gp[:, 1, :], gr[:, 0, :]))
            after(ve.tensor_tensor(gr[:, 1, :], gr[:, 0, :], t.gp[:, 1, :], ALU.subtract))
            after(ve.tensor_copy(t.gp[:, 2, :], gr[:, 1, :]))


SEGS, SEGW = 4, 32
NE = 128
GT = ROWS // SEGW
HWC = TILES * P
UN = 4


def expert_block(nc, d, t, s):
    with ExitStack() as ctx:
        sb = lambda n, sh, dt=F32: ctx.enter_context(nc.sbuf_tensor(n, sh, dt))
        W = sb("gate_matrix", [P, 2, SEGW, ROWS])
        us, vs = sb("u_in", [P, 2, D]), sb("v_in", [P, 2, D])
        uh, ul = sb("u_hi", [P, 2, D], F32R), sb("u_lo", [P, 2, D], F32R)
        vh, vl = sb("v_hi", [P, 2, D], F32R), sb("v_lo", [P, 2, D], F32R)
        hg = sb("hidden", [P, ROWS])
        hw = sb("gated", [P, ROWS])
        hwh, hwl = sb("gated_hi", [P, 2, HWC], F32R), sb("gated_lo", [P, 2, HWC], F32R)
        A = sb("onehot_i1", [P, 2, GT, P], BF16)
        E = sb("onehot_i2", [P, 2, GT, SEGW], BF16)
        B = sb("gated_i2", [P, 2, 3, GT, SEGW], BF16)
        iof = sb("iota_in_f32", [P, P])
        io = sb("iota", [P, P], BF16)
        ln = sb("ln2", [P, 2, D])
        bn = sb("ln2_bn", [P, 12])
        mv = sb("ln2_mv", [P, 3])
        block = ctx.enter_context(nc.Block())
        bank = lambda i: t.psum[:, i]
        H, WP = bank(6), bank(7)
        x1h, x1l = t.x1h, t.x1l

        @block.sync
        def _(sp):
            for m in range(2):
                sp.dma_start(us[:, m], d.peer_u[m]).then_inc(s[f"ld_u{m}"], 16)
                sp.dma_start(vs[:, m], d.peer_v[m]).then_inc(s[f"ld_v2{m}"], 16)
            sp.dma_start(ln[:, 0, :], d.ln2_g.partition_broadcast(P)).then_inc(s["ld_ln2"], 16)
            sp.dma_start(ln[:, 1, :], d.ln2_b.partition_broadcast(P)).then_inc(s["ld_ln2"], 16)
            with sp.Fori(0, NE // 2 - 1) as i:
                for m in range(2):
                    sp.wait_ge(s["u_lo"], i * 2 + (m + 1))
                    sp.dma_start(us[:, m], d.peer_u[bass.ds(i * 2 + (m + 2), 1)].rearrange("a p n -> p (a n)")).then_inc(s[f"ld_u{m}"], 16)
                    sp.wait_ge(s["v_lo"], i * 2 + (m + 1))
                    sp.dma_start(vs[:, m], d.peer_v[bass.ds(i * 2 + (m + 2), 1)].rearrange("a p n -> p (a n)")).then_inc(s[f"ld_v2{m}"], 16)
            for i in range(TILES):
                sp.wait_ge(s["l2_ln"], i + 1)
                sp.dma_start(d.o_y[P * i:P * i + RT[i], :], t.x1[0:RT[i], i, :]).then_inc(s["st_y"], 16)
            sp.wait_ge(s["st_y"], 48)

        def segments(eng, body, last):
            for g in range(SEGS):
                with eng.Fori(0, SEGW // UN - (g == SEGS - 1)) as i:
                    for k in range(UN):
                        body(g, i * UN + (SEGW * g + k), i * UN + k, k)
            for k in range(UN):
                last(NE - UN + k, SEGW - UN + k, k)

        @block.tensor
        def _(pe):
            pe.sem_inc(s["c_mm"], 2)
            pe.sem_inc(s["y_mm"], 1)

            def product1(n, q):
                pe.wait_ge(s["u_lo"], n + 1)
                pe.wait_ge(s["gelu"], n)
                for k in range(KD):
                    kc = slice(k * P, (k + 1) * P)
                    pe.matmul(H[:, 0:ROWS], uh[:, q, kc], x1h[:, k, :], start=(k == 0), stop=False)
                    pe.matmul(H[:, 0:ROWS], uh[:, q, kc], x1l[:, k, :], start=False, stop=False)
                    mm = pe.matmul(H[:, 0:ROWS], ul[:, q, kc], x1h[:, k, :], start=False, stop=(k == KD - 1))
                mm.then_inc(s["h_mm"], 1)

            def product2(n, q, stop):
                pe.wait_ge(s["hw_lo"], n + 2)
                pe.wait_ge(s["v_lo"], n + 1)
                for i in range(TILES):
                    r = slice(i * P, (i + 1) * P)
                    for a, b in ((hwh, vh), (hwh, vl), (hwl, vh)):
                        for h in range(2):
                            mm = pe.matmul(bank(2 * i + h), a[:, q, r], b[:, q, 512 * h:512 * (h + 1)], start=False,
                                           stop=stop and a is hwl, skip_group_check=True)
                mm.then_inc(s["y_mm"], 1)

            def gate_rows(c, q):
                pe.wait_ge(s["onehot"], c + 1)
                pe.wait_ge(s["W_out"], c + 1)
                for r in range(GT):
                    for x in range(3):
                        mm = pe.matmul(WP[:, r * SEGW:(r + 1) * SEGW], A[:, q, r, :], B[:, q, x, r, :], start=(x == 0), stop=(x == 2))
                mm.then_inc(s["c_mm"], 1)

            pe.wait_ge(s["zero"], 3)
            for i in range(2 * TILES):
                mm = pe.matmul(bank(i), hwh[:, 1, 0:P], vh[:, 1, 0:512], start=True, stop=False, skip_group_check=True)
            mm.then_inc(s["y_mm"], 1)
            with pe.Fori(0, SEGW // 2) as i:
                for q in range(2):
                    gate_rows(i * 2 + q, q)
            product1(0, 0)

            def body(g, n, j, k):
                product1(n + 1, (k + 1) % 2)
                if g < SEGS - 1:
                    gate_rows(n + SEGW, k % 2)
                product2(n, k % 2, False)

            def last(n, j, k):
                if k < UN - 1:
                    product1(n + 1, (k + 1) % 2)
                product2(n, k % 2, k == UN - 1)

            segments(pe, body, last)

        @block.scalar
        def _(act):
            def u_hi(n, q, w):
                act.wait_ge(s[f"ld_u{q}"], w)
                act.activation(uh[:, q], us[:, q], ACT.Copy).then_inc(s["u_hi"], 1)

            def W_out(c, seg, g):
                act.wait_ge(s["c_mm"], c + 3)
                act.activation(W[:, seg % 2, :, bass.ds(g * GT, GT)].rearrange("p j r -> p r j"),
                               WP[:, 0:GT * SEGW].rearrange("p (r j) -> p r j", j=SEGW), ACT.Copy).then_inc(s["W_out"], 1)

            act.sem_inc(s["W_out"], 1)
            with act.Fori(0, SEGW // 2) as i:
                for q in range(2):
                    W_out(i * 2 + q, 0, i * 2 + q)
            u_hi(0, 0, 16)

            def body(g, n, j, k):
                q = k % 2
                act.wait_ge(s["h_mm"], n + 1)
                act.wait_ge(s["hw"], n + 1)
                act.activation(hg[:], H[:, 0:ROWS], ACT.Gelu_apprx_tanh).then_inc(s["gelu"], 1)
                act.wait_ge(s["hw"], n + 2)
                act.wait_ge(s["y_mm"], n + 1)
                act.activation(hwh[:, q, 0:ROWS], hw[:], ACT.Copy).then_inc(s["hw_hi"], 1)
                if g < SEGS - 1 or k < UN - 1 or type(n) is not int:
                    act_loads(n + 1, k + 1)
                act.wait_ge(s[f"ld_v2{q}"], loads(n, k))
                act.activation(vh[:, q], vs[:, q], ACT.Copy).then_inc(s["v_hi"], 1)
                if g < SEGS - 1:
                    W_out(n + SEGW, g + 1, j)

            def loads(n, k):
                return (n - k % 2) * 8 + 16

            def act_loads(n, k):
                u_hi(n, k % 2, loads(n, k))

            segments(act, body, lambda n, j, k: body(SEGS - 1, n, j, k))
            for i in range(TILES):
                act.wait_ge(s["l2_var"], i + 1)
                act.activation(mv[0:RT[i], 2:3], mv[0:RT[i], 2:3], ACT.Sqrt).then_inc(s["l2_root"], 1)

        @block.vector
        def _(ve):
            for z in (hwh, hwl, vh):
                ve.memset(z[:].bitcast(F32), 0.0).then_inc(s["zero"], 1)
            ve.wait_ge(s["iota_in"], 16)
            ve.tensor_copy(io[:], iof[:]).then_inc(s["iota"], 1)
            ve.wait_ge(s["iota"], 1)
            ve.sem_inc(s["hw"], 1)
            ve.sem_inc(s["hw_lo"], 1)

            def onehots(c, seg, g, q):
                r = bass.ds(g * GT, GT)
                ve.wait_ge(s["c_mm"], c + 1)
                ve.tensor_tensor(E[:, q], io[:, 0:SEGW].unsqueeze(1).broadcast_to([P, GT, SEGW]),
                                 t.i2[:, seg, r].unsqueeze(2).broadcast_to([P, GT, SEGW]), ALU.is_equal).then_inc(s["oh_e"], 1)
                ve.tensor_tensor(A[:, q], io[:].unsqueeze(1).broadcast_to([P, GT, P]),
                                 t.i1[:, r].unsqueeze(2).broadcast_to([P, GT, P]), ALU.is_equal)
                ve.wait_ge(s["oh_e"], c + 1)
                ve.tensor_tensor(B[:, q], E[:, q].unsqueeze(1).broadcast_to([P, 3, GT, SEGW]),
                                 t.gp[:, :, r].unsqueeze(3).broadcast_to([P, 3, GT, SEGW]), ALU.mult).then_inc(s["onehot"], 1)

            def u_lo(n, q):
                ve.wait_ge(s["u_hi"], n + 1)
                ve.tensor_tensor(ul[:, q], us[:, q], uh[:, q].bitcast(F32), ALU.subtract).then_inc(s["u_lo"], 1)

            with ve.Fori(0, SEGW // 2) as i:
                for q in range(2):
                    onehots(i * 2 + q, 0, i * 2 + q, q)
            u_lo(0, 0)

            def body(g, n, j, k):
                q = k % 2
                if k == 0:
                    ve.wait_ge(s["W_out"], SEGW * (g + 1) + 1)
                ve.wait_ge(s["gelu"], n + 1)
                ve.wait_ge(s["hw_lo"], n + 1)
                ve.tensor_tensor(hw[:], hg[:], W[:, g % 2, bass.ds(j, 1), :].rearrange("p a r -> p (a r)"), ALU.mult).then_inc(s["hw"], 1)
                ve.wait_ge(s["hw_hi"], n + 1)
                ve.tensor_tensor(hwl[:, q, 0:ROWS], hw[:], hwh[:, q, 0:ROWS].bitcast(F32), ALU.subtract).then_inc(s["hw_lo"], 1)
                if type(n) is not int or k < UN - 1:
                    u_lo(n + 1, (k + 1) % 2)
                ve.wait_ge(s["v_hi"], n + 1)
                ve.tensor_tensor(vl[:, q], vs[:, q], vh[:, q].bitcast(F32), ALU.subtract).then_inc(s["v_lo"], 1)
                if g < SEGS - 1:
                    onehots(n + SEGW, g + 1, j, q)

            segments(ve, body, lambda n, j, k: body(SEGS - 1, n, j, k))
            ve.wait_ge(s["y_mm"], NE + 2)
            ve.wait_ge(s["ld_ln2"], 32)
            for i in range(TILES):
                r = RT[i]
                norm_rows(ve, s, "l2", i, r, t.x1[0:r, i, :], [bank(2 * i + h)[0:r, :] for h in range(2)], t.x1[0:r, i, :], ln, bn, mv)

        @block.gpsimd
        def _(gp):
            gp.dma_start(iof[:], d.iota).then_inc(s["iota_in"], 16)


def constants():
    c0 = np.zeros((P, C0_W), np.float32)
    c0[:, 0:P] = np.eye(P, dtype=np.float32)
    inv = np.power(np.float32(500000.0), -np.arange(HALF, dtype=np.float32) / np.float32(HALF)).astype(np.float32)
    for i in range(TILES):
        pos = (np.arange(P) + P * i) if i < 2 else PAST + np.arange(P) % NT
        ang = pos.astype(np.float32)[:, None] * inv[None, :]
        c0[:, P + HALF * i:P + HALF * (i + 1)] = np.cos(ang)
        c0[:, P + HALF * (TILES + i):P + HALF * (TILES + i + 1)] = np.sin(ang)
    ca = np.zeros((P, CA_W), np.float32)
    many = lambda dist: sum(((dist >= 0) & (dist <= w) & (dist % dil == 0)) for w, dil in ((128, 1), (512, 4), (2048, 16)))
    log = lambda n: np.where(n > 0, np.log(np.maximum(n, 1)), NEG).astype(np.float32)
    mask = lambda ok: np.where(ok, 0.0, NEG).astype(np.float32)
    for i in range(2):
        dist = (np.arange(P) + P * i)[:, None] - np.arange(SEQ)[None, :]
        ca[:, CA_PA + SEQ * i:CA_PA + SEQ * (i + 1)] = log(many(dist))
        ca[:, CA_PC + SEQ * i:CA_PC + SEQ * (i + 1)] = mask(dist >= 0)
        ca[:, CA_PB + NC_P * i:CA_PB + NC_P * (i + 1)] = mask(16 * np.arange(NC_P)[None, :] + 31 <= (np.arange(P) + P * i)[:, None])
    tt = (np.arange(64) % NT)[:, None]
    ca[0:64, CA_SA:CA_SA + NKA] = log(many(PAST + tt - np.arange(NKA)[None, :]))
    dist = 512 + tt - np.arange(NKW)[None, :]
    ca[0:64, CA_SW:CA_SW + NKW] = mask((dist >= 0) & (dist <= 512))
    ca[0:64, CA_SN:CA_SN + NT] = mask(np.arange(NT)[None, :] <= tt)
    c, j = 16 * np.arange(NC_S)[:, None], 64 * np.arange(NSEL)[None, :]
    ca[0:NC_S, CA_OV:CA_OV + NSEL] = (c < j + 64) & (c + 32 > j)
    r = np.arange(64)
    ca[0:64, CA_GS:CA_GS + 64] = (r[:, None] // 32 == r[None, :] // 32) & (r[:, None] % NT == r[None, :] % NT)
    ca[:, CA_RV:CA_RV + 14] = 13 - np.arange(14)
    return {"c0": c0, "ca": ca, "iota_pairs": np.tile(np.arange(NPAIR, dtype=np.float32), (P, 1)),
            "iota": np.tile(np.arange(P, dtype=np.float32), (P, 1))}


def layouts(x):
    a = {n: np.asarray(v) for n, v in x.items()}
    out = constants()
    rows = np.concatenate([a["x_prompt"].reshape(SEQ, D), a["x_sample"].reshape(NB * NT, D)])
    out["xT"] = rows.reshape(ROWS, KD, P).transpose(2, 1, 0)
    out["x_rows"] = rows
    w = a["w_in"][0]
    cut = np.cumsum([0, 512, 512, 512, 512] + [128] * 6 + [24])
    qa, ka, va, qb, kc, vc, ks, vs, kw, vw, gl = [w[:, cut[i]:cut[i + 1]] for i in range(11)]
    pair = [h for g in range(G) for h in (g, g + G)]
    qb = qb.reshape(D, HEADS, HD)[:, pair].reshape(D, 512)
    blocks = [qb, qa, ka, np.concatenate([ks, kw, gl], 1), va, np.concatenate([kc, vc, vs, vw], 1)]
    out["w_in"] = np.concatenate([b.reshape(KD, P, -1).transpose(1, 0, 2).reshape(P, -1) for b in blocks], 1)
    pool = lambda n: a[n][0]
    cp = [pool(n).reshape(80, 8, 8, 2, KVH, HD).transpose(0, 3, 5, 4, 2, 1) for n in ("cache_cmp_k", "cache_cmp_v")]
    out["cmp_pool"] = np.stack([c.reshape(80, P, P) for c in cp], 2).reshape(80, P, 2 * P)
    kp = pool("cache_sel_k").transpose(0, 2, 3, 1).reshape(80, P, P)
    out["sel_pool"] = np.stack([kp, pool("cache_sel_v").reshape(80, P, P)], 2).reshape(80, P, 2 * P)
    out["a_k"] = a["cache_a_k"][0].reshape(NB, PAST, 4, P).transpose(0, 3, 2, 1)
    out["a_v"] = a["cache_a_v"][0].reshape(NB, P, 8 * 512)
    out["w_k"] = a["cache_win_k"][0].reshape(NB, 512, P).transpose(0, 2, 1)
    out["w_v"] = a["cache_win_v"][0].reshape(NB, P, 4 * P)
    wo = a["w_o"][0]
    wo = np.concatenate([wo[0:512], wo[512:].reshape(HEADS, HD, D)[pair].reshape(512, D)])
    out["w_o"] = wo.reshape(KD, P, D).transpose(1, 0, 2)
    for n in ("ln1_g", "ln1_b", "ln2_g", "ln2_b"):
        out[n] = a[n][0]
    out["peer_wq"] = a["peer_wq"][0].reshape(KD, P, HH, P).transpose(2, 1, 0, 3)
    out["peer_keys"] = np.stack([a["peer_k1"][0], a["peer_k2"][0]], 1).reshape(HH, P, P).transpose(2, 0, 1)
    out["peer_u"] = a["peer_u"][0].reshape(P, NE, KD, P).transpose(1, 3, 2, 0).reshape(NE, P, D)
    out["peer_v"] = a["peer_v"][0].reshape(P, NE, D).transpose(1, 0, 2)
    out["page_table"] = a["page_table"].reshape(1, -1)
    for n in "kv":
        out[f"w1{n}"] = a[f"cmp_w1_{n}"][0].reshape(CMP_W1, P, 256).transpose(1, 0, 2)
        out[f"w2{n}"] = a[f"cmp_w2_{n}"][0].reshape(2, P, HD).transpose(1, 0, 2)
    out["pe"] = np.stack([a[f"cmp_pe_{n}"][0].reshape(CMP_W1, P).T for n in "kv"], 1)
    return {n: np.ascontiguousarray(v) for n, v in out.items()}


OUTS = {"o_ak": (ROWS, 512), "o_av": (ROWS, 512), "o_kv": (ROWS, 512), "o_ksw": (ROWS, 256), "o_y": (ROWS, D),
        "keep_ak": (NB, P, 4, PAST - NT), "keep_av": (NB, P - 1, 8 * 512),
        "keep_wk": (NB, P, 512 - NT), "keep_wv": (NB, P - 2, 4 * P)}
SEMS = """x_in proj w_in0 w_in1 c0 w1 evac roped out0 out_kv gate gate_e gate_a gate_out turned turned_out rope_c
ptab c16 cmp_slot_free cmp_pg0 cmp_pg1 cmp_b cmp_bias cmp_turn cmp_rp cmp_hid cmp_gelu cmp_second cmp_done
ca gs ld_ka0 ld_ka1 ld_kw0 ld_kw1 ld_pg0 ld_pg1 ld_v0 ld_v1 st_k0 st_k1 st_v0 st_v1 diag0 diag
p_scores p_masked p_max p_cmax p_csum p_exp p_rec p_fac p_turned p_turned_out p_pv p_normed p_O_turned p_OT
s_scores s_read s_max s_exp s_rec s_fac s_w1 s_weights s_turned s_turned_out s_pv s_OT i_pc i_mm i_cp i_sel i_pen
ld_wo0 ld_wo1 ld_wo2 ld_wo3 ld_xr ld_ky ld_wq0 ld_wq1 ld_wq2 ld_wq3 o_mm x_turn x_out x_hi x_lo q_mm q_out sc_mm sc_out
l1_sum l1_st l1_var l1_root l1_g l1_ln top topr topb top2 ixf be ber beb bei pr128 pair bf g_max g_sub g_exp g_den g_fin
id_eq id_mul id_sum ids id_turn id_out split
l2_sum l2_st l2_var l2_root l2_g l2_ln ld_u0 ld_u1 ld_v20 ld_v21 ld_ln2 u_hi u_lo v_hi v_lo h_mm gelu hw hw_hi hw_lo y_mm
c_mm W_out onehot oh_e zero iota iota_in st_y""".split()


def build(nc, d, upto=9):
    with ExitStack() as ctx:
        sb = lambda n, sh, dt=F32: ctx.enter_context(nc.sbuf_tensor(n, sh, dt))
        s = {n: ctx.enter_context(nc.semaphore(n)) for n in SEMS}
        t = Names()
        t.psum = ctx.enter_context(nc.psum_tensor("psum", [P, 8, 512], F32))
        t.c0 = sb("c0", [P, C0_W])
        t.OT = sb("OT", [P, KD, ROWS])
        att = ctx.enter_context(ExitStack())
        ab = lambda n, sh, dt=F32: att.enter_context(nc.sbuf_tensor(n, sh, dt))
        t.hk = ab("h_keep", [P, TILES, HK_W])
        t.TT = ab("qk_turned", [P, NTT, ROWS])
        t.gates = ab("gates", [P, TILES, 24])
        t.kc = ab("kc", [P, NB + 1, NC_S])
        t.vc = ab("vc", [NC_S, NB + 1, P])
        t.ptab = ab("ptab", [1, NB * PAGES], I32)
        with ExitStack() as c1:
            cb = lambda n, sh, dt=F32: c1.enter_context(nc.sbuf_tensor(n, sh, dt))
            t.w1k, t.w1v = cb("w1k", [P, CMP_W1, 256]), cb("w1v", [P, CMP_W1, 256])
            t.w2k, t.w2v = cb("w2k", [P, 2, HD]), cb("w2v", [P, 2, HD])
            t.pe = cb("pe", [P, 2, CMP_W1])
            project_block(nc, d, t, s)
            compress_block(nc, d, t, s)
        attention_block(nc, d, t, s)
        att.close()
        t.x1 = sb("x1", [P, TILES, D])
        t.x1h, t.x1l = sb("x1_hi", [P, KD, ROWS], F32R), sb("x1_lo", [P, KD, ROWS], F32R)
        t.i1 = sb("i1", [P, ROWS], BF16)
        t.i2 = sb("i2", [P, SEGS, ROWS], BF16)
        t.gp = sb("gate_parts", [P, 3, ROWS], BF16)
        route_block(nc, d, t, s)
        expert_block(nc, d, t, s)


def kernel(**inputs):
    import concourse.bacc as bacc
    from concourse.bass_utils import run_bass_kernel_spmd

    nc = bacc.Bacc("TRN2", target_bir_lowering=False, num_devices=1)
    arrays = layouts(inputs)
    d = Names()
    for n, v in arrays.items():
        d.__dict__[n] = nc.dram_tensor("in_" + n, v.shape, mybir.dt.from_np(v.dtype), kind="ExternalInput").ap()
    for n, shape in OUTS.items():
        d.__dict__[n] = nc.dram_tensor(n, shape, F32, kind="ExternalOutput").ap()
    d.gate_rows = nc.dram_tensor("gate_rows", (NB * NT, 24), F32, kind="Internal").ap()
    build(nc, d)
    r = run_bass_kernel_spmd(nc, [{"in_" + n: v for n, v in arrays.items()}], core_ids=[0]).results[0]
    o = {n: r[n] for n in OUTS}
    new = lambda a: a[SEQ:].reshape(1, NB, NT, -1, HD)
    old = lambda a: a[:SEQ].reshape(1, 1, SEQ, -1, HD)
    kc, vc, vs, vw = [o["o_kv"][:, P * i:P * (i + 1)] for i in range(4)]
    ks, kw = o["o_ksw"][:, 0:P], o["o_ksw"][:, P:2 * P]
    join = lambda kept, fresh: np.concatenate([kept, new(fresh)], 2)
    a_k = o["keep_ak"].transpose(0, 3, 2, 1).reshape(1, NB, PAST - NT, HEADS, HD)
    a_v = o["keep_av"].reshape(1, NB, PAST - NT, HEADS, HD)
    w_k = o["keep_wk"].transpose(0, 2, 1).reshape(1, NB, 512 - NT, KVH, HD)
    w_v = o["keep_wv"].reshape(1, NB, 512 - NT, KVH, HD)
    y = o["o_y"]
    return (y[:SEQ].reshape(1, SEQ, D), y[SEQ:].reshape(NB, NT, D),
            old(o["o_ak"]), old(o["o_av"]), old(kc), old(vc), old(ks), old(vs), old(kw), old(vw),
            join(a_k, o["o_ak"]), join(a_v, o["o_av"]), new(kc), new(vc), new(ks), new(vs),
            join(w_k, kw), join(w_v, vw))
```

```python
from contextlib import ExitStack

import numpy as np
import concourse.bass as bass
from concourse import mybir

F32 = mybir.dt.float32
F32R = mybir.dt.float32r
BF16 = mybir.dt.bfloat16
I32 = mybir.dt.int32
U32 = mybir.dt.uint32
ALU = mybir.AluOpType
ACT = mybir.ActivationFunctionType
AX = mybir.AxisListType

class Names:
    pass


P = 128
D = 1024
KD = D // P
SEQ = 256
NB = 8
NT = 8
ROWS = SEQ + NB * NT
TILES = 3
RT = [P, P, NB * NT]
PAST = 1024
HD = 64
HEADS = 8
KVH = 2
G = HEADS // KVH
SCALE = HD ** -0.5
NEG = -1e30
ROT = HD // 4
HALF = ROT // 2
ALPHA = 2.0 ** 0.25
EPS = 1e-5
TINY = float(np.finfo(np.float32).tiny)

HK_VA, HK_KC, HK_VC, HK_VS, HK_VW, HK_GL, HK_W = 0, 512, 640, 768, 896, 1024, 1048
HR_QB, HR_QR, HR_QA, HR_KA, HR_KS, HR_W = 0, 512, 1024, 1536, 2048, 2304
ROPED = (HR_W - HR_QR) // HD
WCOLS = [512, 512, 512, 280, 512, 512]
WOFF = [KD * c for c in np.cumsum([0] + WCOLS).tolist()]
QB0, QR0, QA0, KA0, KS0, KW0, NTT = 0, 4, 8, 12, 16, 17, 18

PAGES = PAST // P
CMP_W1 = 16
NC_S = 63
NC_P = 15
NC_ALL = 64 + NC_P
PE_BLOCK = 80
NG_ALL = 8 * (PAGES + 3)
C0_W = P + 2 * TILES * HALF
GELU_BANKS = 2


XP = 4
BIG_X = 2 * KVH * 16 * HD
BIG_RT = BIG_X + KD * ROWS
BIG_W2 = BIG_RT + 4 * ROPED * HALF
BIG_PE = BIG_W2 + 2 * 2 * HD
BIG_END = BIG_PE + 2 * CMP_W1


def project_block(nc, d, t, s):
    with ExitStack() as ctx:
        sb = lambda n, sh, dt=F32: ctx.enter_context(nc.sbuf_tensor(n, sh, dt))
        xT = t.big[:, BIG_X:BIG_RT].rearrange("p (k n) -> p k n", k=KD)
        w = sb("w_in_ring", [P, 2, KD * 512])
        hr = sb("h_rope", [P, TILES, HR_W])
        rt = t.big[:, BIG_RT:BIG_W2].rearrange("p (x g n) -> p x g n", x=4, g=ROPED)
        ps = [t.psum[:, i] for i in range(6)]
        pt = [t.psum[:, 6 + i].rearrange("p (c n) -> p c n", n=P) for i in range(2)]
        block = ctx.enter_context(nc.Block())
        hk, TT, c0 = t.hk, t.TT, t.c0
        ident = c0[:, 0:P]
        nblk = len(WCOLS)
        turns = [(i, g) for i in range(TILES) for g in range(5)]
        c16 = t.big[0:16, 0:BIG_X].rearrange("p (a k r n) -> p a k r n", a=2, k=KVH, r=16)
        pr = t.psum[:, 0].rearrange("p (x g) -> p x g", g=16)

        @block.sync
        def _(sp):
            for x in range(XP):
                k, c = KD // XP * x, KD // XP * (x + 1)
                sp.dma_start(xT[:, k:c], d.xT[:, k:c]).then_inc(s[f"x_in{x}"], 16)
                sp.dma_start(w[:, 0, k * 512:c * 512], d.w_in[:, k * 512:c * 512]).then_inc(s[f"x_in{x}"], 16)
            for n in range(nblk):
                if n >= 2:
                    sp.wait_ge(s["proj"], 3 * (n - 1))
                c = WCOLS[n]
                if n:
                    sp.dma_start(w[:, n % 2, 0:KD * c], d.w_in[:, WOFF[n]:WOFF[n] + KD * c]).then_inc(s[f"w_in{n % 2}"], 16)
                if n == 1:
                    sp.dma_start(c0[:], d.c0).then_inc(s["c0"], 16)
                    sp.dma_start(t.w1k[:], d.w1k).then_inc(s["w1"], 16)
                    sp.dma_start(t.w1v[:], d.w1v).then_inc(s["w1"], 16)
                    sp.dma_start(t.w2k, d.w2k).then_inc(s["w1"], 16)
                    sp.dma_start(t.w2v, d.w2v).then_inc(s["w1"], 16)
                    sp.dma_start(t.pe, d.pe).then_inc(s["pe_in"], 16)
                    sp.dma_start(t.ptab[:], d.page_table).then_inc(s["ptab"], 16)
            sp.wait_ge(s["ptab"], 16)
            for b in range(2):
                load_cmp_pages(sp, t, d, s, b, b * PAGES)
            sp.wait_ge(s["evac"], 3 * nblk)
            for i in range(TILES):
                sp.dma_start(d.o_kv[P * i:P * i + RT[i], :], hk[0:RT[i], i, 512:1024]).then_inc(s["out_kv"], 16)
            sp.wait_ge(s["out_kv"], 48)
            for x in range(2 * KVH):
                sp.dma_start(c16[:, x // KVH, x % KVH], d.o_kv.rearrange("(j r) c -> j r c", r=16)[0:16, :, x * HD:(x + 1) * HD])\
                  .then_inc(s["c16"], 16)
            for i in range(TILES):
                r, o = RT[i], P * i
                sp.dma_start(d.o_av[o:o + r, :], hk[0:r, i, 0:512]).then_inc(s["out0"], 16)
                sp.wait_ge(s["roped"], i + 1)
                sp.dma_start(d.o_ak[o:o + r, :], hr[0:r, i, HR_KA:HR_KS]).then_inc(s["out0"], 16)
                sp.dma_start(d.o_ksw[o:o + r, :], hr[0:r, i, HR_KS:HR_W]).then_inc(s["out0"], 16)
            sp.wait_ge(s["gate"], 2)
            sp.dma_start(d.gate_rows, t.gates[0:RT[2], 2, :]).then_inc(s["gate_out"], 16)
            sp.wait_ge(s["out0"], 16 * 9)
            sp.wait_ge(s["gate_out"], 16)

        @block.tensor
        def _(pe):
            for n in range(nblk):
                if n:
                    pe.wait_ge(s[f"w_in{n % 2}"], 16 * ((n + 1) // 2))
                c = WCOLS[n]
                for i in range(TILES):
                    if n >= 2:
                        pe.wait_ge(s["evac"], 3 * (n - 2) + i + 1)
                    out = ps[3 * (n % 2) + i]
                    for k in range(KD):
                        if n == 0 and i == 0 and k % (KD // XP) == 0:
                            pe.wait_ge(s[f"x_in{k * XP // KD}"], 32)
                        mm = pe.matmul(out[0:RT[i], 0:c], xT[:, k, P * i:P * i + RT[i]],
                                       w[:, n % 2, k * c:(k + 1) * c], start=(k == 0), stop=(k == KD - 1))
                    mm.then_inc(s["proj"], 1)
            pe.wait_ge(s["c0"], 16)
            for u, (i, g) in enumerate(turns):
                pe.wait_ge(s["roped"], i + 1)
                if u >= 2:
                    pe.wait_ge(s["turned_out"], u - 1)
                for c in range(4 if g < 4 else 2):
                    mm = pe.transpose(pt[u % 2][:, c, 0:RT[i]], hr[0:RT[i], i, (4 * g + c) * P:(4 * g + c + 1) * P],
                                      ident[0:RT[i], 0:RT[i]])
                mm.then_inc(s["turned"], 1)
            pe.wait_ge(s["c16"], 64)
            pe.wait_ge(s["evac"], 3 * nblk)
            for a in range(2):
                for k in range(KVH):
                    for r in range(8):
                        mm = pe.transpose(pr[:, (a * KVH + k) * 8 + r, :], c16[0:16, a, k, 2 * r:2 * r + 2, :].rearrange("j r e -> j (r e)"), ident[0:16, 0:16])
            mm.then_inc(s["cmp_turn"], 1)

        @block.scalar
        def _(act):
            for n in range(nblk):
                for i in range(TILES):
                    act.wait_ge(s["proj"], 3 * n + i + 1)
                    r, src = RT[i], ps[3 * (n % 2) + i]
                    if n == 0:
                        ins = act.activation(hr[0:r, i, HR_QB:HR_QB + 512], src[0:r, :], ACT.Copy)
                    elif n in (1, 2):
                        ins = act.activation(hr[0:r, i, 512 * (n + 1):512 * (n + 2)], src[0:r, :], ACT.Copy)
                    elif n == 3:
                        act.activation(hr[0:r, i, HR_KS:HR_W], src[0:r, 0:256], ACT.Copy)
                        ins = act.activation(hk[0:r, i, HK_GL:HK_W], src[0:r, 256:280], ACT.Copy)
                    else:
                        ins = act.activation(hk[0:r, i, 512 * (n - 4):512 * (n - 3)], src[0:r, :], ACT.Copy)
                    ins.then_inc(s["evac"], 1)
            act.wait_ge(s["evac"], 12)
            act.activation(t.gates[:, 0:2, :], hk[:, 0:2, HK_GL:HK_W], ACT.Exp, scale=-1.0).then_inc(s["gate_e"], 1)
            act.activation(t.gates[0:RT[2], 2, :], hk[0:RT[2], 2, HK_GL:HK_W], ACT.Exp, scale=-1.0).then_inc(s["gate_e"], 1)

        @block.vector
        def _(ve):
            cos = lambda i: c0[:, P + HALF * i:P + HALF * (i + 1)]
            sin = lambda i: c0[:, P + HALF * (TILES + i):P + HALF * (TILES + i + 1)]
            ve.wait_ge(s["c0"], 16)
            for i in range(TILES):
                r = RT[i]
                ve.wait_ge(s["evac"], 9 + i + 1)
                ve.tensor_copy(hr[0:r, i, HR_QR:HR_QA], hr[0:r, i, HR_QB:HR_QR]).then_inc(s["rope_c"], 1)
                ve.wait_ge(s["rope_c"], 3 * i + 1)
                z = hr[0:r, i, HR_QR:HR_W].rearrange("p (g d) -> p g d", d=HD)
                x1, x2 = z[:, :, 0:HALF], z[:, :, HALF:ROT]
                cb = cos(i)[0:r].unsqueeze(1).broadcast_to([r, ROPED, HALF])
                sn = sin(i)[0:r].unsqueeze(1).broadcast_to([r, ROPED, HALF])
                if i:
                    ve.wait_ge(s["roped"], i)
                for j, (a, b) in enumerate([(x1, cb), (x2, sn), (x2, cb), (x1, sn)]):
                    ins = ve.tensor_tensor(rt[0:r, j], a, b, ALU.mult)
                ins.then_inc(s["rope_c"], 1)
                ve.wait_ge(s["rope_c"], 3 * i + 2)
                ve.tensor_tensor(x1, rt[0:r, 0], rt[0:r, 1], ALU.subtract).then_inc(s["rope_c"], 1)
                ve.tensor_tensor(x2, rt[0:r, 2], rt[0:r, 3], ALU.add).then_inc(s["roped"], 1)
            for u, (i, g) in enumerate(turns):
                ve.wait_ge(s["turned"], u + 1)
                n = 4 if g < 4 else 2
                ve.tensor_copy(TT[:, 4 * g:4 * g + n, P * i:P * i + RT[i]], pt[u % 2][:, 0:n, 0:RT[i]]).then_inc(s["turned_out"], 1)
            ve.wait_ge(s["gate_e"], 2)
            g2 = [t.gates[:, 0:2, :], t.gates[0:RT[2], 2, :]]
            for a in g2:
                ve.tensor_scalar(a, a, 1.0, None, ALU.add).then_inc(s["gate_a"], 1)
            ve.wait_ge(s["gate_a"], 2)
            for a in g2:
                ve.reciprocal(a, a).then_inc(s["gate"], 1)
            own = t.cpg[:, 0, PAGES:PAGES + 2].rearrange("p w a k r g -> p (a k r) w g")
            ve.wait_ge(s["cmp_zero"], 1)
            ve.wait_ge(s["pe_in"], 16)
            for g in range(2):
                for k in range(KVH):
                    ve.tensor_copy(t.cpg[:, 0, PAGES + 2, :, k, :, g], t.pe[:, :, 8 * g:8 * g + 8])
            ve.wait_ge(s["cmp_turn"], 1)
            ve.tensor_copy(own, pr.rearrange("p x (w g) -> p x w g", w=2)).then_inc(s["cmp_rp"], 1)

        @block.gpsimd
        def _(gp):
            gp.memset(t.cpg[:, 0, PAGES + 2], 0.0).then_inc(s["cmp_zero"], 1)


def load_cmp_pages(eng, t, d, s, slot, first):
    for p in range(PAGES):
        r = eng.value_load(t.ptab[0:1, bass.ds(first + p, 1)], min_val=0, max_val=79)
        eng.dma_start(t.cpg[:, slot, p].rearrange("p a k r g -> p (a k r g)"),
                      d.cmp_pool[bass.ds(r, 1)].rearrange("a p n -> p (a n)")).then_inc(s[f"cmp_pg{slot}"], 16)


def compress_block(nc, d, t, s):
    with ExitStack() as ctx:
        sb = lambda n, sh, dt=F32: ctx.enter_context(nc.sbuf_tensor(n, sh, dt))
        hid = sb("cmp_hidden", [P, 2, 2, KVH, NC_ALL])
        bias = sb("cmp_bias", [P, 2, 2])
        ph = [t.psum[:, i, 0:4 * (NG_ALL + 1)].rearrange("p (h k n) -> p h k n", h=2, k=KVH) for i in range(2)]
        po = [t.psum[:, 2 + i] for i in range(2)]
        block = ctx.enter_context(nc.Block())
        pages, w1, w2 = t.cpg, [t.w1k, t.w1v], [t.w2k, t.w2v]
        units = [(b, a) for b in range(NB) for a in range(2)]
        blocks = lambda b: NC_S if b else NC_ALL

        @block.sync
        def _(sp):
            sp.dma_start(t.ca[:], d.ca).then_inc(s["ca"], 16)
            for br in range(3):
                rows = d.gate_rows.rearrange("(b t) (r h) -> r h t b", t=NT, r=3)[br]
                for h in range(HEADS):
                    sp.dma_start(t.gs[h * NT:(h + 1) * NT, :, br], rows[h], allow_slow_non_contiguous=True).then_inc(s["gs"], 16)
            with sp.Fori(0, NB // 2 - 1) as i:
                for b in range(2):
                    sp.wait_ge(s["cmp_slot_free"], i * 4 + (2 * b + 2))
                    load_cmp_pages(sp, t, d, s, b, i * (2 * PAGES) + (b + 2) * PAGES)

        @block.tensor
        def _(pe):
            pe.wait_ge(s["w1"], 64)

            def hidden(u):
                b, a = units[u]
                pe.wait_ge(s[f"cmp_pg{b % 2}"], 16 * PAGES * (b // 2 + 1))
                if u >= 2:
                    pe.wait_ge(s["cmp_gelu"], 2 * (u - 1))
                pages_n = PAGES if b else PAGES + 3
                n = 8 * pages_n
                for h in range(2):
                    for c in range(CMP_W1):
                        rhs = pages[:, b % 2, 0:pages_n, a, :, c % 8, :].rearrange("p g k b -> p k g b")
                        o = ph[u % 2][:, h, :, 1:1 + n] if c < 8 else ph[u % 2][:, h, :, 0:n]
                        mm = pe.matmul(o.rearrange("p k (g b) -> p k g b", b=8), w1[a][:, c, h * P:(h + 1) * P], rhs,
                                       start=(c == 0), stop=(c == CMP_W1 - 1), skip_group_check=True)
                mm.then_inc(s["cmp_hid"], 1)

            def second(u):
                b, a = units[u]
                n = blocks(b)
                pe.wait_ge(s["cmp_gelu"], 2 * (u + 1))
                if u >= 2:
                    pe.wait_ge(s["cmp_done"], u - 1)
                if a == 0:
                    for k in range(KVH):
                        for h in range(2):
                            mm = pe.matmul(po[u % 2][k * HD:(k + 1) * HD, 0:n], w2[0][:, h, :], hid[:, u % 2, h, k, 0:n], start=(h == 0), stop=(h == 1))
                else:
                    for x, (c0, c1) in enumerate([(0, NC_S)] if b else [(0, NC_S), (64, NC_ALL)]):
                        for k in range(KVH):
                            for h in range(2):
                                mm = pe.matmul(po[u % 2][0:c1 - c0, x * P + k * HD:x * P + (k + 1) * HD], hid[:, u % 2, h, k, c0:c1], w2[1][:, h, :],
                                               start=(h == 0), stop=(h == 1))
                mm.then_inc(s["cmp_second"], 1)

            for u in range(len(units)):
                hidden(u)
                if u >= 1:
                    second(u - 1)
            second(len(units) - 1)

        @block.scalar
        def _(act):
            for u, (b, a) in enumerate(units):
                n = blocks(b)
                act.wait_ge(s["cmp_hid"], u + 1)
                if b == 0:
                    act.wait_ge(s["cmp_bias"], a + 1)
                if u >= 2:
                    act.wait_ge(s["cmp_second"], u - 1)
                for h in range(2):
                    act.activation(hid[:, u % 2, h, :, 0:n], ph[u % 2][:, h, :, 1:1 + n], ACT.Gelu_apprx_tanh,
                                   bias=bias[:, a, h:h + 1]).then_inc(s["cmp_gelu"], 1)

        @block.vector
        def _(ve):
            for u, (b, a) in enumerate(units):
                ve.wait_ge(s["cmp_hid"], u + 1)
                ve.sem_inc(s["cmp_slot_free"], 1)
                if b == 0:
                    ve.tensor_copy(bias[:, a, :], ph[u % 2][:, :, 0, 1 + PE_BLOCK]).then_inc(s["cmp_bias"], 1)
                ve.wait_ge(s["cmp_second"], u + 1)
                if a == 0:
                    if b == 0:
                        ve.tensor_copy(t.kc[:, NB, 0:NC_P], po[u % 2][:, 64:NC_ALL])
                    ve.tensor_copy(t.kc[:, b, :], po[u % 2][:, 0:NC_S]).then_inc(s["cmp_done"], 1)
                else:
                    if b == 0:
                        ve.tensor_copy(t.vc[0:NC_P, NB, :], po[u % 2][0:NC_P, P:2 * P])
                    ve.tensor_copy(t.vc[:, b, :], po[u % 2][0:NC_S, 0:P]).then_inc(s["cmp_done"], 1)


NKA, NKW = PAST + NT, 512 + NT
SS, SW = 0, NKA
SB_COLS = NKA + NKW
PR = 32
CA_PA = 0
CA_PC = CA_PA + 3 * P
CA_PB = CA_PC + 3 * P
CA_SA = CA_PB + 2 * NC_P
CA_SW = CA_SA + NKA
CA_SN = CA_SW + NKW
CA_OV = CA_SN + NT
CA_GS = CA_OV + 17
CA_RV = CA_GS + 64
CA_W = CA_RV + 14
NSEL = 17


def attention_block(nc, d, t, s):
    with ExitStack() as ctx:
        sb = lambda n, sh, dt=F32: ctx.enter_context(nc.sbuf_tensor(n, sh, dt))
        wk = sb("att_work", [P, 2 * (NKA + SB_COLS)])
        pp = wk[:, 0:2048].rearrange("p (s e n) -> p s e n", s=4, e=2)
        pT = wk[:, 2048:3072].rearrange("p (s x q) -> p s x q", s=2, x=4)
        nm = sb("att_negmax", [P, 64])
        sm = sb("att_sum", [P, 64])
        rs = sb("att_rsum", [P, 64])
        qd = wk[:, 3072:4096].rearrange("p (s e q) -> p s e q", s=4, e=2)
        ka = t.big[:].rearrange("p (s c n) -> p s c n", s=2, c=4)
        va = sb("a_vals", [P, 2, 8, 512])
        pg = sb("sel_pages", [P, 2, PAGES, 2, P])
        kw = sb("win_keys", [P, 2, 512])
        vw = sb("win_vals", [P, 2, 4, P])
        vn = sb("new_vals", [NT, 2, 768])
        qa = sb("qa_diag", [P, NB, 4, PR])
        qn = sb("qn_diag", [P, 2, NB, 64])
        sA = wk[:, 0:2 * NKA].rearrange("p (s n) -> p s n", s=2)
        sB = wk[0:64, 2 * NKA:2 * (NKA + SB_COLS)].rearrange("p (s n) -> p s n", s=2)
        zA = sb("smp_turned_a", [P, 2, 8, P])
        zAn = sb("smp_turned_a_new", [NT, 2, P])
        zB = sb("smp_turned_b", [P, 2, 14, 64])
        oA = sb("smp_out_a", [P, 2, P])
        oB = sb("smp_out_b", [64, 2, P])
        stA = sb("smp_stats_a", [P, NB, 3])
        stB = sb("smp_stats_b", [64, NB, 2, 4])
        pc = wk[0:64, 0:NB * NC_S].rearrange("p (b n) -> p b n", n=NC_S)
        pcT = sb("smp_cmp_turned", [NC_S, NB, 64])
        cst = sb("smp_cmp_stats", [64, 2, NB])
        x1 = wk[0:64, 512:512 + NB * NSEL]
        imp = wk[0:64, 704:704 + NB * 14].rearrange("p (b j) -> p b j", j=14)
        top = wk[0:64, 832:832 + NB * 8].rearrange("p (b j) -> p b j", j=8)
        tix = sb("smp_topi", [64, NB, 8], U32)
        tif = sb("smp_topf", [64, NB])
        pen = sb("smp_pen", [64, NB, 16])
        block = ctx.enter_context(nc.Block())
        hk, TT, OT, ident = t.hk, t.TT, t.OT, t.c0[:, 0:P]
        ca, gs = t.ca, t.gs
        bank = lambda i: t.psum[:, i]
        KINDS = ["A", "cmp", "sel", "win"]
        units = [(i, c, k) for i in range(2) for c in range(4) for k in KINDS]
        NU = len(units)

        def shape(u):
            i, _, k = units[u]
            return (NC_P, 1, NC_P) if k == "cmp" else (P * (i + 1), i + 1, P)

        def queries(u):
            return 3 * (u // 4) + min(u % 4, 2)

        last_reader = lambda x: 4 * (x // 3) + (0, 1, 3)[x % 3]

        chunk = lambda b, n: 6 * b + n

        @block.sync
        def _(sp):
            for b in range(NB):
                q = b % 2
                if b >= 2:
                    sp.wait_ge(s["s_scores"], chunk(b - 2, 3) + 1)
                sp.dma_start(ka[:, q], d.a_k[b]).then_inc(s[f"ld_ka{q}"], 16)
                sp.dma_start(kw[:, q], d.w_k[b]).then_inc(s[f"ld_ka{q}"], 16)
                if b >= 2:
                    sp.wait_ge(s["s_sel_used"], b - 1)
                for p in range(PAGES):
                    r = sp.value_load(t.ptab[0:1, b * PAGES + p:b * PAGES + p + 1], min_val=0, max_val=79)
                    sp.dma_start(pg[:, q, p].rearrange("p a n -> p (a n)"),
                                 d.sel_pool[bass.ds(r, 1)].rearrange("a p n -> p (a n)")).then_inc(s[f"ld_pg{q}"], 16)
                if b >= 2:
                    sp.wait_ge(s["s_pv"], b - 1)
                sp.dma_start(va[:, q].rearrange("p j n -> p (j n)"), d.a_v[b]).then_inc(s[f"ld_v{q}"], 16)
                sp.dma_start(vw[:, q].rearrange("p j n -> p (j n)"), d.w_v[b]).then_inc(s[f"ld_v{q}"], 16)
                o = SEQ + NT * b
                sp.dma_start(vn[:, q, 0:512], d.o_av[o:o + NT, :]).then_inc(s[f"ld_v{q}"], 16)
                sp.dma_start(vn[:, q, 512:768], d.o_kv[o:o + NT, 256:512]).then_inc(s[f"ld_v{q}"], 16)
            wo = t.big[:].rearrange("p (k n) -> p k n", k=KD)
            for k in range(0, KD, 2):
                if k == 0 or k == 4:
                    sp.wait_ge(s["s_scores"], chunk(NB - 2 + k // 4, 3) + 1)
                sp.dma_start(wo[:, k:k + 2], d.w_o[:, k:k + 2]).then_inc(s[f"ld_wo{k // 4}"], 16)

        @block.gpsimd
        def _(gp):
            gp.memset(qd, 0.0).then_inc(s["p_zero"], 1)
            gp.memset(qa[:], 0.0).then_inc(s["diag0"], 1)
            gp.memset(qn[:], 0.0).then_inc(s["diag0"], 1)
            gp.memset(pen[:], 0.0).then_inc(s["diag0"], 1)
            gp.wait_ge(s["p_zero"], 1)
            gp.wait_ge(s["diag0"], 3)
            for x in range(3 * NU // 4):
                i, c, k = units[last_reader(x)]
                q = {"A": QA0, "cmp": QB0, "win": QR0}[k] + c
                if x >= 4:
                    gp.wait_ge(s["p_scores"], last_reader(x - 4) + 1)
                for e in range(2):
                    h = slice(e * HD, (e + 1) * HD)
                    ins = gp.tensor_copy(qd[h, x % 4, e, :], TT[h, q, P * i:P * i + P])
                ins.then_inc(s["p_q"], 1)

        @block.tensor
        def _(pe):
            def p_scores(u):
                i, c, k = units[u]
                n = shape(u)[0]
                if u >= 2:
                    pe.wait_ge(s["p_masked"], u - 1)
                pe.wait_ge(s["p_q"], queries(u) + 1)
                keys = {"A": TT[:, KA0 + c, 0:n], "cmp": t.kc[:, NB, 0:min(n, NC_P)], "sel": TT[:, KS0, 0:n], "win": TT[:, KW0, 0:n]}[k]
                for e in range(2):
                    mm = pe.matmul(bank(2 * (u % 2) + e)[:, 0:n], qd[:, queries(u) % 4, e, :], keys, start=True, stop=True)
                mm.then_inc(s["p_scores"], 1)

            def p_turn(u):
                n, nk, kr = shape(u)
                pe.wait_ge(s["p_weighed"], u + 1)
                if u >= 2:
                    pe.wait_ge(s["p_turned_out"], u - 1)
                for e in range(2):
                    for x in range(nk):
                        mm = pe.transpose(bank(4 + u % 2)[0:kr, (2 * e + x) * P:(2 * e + x + 1) * P], pp[:, u % 4, e, x * P:x * P + kr], ident)
                mm.then_inc(s["p_turned"], 1)

            def p_pv(u):
                i, c, k = units[u]
                n, nk, kr = shape(u)
                pe.wait_ge(s["p_turned_out"], u + 1)
                g = u // 4
                if g and k in ("A", "cmp"):
                    pe.wait_ge(s["p_OT"], 2 * g - (k == "A"))
                for x in range(nk):
                    for e in range(2):
                        v = {"A": hk[:, x, (2 * c + e) * HD:(2 * c + e + 1) * HD], "cmp": t.vc[0:min(kr, NC_P), NB, e * HD:(e + 1) * HD],
                             "sel": hk[:, x, HK_VS + e * HD:HK_VS + (e + 1) * HD],
                             "win": hk[:, x, HK_VW + e * HD:HK_VW + (e + 1) * HD]}[k]
                        mm = pe.matmul(bank(6 + (k != "A"))[e * HD:(e + 1) * HD, 0:P], v, pT[0:kr, u % 2, 2 * e + x, :],
                                       start=(x == 0 and k in ("A", "cmp")), stop=(x == nk - 1 and k in ("A", "win")), skip_group_check=True)
                mm.then_inc(s["p_pv"], 1)

            for u in range(NU + 3):
                if u < NU:
                    p_scores(u)
                if 2 <= u < NU + 2:
                    p_turn(u - 2)
                if u >= 3:
                    p_pv(u - 3)
            pe.wait_ge(s["diag"], 12)
            for b in range(NB):
                mm = pe.matmul(bank(0)[0:64, b * NC_S:(b + 1) * NC_S], qn[:, 0, b, :], t.kc[:, b, :], start=True, stop=True)
            mm.then_inc(s["i_mm"], 1)
            pe.wait_ge(s["i_pc"], 4)
            for b in range(NB):
                mm = pe.transpose(bank(1)[0:NC_S, b * 64:(b + 1) * 64], pc[:, b, :], ident[0:64, 0:64])
            mm.then_inc(s["i_mm"], 1)
            pe.wait_ge(s["i_pc"], 5)
            for b in range(NB):
                mm = pe.matmul(bank(2)[0:64, b * NSEL:(b + 1) * NSEL], pcT[:, b, :], ca[0:NC_S, CA_OV:CA_OV + NSEL], start=True, stop=True)
            mm.then_inc(s["i_mm"], 1)
            pe.wait_ge(s["i_pc"], 6)
            pe.matmul(bank(7)[0:64, 0:NB * NSEL], ca[0:64, CA_GS:CA_GS + 64], x1[:], start=True, stop=True).then_inc(s["i_mm"], 1)

            def chunk_begin(b, n):
                q = chunk(b, n)
                if q >= 3:
                    pe.wait_ge(s["s_read"], q - 2)
                return bank(q % 3)

            def scores(b):
                q = b % 2
                o = chunk_begin(b, 0)
                r = slice(SEQ + NT * b, SEQ + NT * (b + 1))
                for c in range(4):
                    pe.matmul(o[c * PR:(c + 1) * PR, 0:NT], qa[:, b, c, :], TT[:, KA0 + c, r], start=True, stop=True)
                pe.matmul(o[0:64, 8:16], qn[:, 1, b, :], TT[:, KS0, r], start=True, stop=True)
                pe.matmul(o[0:64, 16:24], qn[:, 1, b, :], TT[:, KW0, r], start=True, stop=True).then_inc(s["s_scores"], 1)
                pe.wait_ge(s[f"ld_ka{q}"], 32 * (b // 2 + 1))
                for x in range(2):
                    o = chunk_begin(b, 1 + x)
                    for c in range(4):
                        mm = pe.matmul(o[c * PR:(c + 1) * PR, :], qa[:, b, c, :], ka[:, q, c, x * 512:(x + 1) * 512], start=True, stop=True)
                    mm.then_inc(s["s_scores"], 1)
                o = chunk_begin(b, 3)
                pe.matmul(o[0:64, :], qn[:, 1, b, :], kw[:, q, :], start=True, stop=True).then_inc(s["s_scores"], 1)

            def sel_scores(b):
                q = b % 2
                pe.wait_ge(s[f"ld_pg{q}"], 16 * PAGES * (b // 2 + 1))
                for x in range(2):
                    o = chunk_begin(b, 4 + x)
                    pe.matmul(o[0:64, :], qn[:, 1, b, :], pg[:, q, 4 * x:4 * x + 4, 0, :], start=True, stop=True).then_inc(s["s_scores"], 1)

            def turn(b, n):
                w = 4 * b + n
                pe.wait_ge(s["s_exp"], 3 * b + (1 if n < 2 else 3))
                if w >= 2:
                    pe.wait_ge(s["s_turned_out"], w - 1)
                o = bank(3 + w % 2)
                a, z = sA[:, b % 2, :], sB[:, b % 2, :]
                id64 = ident[0:64, 0:64]
                if n < 2:
                    for j in range(4):
                        mm = pe.transpose(o[:, j * P:(j + 1) * P], a[:, 4 * n + j:PAST:8], ident)
                elif n == 2:
                    for j in range(8):
                        mm = pe.transpose(o[:, j * 64:(j + 1) * 64], z[:, SS + j * P:SS + (j + 1) * P], id64)
                else:
                    for j in range(4):
                        pe.transpose(o[:, j * 64:(j + 1) * 64], z[:, SW + j:SW + 512:4], id64)
                    pe.transpose(o[0:NT, 256:320], z[:, SS + PAST:SS + NKA], id64)
                    pe.transpose(o[0:NT, 320:384], z[:, SW + 512:SW + NKW], id64)
                    mm = pe.transpose(o[0:NT, 384:512], a[:, PAST:NKA], ident)
                mm.then_inc(s["s_turned"], 1)

            def values(b):
                q = b % 2
                pe.wait_ge(s["s_turned_out"], 4 * b + 4)
                pe.wait_ge(s[f"ld_v{q}"], 64 * (b // 2 + 1))
                if b >= 2:
                    pe.wait_ge(s["s_normed"], b - 1)
                o = bank(5 + q)
                for j in range(8):
                    mm = pe.matmul(o[0:64, 2 * P:3 * P], zB[:, q, j, :], pg[:, q, j, 1, :], start=(j == 0), stop=False)
                mm.then_inc(s["s_sel_used"], 1)
                pe.matmul(o[0:64, 2 * P:3 * P], zB[0:NT, q, 12, :], vn[:, q, 512:640], start=False, stop=True)
                pe.matmul(o[0:64, P:2 * P], pcT[:, b, :], t.vc[:, b, :], start=True, stop=True)
                for j in range(4):
                    pe.matmul(o[0:64, 3 * P:4 * P], zB[:, q, 8 + j, :], vw[:, q, j, :], start=(j == 0), stop=False)
                pe.matmul(o[0:64, 3 * P:4 * P], zB[0:NT, q, 13, :], vn[:, q, 640:768], start=False, stop=True)
                for j in range(9):
                    for c in range(4):
                        w, v = (zA[:, q, j, :], va[:, q, j, :]) if j < 8 else (zAn[:, q, :], vn[:, q, 0:512])
                        mm = pe.matmul(o[c * PR:(c + 1) * PR, 0:P], w[:, c * PR:(c + 1) * PR], v[:, c * P:(c + 1) * P], start=(j == 0), stop=(j == 8))
                mm.then_inc(s["s_pv"], 1)

            def turn_out(b):
                pe.wait_ge(s["s_normed"], b + 1)
                if b:
                    pe.wait_ge(s["s_OT"], b)
                pe.transpose(bank(7)[:, 0:P], oA[:, b % 2, :], ident)
                pe.transpose(bank(7)[:, P:P + 64], oB[:, b % 2, :], ident[0:64, 0:64]).then_inc(s["s_out_turned"], 1)

            pe.wait_ge(s["i_sel"], 1)
            for b in range(NB + 2):
                if b < NB:
                    scores(b)
                if 1 <= b <= NB:
                    for n in range(4):
                        turn(b - 1, n)
                if b >= 2:
                    turn_out(b - 2)
                if b < NB:
                    sel_scores(b)
                if 1 <= b <= NB:
                    values(b - 1)

        @block.scalar
        def _(act):
            def p_exp(u):
                n = shape(u)[0]
                act.wait_ge(s["p_max"], u + 1)
                for e in range(2):
                    v = pp[:, u % 4, e, 0:n]
                    ins = act.activation(v, v, ACT.Exp, bias=nm[:, 2 * u + e:2 * u + e + 1], accum_out=sm[:, 2 * u + e:2 * u + e + 1])
                ins.then_inc(s["p_exp"], 1)

            def p_out(u):
                n, nk, kr = shape(u)
                act.wait_ge(s["p_turned"], u + 1)
                if u >= 2:
                    act.wait_ge(s["p_pv"], u - 1)
                src = bank(4 + u % 2)[0:kr, :].rearrange("p (e x q) -> p e x q", e=2, x=2)[:, :, 0:nk, :]
                dst = pT[0:kr, u % 2].rearrange("p (e x) q -> p e x q", e=2)[:, :, 0:nk, :]
                act.activation(dst, src, ACT.Copy).then_inc(s["p_turned_out"], 1)

            def p_OT(u):
                i, c, k = units[u]
                act.wait_ge(s["p_pv"], u + 1)
                act.activation(OT[:, c + (0 if k == "A" else 4), P * i:P * i + P], bank(6 + (k != "A"))[:, 0:P], ACT.Copy).then_inc(s["p_OT"], 1)

            for u in range(NU + 4):
                if u < NU:
                    p_exp(u)
                if 2 <= u < NU + 2:
                    p_out(u - 2)
                if u >= 4 and units[u - 4][2] in ("A", "win"):
                    p_OT(u - 4)
            act.wait_ge(s["i_pc"], 2)
            act.activation(pc[:], pc[:], ACT.Exp).then_inc(s["i_pc"], 1)
            act.wait_ge(s["i_mm"], 2)
            act.activation(pcT[:].rearrange("p b r -> p (b r)"), bank(1)[0:NC_S, :], ACT.Copy).then_inc(s["i_pc"], 1)

            def s_exp(b, n):
                act.wait_ge(s["s_max"], 3 * b + n + 1)
                if n == 0:
                    v, z = sA[:, b % 2, :], stA[:, b, :]
                elif n == 1:
                    v, z = sB[:, b % 2, SW:SW + NKW], stB[:, b, 1, :]
                else:
                    v, z = sB[:, b % 2, SS:SS + NKA], stB[:, b, 0, :]
                act.activation(v, v, ACT.Exp, bias=z[:, 0:1], accum_out=z[:, 1:2]).then_inc(s["s_exp"], 1)

            def s_out(b, n):
                w, q = 4 * b + n, b % 2
                act.wait_ge(s["s_turned"], w + 1)
                if n == 0 and b >= 2:
                    act.wait_ge(s["s_pv"], b - 1)
                o = bank(3 + w % 2)
                if n < 2:
                    ins = act.activation(zA[:, q, 4 * n:4 * n + 4, :].rearrange("p j r -> p (j r)"), o, ACT.Copy)
                elif n == 2:
                    ins = act.activation(zB[:, q, 0:8, :].rearrange("p j r -> p (j r)"), o, ACT.Copy)
                else:
                    act.activation(zB[:, q, 8:12, :].rearrange("p j r -> p (j r)"), o[:, 0:256], ACT.Copy)
                    act.activation(zB[0:NT, q, 12:14, :].rearrange("p j r -> p (j r)"), o[0:NT, 256:384], ACT.Copy)
                    ins = act.activation(zAn[:, q, :], o[0:NT, 384:512], ACT.Copy)
                ins.then_inc(s["s_turned_out"], 1)

            def s_OT(b):
                act.wait_ge(s["s_out_turned"], b + 1)
                r = slice(SEQ + NT * b, SEQ + NT * (b + 1))
                o = bank(7)
                for e in range(2):
                    h = slice(e * HD, (e + 1) * HD)
                    act.activation(OT[h, 0:4, r], o[h, 0:P].rearrange("p (c q) -> p c q", c=4)[:, :, e * NT:(e + 1) * NT], ACT.Copy)
                    ins = act.activation(OT[h, 4:8, r], o[h, P:P + 64].rearrange("p (k g q) -> p k g q", k=KVH, g=G)[:, e], ACT.Copy)
                ins.then_inc(s["s_OT"], 1)

            for b in range(NB + 2):
                if b < NB:
                    s_exp(b, 0)
                if 1 <= b <= NB:
                    for n in range(3):
                        s_out(b - 1, n)
                if b < NB:
                    s_exp(b, 1)
                if 1 <= b <= NB:
                    s_out(b - 1, 3)
                if b >= 2:
                    s_OT(b - 2)
                if b < NB:
                    s_exp(b, 2)

        @block.vector
        def _(ve):
            def sample_queries():
                ve.wait_ge(s["diag0"], 3)
                for c in range(4):
                    for e in range(2):
                        h = slice(e * HD, (e + 1) * HD)
                        n = e * NT
                        ve.tensor_copy(qa[h, :, c, n:n + NT], TT[h, QA0 + c, SEQ:ROWS].rearrange("p (b t) -> p b t", t=NT)).then_inc(s["diag"], 1)
                for x, q0 in enumerate((QB0, QR0)):
                    for e in range(2):
                        h = slice(e * HD, (e + 1) * HD)
                        ve.tensor_copy(qn[h, x, :, e * 32:(e + 1) * 32].rearrange("p b (g t) -> p b g t", t=NT),
                                       TT[h, q0:q0 + G, SEQ:ROWS].rearrange("p g (b t) -> p b g t", t=NT)).then_inc(s["diag"], 1)

            ve.wait_ge(s["ca"], 16)
            ve.wait_ge(s["gs"], 16 * 3 * HEADS)

            def p_mask(u):
                i, c, k = units[u]
                n = shape(u)[0]
                ve.wait_ge(s["p_scores"], u + 1)
                if u >= 4:
                    ve.wait_ge(s["p_turned"], u - 3)
                base, w = {"A": (CA_PA, P), "cmp": (CA_PB, NC_P)}.get(k, (CA_PC, P))
                mask = ca[:, base + w * i:base + w * i + n].unsqueeze(1).broadcast_to([P, 2, n])
                v = pp[:, u % 4, :, 0:n]
                ve.scalar_tensor_tensor(v, t.psum[:, 2 * (u % 2):2 * (u % 2) + 2, 0:n], SCALE, mask, ALU.mult, ALU.add)\
                  .then_inc(s["p_masked"], 1)
                ve.wait_ge(s["p_masked"], u + 1)
                z = nm[:, 2 * u:2 * u + 2]
                if k != "cmp":
                    ve.tensor_reduce(z, v, AX.X, ALU.max, negate=True).then_inc(s["p_max"], 1)
                else:
                    j = (u // 4) + 1
                    ve.tensor_reduce(z, v, AX.X, ALU.max, negate=True).then_inc(s["p_cmax"], 1)
                    ve.wait_ge(s["p_cmax"], j)
                    ve.tensor_scalar(z, z, -NEG * 0.1, None, ALU.min).then_inc(s["p_max"], 1)

            def p_weigh(u):
                i, c, k = units[u]
                n = shape(u)[0]
                ve.wait_ge(s["p_exp"], u + 1)
                zs, z = sm[:, 2 * u:2 * u + 2], rs[:, 2 * u:2 * u + 2]
                if k == "cmp":
                    ve.tensor_scalar(zs, zs, TINY, None, ALU.max).then_inc(s["p_csum"], 1)
                    ve.wait_ge(s["p_csum"], u // 4 + 1)
                ve.reciprocal(z, zs).then_inc(s["p_rec"], 1)
                if k != "A":
                    br = KINDS.index(k) - 1
                    gate = t.gates[:, i, br * HEADS:(br + 1) * HEADS].rearrange("p (k g) -> p k g", k=KVH)[:, :, c]
                    ve.wait_ge(s["p_rec"], u + 1)
                    ve.tensor_tensor(z, z, gate, ALU.mult).then_inc(s["p_fac"], 1)
                    ve.wait_ge(s["p_fac"], u - u // 4)
                else:
                    ve.wait_ge(s["p_rec"], u + 1)
                for e in range(2):
                    v = pp[:, u % 4, e, 0:n]
                    ins = ve.tensor_scalar(v, v, rs[:, 2 * u + e:2 * u + e + 1], None, ALU.mult)
                ins.then_inc(s["p_weighed"], 1)

            for u in range(NU + 1):
                if u < NU:
                    p_mask(u)
                if u == 8:
                    sample_queries()
                if u >= 1:
                    p_weigh(u - 1)
            ve.wait_ge(s["p_pv"], NU)
            over = lambda z: z.unsqueeze(2).broadcast_to([64, NB, NC_S])
            ve.wait_ge(s["i_mm"], 1)
            ve.tensor_scalar(pc[:].rearrange("p b n -> p (b n)"), bank(0)[0:64, 0:NB * NC_S], SCALE, None, ALU.mult).then_inc(s["i_dve"], 1)
            ve.wait_ge(s["i_dve"], 1)
            ve.tensor_reduce(cst[:, 0], pc[:], AX.X, ALU.max, negate=True).then_inc(s["i_pc"], 1)
            ve.wait_ge(s["i_pc"], 1)
            ve.tensor_tensor(pc[:], pc[:], over(cst[:, 0]), ALU.add).then_inc(s["i_pc"], 1)
            ve.wait_ge(s["i_pc"], 3)
            ve.tensor_reduce(cst[:, 1], pc[:], AX.X, ALU.add).then_inc(s["i_dve"], 1)
            ve.wait_ge(s["i_dve"], 2)
            ve.reciprocal(cst[:, 1], cst[:, 1]).then_inc(s["i_dve"], 1)
            ve.wait_ge(s["i_dve"], 3)
            ve.tensor_tensor(pc[:], pc[:], over(cst[:, 1]), ALU.mult).then_inc(s["i_pc"], 1)
            ve.wait_ge(s["i_mm"], 3)
            ve.tensor_copy(x1[:], bank(2)[0:64, 0:NB * NSEL]).then_inc(s["i_pc"], 1)
            ve.wait_ge(s["i_mm"], 4)
            ve.tensor_scalar(imp[:], bank(7)[0:64, 0:NB * NSEL].rearrange("p (b j) -> p b j", j=NSEL)[:, :, 14:0:-1], -1.0, None, ALU.mult).then_inc(s["i_sel"], 1)
            ve.wait_ge(s["i_sel"], 1)
            for b in range(NB):
                ve.max(top[:, b], imp[:, b]).then_inc(s["i_sel"], 1)
            ve.wait_ge(s["i_sel"], 1 + NB)
            for b in range(NB):
                ve.max_index(tix[:, b], top[:, b], imp[:, b]).then_inc(s["i_sel"], 1)
            ve.wait_ge(s["i_sel"], 1 + 2 * NB)
            ve.tensor_copy(tif[:], tix[:, :, 0]).then_inc(s["i_sel"], 1)
            ve.wait_ge(s["i_sel"], 2 + 2 * NB)
            ve.tensor_tensor(pen[:, :, 1:15], ca[0:64, CA_RV:CA_RV + 14].unsqueeze(1).broadcast_to([64, NB, 14]),
                             tif[:].unsqueeze(2).broadcast_to([64, NB, 14]), ALU.is_equal).then_inc(s["i_sel"], 1)
            ve.wait_ge(s["i_sel"], 3 + 2 * NB)
            ve.tensor_scalar(pen[:, :, 1:15], pen[:, :, 1:15], NEG, None, ALU.mult).then_inc(s["i_pen"], 1)
            ve.wait_ge(s["i_pen"], 1)

            read = lambda ins: ins.then_inc(s["s_read"], 1)

            def masked(b, n, dst, bk0, w, mask):
                r = dst.shape[0]
                return ve.scalar_tensor_tensor(dst, bank(chunk(b, n) % 3)[0:r, bk0:bk0 + w], SCALE, mask, ALU.mult, ALU.add)

            def negmax(b, n):
                ve.wait_ge(s["s_read"], chunk(b, [2, 3, 5][n]) + 1)
                v, z = [(sA[:, b % 2, :], stA[:, b, 0:1]), (sB[:, b % 2, SW:SW + NKW], stB[:, b, 1, 0:1]),
                        (sB[:, b % 2, SS:SS + NKA], stB[:, b, 0, 0:1])][n]
                ve.tensor_reduce(z, v, AX.X, ALU.max, negate=True).then_inc(s["s_max"], 1)

            def normed(b):
                q = b % 2
                ve.wait_ge(s["s_exp"], 3 * b + 3)
                ve.reciprocal(stA[:, b, 2:3], stA[:, b, 1:2])
                ve.reciprocal(stB[:, b, :, 2], stB[:, b, :, 1]).then_inc(s["s_rec"], 1)
                ve.wait_ge(s["s_rec"], b + 1)
                ve.tensor_tensor(stB[:, b, :, 3], stB[:, b, :, 2], gs[:, b, 1:3], ALU.mult).then_inc(s["s_fac"], 1)
                ve.wait_ge(s["s_fac"], b + 1)
                ve.wait_ge(s["s_pv"], b + 1)
                if b >= 2:
                    ve.wait_ge(s["s_out_turned"], b - 1)
                o, z = bank(5 + q), oB[:, q, :]
                ve.tensor_scalar(z, o[0:64, P:2 * P], gs[:, b, 0:1], None, ALU.mult).then_inc(s["s_branch"], 1)
                ve.tensor_scalar(oA[:, q, :], o[:, 0:P], stA[:, b, 2:3], None, ALU.mult)
                ve.wait_ge(s["s_branch"], 2 * b + 1)
                ve.scalar_tensor_tensor(z, o[0:64, 2 * P:3 * P], stB[:, b, 0, 3:4], z, ALU.mult, ALU.add).then_inc(s["s_branch"], 1)
                ve.wait_ge(s["s_branch"], 2 * b + 2)
                ve.scalar_tensor_tensor(z, o[0:64, 3 * P:4 * P], stB[:, b, 1, 3:4], z, ALU.mult, ALU.add).then_inc(s["s_normed"], 1)

            for b in range(NB):
                a, z = sA[:, b % 2, :], sB[:, b % 2, :]
                ve.wait_ge(s["s_scores"], chunk(b, 0) + 1)
                if b >= 2:
                    ve.wait_ge(s["s_turned"], 4 * (b - 1))
                masked(b, 0, a[:, PAST:NKA], 0, NT, ca[:, CA_SA + PAST:CA_SA + NKA])
                masked(b, 0, z[:, SS + PAST:SS + NKA], 8, NT, ca[0:64, CA_SN:CA_SN + NT])
                read(masked(b, 0, z[:, SW + 512:SW + NKW], 16, NT, ca[0:64, CA_SW + 512:CA_SW + NKW]))
                for x in range(2):
                    ve.wait_ge(s["s_scores"], chunk(b, 1 + x) + 1)
                    c = slice(512 * x, 512 * (x + 1))
                    read(masked(b, 1 + x, a[:, c], 0, 512, ca[:, CA_SA + 512 * x:CA_SA + 512 * (x + 1)]))
                negmax(b, 0)
                ve.wait_ge(s["s_scores"], chunk(b, 3) + 1)
                read(masked(b, 3, z[:, SW:SW + 512], 0, 512, ca[0:64, CA_SW:CA_SW + 512]))
                negmax(b, 1)
                if b >= 2:
                    normed(b - 2)
                for x in range(2):
                    ve.wait_ge(s["s_scores"], chunk(b, 4 + x) + 1)
                    m = pen[:, b, 8 * x:8 * x + 8].unsqueeze(2).broadcast_to([64, 8, 64])
                    read(ve.scalar_tensor_tensor(z[:, SS + 512 * x:SS + 512 * (x + 1)].rearrange("p (j n) -> p j n", n=64),
                                                 bank(chunk(b, 4 + x) % 3)[0:64].rearrange("p (j n) -> p j n", n=64), SCALE, m, ALU.mult, ALU.add))
                negmax(b, 2)
            normed(NB - 2)
            normed(NB - 1)


NH = 8
HH = 2 * NH
TOPK = 16
PAIRS = [TOPK // (a + 1) for a in range(8)]
POFF = [sum(PAIRS[:a]) for a in range(9)]
NPAIR = POFF[8] + 8
HU = 2 * NH + NH // 2
LOW = -3e38


def norm_rows(ve, s, key, i, r, x, psum, y, lnp, bn, mv):
    for h in range(2):
        c = slice(512 * h, 512 * (h + 1))
        ve.scalar_tensor_tensor(y[:, c], x[:, c], ALPHA, psum[h], ALU.mult, ALU.add).then_inc(s[key + "_sum"], 1)
    ve.wait_ge(s[key + "_sum"], 2 * i + 2)
    for h in range(2):
        ve.bn_stats(bn[0:r, 6 * h:6 * h + 6], y[:, 512 * h:512 * (h + 1)]).then_inc(s[key + "_st"], 1)
    ve.wait_ge(s[key + "_st"], 5 * i + 2)
    ve.bn_aggr(mv[0:r, 0:2], bn[0:r, :]).then_inc(s[key + "_st"], 1)
    ve.wait_ge(s[key + "_st"], 5 * i + 3)
    ve.tensor_scalar(mv[0:r, 2:3], mv[0:r, 1:2], EPS, None, ALU.add).then_inc(s[key + "_var"], 1)
    ve.wait_ge(s[key + "_root"], i + 1)
    ve.reciprocal(mv[0:r, 2:3], mv[0:r, 2:3]).then_inc(s[key + "_st"], 1)
    ve.wait_ge(s[key + "_st"], 5 * i + 4)
    ve.tensor_scalar(y, y, mv[0:r, 0:1], mv[0:r, 2:3], ALU.subtract, ALU.mult).then_inc(s[key + "_st"], 1)
    ve.wait_ge(s[key + "_st"], 5 * i + 5)
    ve.tensor_tensor(y, y, lnp[0:r, 0, :], ALU.mult).then_inc(s[key + "_g"], 1)
    ve.wait_ge(s[key + "_g"], i + 1)
    ve.tensor_tensor(y, y, lnp[0:r, 1, :], ALU.add).then_inc(s[key + "_ln"], 1)


def route_block(nc, d, t, s):
    with ExitStack() as ctx:
        sb = lambda n, sh, dt=F32: ctx.enter_context(nc.sbuf_tensor(n, sh, dt))
        wo = t.big[:].rearrange("p (k n) -> p k n", k=KD)
        xr = sb("x_rows", [P, TILES, D])
        ln = sb("ln1", [P, 2, D])
        wq = sb("wq_ring", [P, 4, KD, P])
        ky = sb("peer_keys", [P, HH, P])
        qT = sb("peer_q", [P, HH, ROWS])
        xT = sb("x1T", [P, KD, ROWS])
        sc = sb("peer_scores", [P, 3, 4, P])
        sc2 = sb("peer_scores2", [P, 4, P])
        v = sb("top_vals", [P, 2, 4, TOPK])
        ix = sb("top_idx", [P, 2, 4, TOPK], U32)
        ixf = sb("top_idxf", [P, 2, 4, TOPK])
        i128 = sb("top_idx128", [P, 2, 2, TOPK])
        cv = sb("pair_vals", [P, 2, NPAIR])
        cv2 = sb("pair_vals2", [P, 2, NPAIR])
        ci = sb("pair_ids", [P, 2, 2, NPAIR])
        bi = sb("best_idx", [P, 2, TOPK], U32)
        bf = sb("best_idxf", [P, 2, TOPK])
        eq = sb("best_onehot", [P, 2, 2, TOPK, NPAIR])
        bv = sb("best_vals", [P, HU, TOPK])
        ids = sb("expert_ids", [P, HU, TOPK])
        den = sb("gate_sum", [P, 2, HU])
        cT = sb("ids_turned", [P, ROWS])
        gT = sb("gates_turned", [P, ROWS])
        ii = sb("ids_int", [P, 2, ROWS], I32)
        gr = sb("gate_rest", [P, 2, ROWS])
        bn = sb("ln1_bn", [P, 12])
        mv = sb("ln1_mv", [P, 3])
        io = sb("iota_pairs", [P, NPAIR])
        block = ctx.enter_context(nc.Block())
        OT, x1, ident = t.OT, t.x1, t.c0[:, 0:P]
        bank = lambda i: t.psum[:, i]
        by_group = [[(0, 0), (1, 0)], [(0, 1), (1, 1)], [(0, 2), (1, 2), (2, 0)], [(0, 3), (1, 3), (2, 1)]]
        units = [x for g in by_group for x in g]
        head = lambda u: 8 * units[u][0] + 2 * units[u][1]

        @block.sync
        def _(sp):
            for i in range(TILES):
                sp.dma_start(xr[0:RT[i], i, :], d.x_rows[P * i:P * i + RT[i], :]).then_inc(s["ld_xr"], 16)
            sp.dma_start(ln[:, 0, :], d.ln1_g.partition_broadcast(P)).then_inc(s["ld_xr"], 16)
            sp.dma_start(ln[:, 1, :], d.ln1_b.partition_broadcast(P)).then_inc(s["ld_xr"], 16)
            sp.dma_start(io[:], d.iota_pairs).then_inc(s["ld_ky"], 16)
            sp.dma_start(ky[:], d.peer_keys).then_inc(s["ld_ky"], 16)
            for j in range(HH):
                if j >= 4:
                    sp.wait_ge(s["q_mm"], j - 3)
                sp.dma_start(wq[:, j % 4], d.peer_wq[j]).then_inc(s[f"ld_wq{j % 4}"], 16)
            for m in range(2):
                sp.dma_start(t.big[:, m * D:(m + 1) * D], d.peer_u[m]).then_inc(s[f"ld_u{m}"], 16)
                sp.dma_start(t.big[:, (2 + m) * D:(3 + m) * D], d.peer_v[m]).then_inc(s[f"ld_v2{m}"], 16)
            sp.dma_start(t.big[:, 4 * D:5 * D], d.ln2_g.partition_broadcast(P)).then_inc(s["ld_ln2"], 16)
            sp.dma_start(t.big[:, 5 * D:6 * D], d.ln2_b.partition_broadcast(P)).then_inc(s["ld_ln2"], 16)

        @block.tensor
        def _(pe):
            for i in range(TILES):
                r = slice(P * i, P * i + RT[i])
                for h in range(2):
                    for k in range(KD):
                        if i == 0 and h == 0 and k % 4 == 0:
                            pe.wait_ge(s[f"ld_wo{k // 4}"], 32)
                        mm = pe.matmul(bank(2 * i + h)[0:RT[i], :], OT[:, k, r], wo[:, k, 512 * h:512 * (h + 1)],
                                       start=(k == 0), stop=(k == KD - 1))
                mm.then_inc(s["o_mm"], 1)
            for x in range(2 * TILES):
                i = x // 2
                pe.wait_ge(s["l1_ln"], i + 1)
                if x >= 2:
                    pe.wait_ge(s["x_out"], x - 1)
                for y in range(4):
                    k = 4 * (x % 2) + y
                    mm = pe.transpose(bank(6 + x % 2)[:, y * P:y * P + RT[i]], x1[0:RT[i], i, k * P:(k + 1) * P], ident[0:RT[i], 0:RT[i]])
                mm.then_inc(s["x_turn"], 1)
            pe.wait_ge(s["x_out"], 6)
            pe.wait_ge(s["ld_ky"], 32)
            for g in range(4):
                for j in range(4 * g, 4 * g + 4):
                    pe.wait_ge(s[f"ld_wq{j % 4}"], 16 * (j // 4 + 1))
                    if j >= 2:
                        pe.wait_ge(s["q_out"], j - 1)
                    for k in range(KD):
                        mm = pe.matmul(bank(j % 2)[:, 0:ROWS], wq[:, j % 4, k, :], xT[:, k, :], start=(k == 0), stop=(k == KD - 1))
                    mm.then_inc(s["q_mm"], 1)
                pe.wait_ge(s["q_out"], 4 * g + 4)
                for i, l in by_group[g]:
                    u = units.index((i, l))
                    if u >= 2:
                        pe.wait_ge(s["sc_out"], u - 1)
                    for j in range(4):
                        for r0, q in ([(0, 4 * l + j)] if i < 2 else [(0, 4 * l + j), (64, 4 * l + 8 + j)]):
                            mm = pe.matmul(bank(2 + u % 2)[r0:r0 + RT[i], j * P:(j + 1) * P], qT[:, q, P * i:P * i + RT[i]], ky[:, q, :],
                                           start=True, stop=True)
                    mm.then_inc(s["sc_mm"], 1)
            pe.wait_ge(s["id_sum"], len(units))
            pe.wait_ge(s["g_fin"], 1)
            for i in range(TILES):
                h = slice(8 * i, min(8 * i + 8, HU))
                n = 16 * (h.stop - h.start)
                pe.transpose(bank(4 + i)[0:n, 0:P], ids[:, h].rearrange("p h k -> p (h k)"), ident)
                pe.transpose(bank(4 + i)[0:n, P:2 * P], bv[:, h].rearrange("p h k -> p (h k)"), ident).then_inc(s["id_turn"], 1)

        @block.scalar
        def _(act):
            for i in range(TILES):
                act.wait_ge(s["l1_var"], i + 1)
                act.activation(mv[0:RT[i], 2:3], mv[0:RT[i], 2:3], ACT.Sqrt).then_inc(s["l1_root"], 1)
            for x in range(2 * TILES):
                i, c = x // 2, 4 * (x % 2)
                act.wait_ge(s["x_turn"], x + 1)
                act.activation(xT[:, c:c + 4, P * i:P * i + RT[i]], bank(6 + x % 2).rearrange("p (c q) -> p c q", q=P)[:, :, 0:RT[i]],
                               ACT.Copy).then_inc(s["x_out"], 1)
            act.wait_ge(s["x_out"], 6)
            for g in range(4):
                for j in range(4 * g, 4 * g + 4):
                    act.wait_ge(s["q_mm"], j + 1)
                    act.activation(qT[:, j, :], bank(j % 2)[:, 0:ROWS], ACT.Copy).then_inc(s["q_out"], 1)
                for x in by_group[g]:
                    u = units.index(x)
                    act.wait_ge(s["sc_mm"], u + 1)
                    if u >= 3:
                        act.wait_ge(s["top2"], 4 * (u - 2))
                    act.activation(sc[:, u % 3], bank(2 + u % 2).rearrange("p (j n) -> p j n", n=P), ACT.Copy).then_inc(s["sc_out"], 1)
                if g == 0:
                    act.activation(t.x1h[:], xT[:], ACT.Copy).then_inc(s["x_hi"], 1)
            act.wait_ge(s["g_sub"], 1)
            act.activation(bv[:], bv[:], ACT.Exp).then_inc(s["g_exp"], 1)

        @block.gpsimd
        def _(gp):
            for u in range(len(units)):
                q = u % 2
                z = ixf[:, q].rearrange("p (h e) k -> p h e k", e=2)
                gp.wait_ge(s["ixf"], u + 1)
                if u >= 2:
                    gp.wait_ge(s["id_mul"], u - 1)
                gp.tensor_scalar(i128[:, q], z[:, :, 0, :], float(P), None, ALU.mult).then_inc(s["pr128"], 1)
                gp.wait_ge(s["pr128"], u + 1)
                for a in range(8):
                    n, o = PAIRS[a], POFF[a]
                    gp.tensor_tensor(ci[:, q, :, o:o + n], z[:, :, 1, 0:n], i128[:, q, :, a].unsqueeze(2).broadcast_to([P, 2, n]), ALU.add)
                gp.tensor_tensor(ci[:, q, :, POFF[8]:NPAIR], i128[:, q, :, 8:16], z[:, :, 1, 0].unsqueeze(2).broadcast_to([P, 2, 8]), ALU.add)\
                  .then_inc(s["pair"], 1)
                gp.wait_ge(s["pair"], u + 1)
                gp.wait_ge(s["id_eq"], u + 1)
                gp.tensor_tensor(eq[:, q], eq[:, q], ci[:, q].unsqueeze(2).broadcast_to([P, 2, TOPK, NPAIR]), ALU.mult).then_inc(s["id_mul"], 1)
                if u == 0:
                    gp.wait_ge(s["x_hi"], 1)
                    gp.tensor_tensor(t.x1l[:], xT[:], t.x1h[:].bitcast(F32), ALU.subtract).then_inc(s["x_lo"], 1)

        @block.vector
        def _(ve):
            ve.wait_ge(s["ld_xr"], 80)
            for i in range(TILES):
                r = RT[i]
                ve.wait_ge(s["o_mm"], i + 1)
                norm_rows(ve, s, "l1", i, r, xr[0:r, i, :], [bank(2 * i + h)[0:r, :] for h in range(2)], x1[0:r, i, :], ln, bn, mv)
            def top16(n, base, src, src2, vals, idxs, names):
                a, b, c = names
                for j in range(n):
                    ve.max(vals(j)[:, 0:8], src(j)).then_inc(s[a], 1)
                ve.wait_ge(s[a], base + n)
                for j in range(n):
                    ve.max_index(idxs(j)[:, 0:8], vals(j)[:, 0:8], src(j))
                    ve.match_replace(src2(j), vals(j)[:, 0:8], src(j), LOW).then_inc(s[b], 1)
                ve.wait_ge(s[b], base + n)
                for j in range(n):
                    ve.max(vals(j)[:, 8:16], src2(j)).then_inc(s[a + "b"], 1)
                ve.wait_ge(s[a + "b"], base + n)
                for j in range(n):
                    ve.max_index(idxs(j)[:, 8:16], vals(j)[:, 8:16], src2(j)).then_inc(s[c], 1)

            def ids_of(u):
                ve.wait_ge(s["id_mul"], u + 1)
                ve.tensor_reduce(ids[:, head(u):head(u) + 2], eq[:, u % 2], AX.X, ALU.add).then_inc(s["id_sum"], 1)

            for u in range(len(units)):
                q = u % 2
                ve.wait_ge(s["sc_out"], u + 1)
                if u >= 2:
                    ve.wait_ge(s["pair"], u - 1)
                top16(4, 4 * u, lambda j: sc[:, u % 3, j], lambda j: sc2[:, j], lambda j: v[:, q, j], lambda j: ix[:, q, j],
                      ("top", "topr", "top2"))
                ve.wait_ge(s["top2"], 4 * (u + 1))
                ve.tensor_copy(ixf[:, q], ix[:, q]).then_inc(s["ixf"], 1)
                z = v[:, q].rearrange("p (h e) k -> p h e k", e=2)
                if u:
                    ve.wait_ge(s["bei"], 2 * u)
                for a in range(8):
                    n, o = PAIRS[a], POFF[a]
                    ve.tensor_tensor(cv[:, :, o:o + n], z[:, :, 1, 0:n], z[:, :, 0, a].unsqueeze(2).broadcast_to([P, 2, n]), ALU.add)
                ve.tensor_tensor(cv[:, :, POFF[8]:NPAIR], z[:, :, 0, 8:16], z[:, :, 1, 0].unsqueeze(2).broadcast_to([P, 2, 8]), ALU.add)\
                  .then_inc(s["pair_v"], 1)
                ve.wait_ge(s["pair_v"], u + 1)
                top16(2, 2 * u, lambda j: cv[:, j], lambda j: cv2[:, j], lambda j: bv[:, head(u) + j], lambda j: bi[:, j], ("be", "ber", "bei"))
                if u:
                    ids_of(u - 1)
                ve.wait_ge(s["bei"], 2 * (u + 1))
                if u:
                    ve.wait_ge(s["id_eq"], u)
                ve.tensor_copy(bf[:], bi[:]).then_inc(s["bf"], 1)
                ve.wait_ge(s["bf"], u + 1)
                if u >= 2:
                    ve.wait_ge(s["id_sum"], u - 1)
                ve.tensor_tensor(eq[:, q], io[:].unsqueeze(1).unsqueeze(1).broadcast_to([P, 2, TOPK, NPAIR]),
                                 bf[:].unsqueeze(3).broadcast_to([P, 2, TOPK, NPAIR]), ALU.is_equal).then_inc(s["id_eq"], 1)
            over = lambda z: z.unsqueeze(2).broadcast_to([P, HU, TOPK])
            ve.tensor_copy(den[:, 1], bv[:, :, 0]).then_inc(s["g_max"], 1)
            ve.wait_ge(s["g_max"], 1)
            ve.tensor_tensor(bv[:], bv[:], over(den[:, 1]), ALU.subtract).then_inc(s["g_sub"], 1)
            ve.wait_ge(s["g_exp"], 1)
            ve.tensor_reduce(den[:, 0], bv[:], AX.X, ALU.add).then_inc(s["g_den"], 1)
            ve.wait_ge(s["g_den"], 1)
            ve.reciprocal(den[:, 0], den[:, 0]).then_inc(s["g_den"], 1)
            ve.wait_ge(s["g_den"], 2)
            ve.tensor_tensor(bv[:], bv[:], over(den[:, 0]), ALU.mult).then_inc(s["g_fin"], 1)
            ids_of(len(units) - 1)
            for i in range(TILES):
                r = slice(P * i, P * i + RT[i])
                ve.wait_ge(s["id_turn"], i + 1)
                for x, dst in enumerate((cT, gT)):
                    o = bank(4 + i)[:, x * P:(x + 1) * P]
                    if i < 2:
                        ins = ve.tensor_copy(dst[:, r], o)
                    else:
                        ve.tensor_copy(dst[0:64, r], o[0:64, 0:64])
                        ins = ve.tensor_copy(dst[64:P, r], o[0:64, 64:P])
                ins.then_inc(s["id_out"], 1)
            step = [0]

            def after(ins):
                step[0] += 1
                ins.then_inc(s["split"], 1)
                ve.wait_ge(s["split"], step[0])

            ve.wait_ge(s["id_out"], 3)
            after(ve.tensor_copy(ii[:, 0, :], cT[:]))
            after(ve.tensor_scalar(ii[:, 1, :], ii[:, 0, :], 7, None, ALU.logical_shift_right))
            after(ve.tensor_copy(t.i1[:], ii[:, 1, :]))
            after(ve.tensor_scalar(ii[:, 1, :], ii[:, 0, :], P - 1, None, ALU.bitwise_and))
            for g in range(SEGS):
                ve.tensor_scalar(t.i2[:, g, :], ii[:, 1, :], float(-g * SEGW), None, ALU.add)
            after(ve.tensor_copy(t.gp[:, 0, :], gT[:]))
            after(ve.tensor_tensor(gr[:, 0, :], gT[:], t.gp[:, 0, :], ALU.subtract))
            after(ve.tensor_copy(t.gp[:, 1, :], gr[:, 0, :]))
            after(ve.tensor_tensor(gr[:, 1, :], gr[:, 0, :], t.gp[:, 1, :], ALU.subtract))
            after(ve.tensor_copy(t.gp[:, 2, :], gr[:, 1, :]))


SEGS, SEGW = 4, 32
NE = 128
GT = ROWS // SEGW
HWC = TILES * P
assert ROWS + RT[2] == HWC
UN = 4


def expert_block(nc, d, t, s):
    with ExitStack() as ctx:
        sb = lambda n, sh, dt=F32: ctx.enter_context(nc.sbuf_tensor(n, sh, dt))
        W = sb("gate_matrix", [P, 2, SEGW, ROWS])
        us = t.big[:, 0:2 * D].rearrange("p (s n) -> p s n", s=2)
        vs = t.big[:, 2 * D:4 * D].rearrange("p (s n) -> p s n", s=2)
        ln = t.big[:, 4 * D:6 * D].rearrange("p (s n) -> p s n", s=2)
        uh, ul = sb("u_hi", [P, 2, D], F32R), sb("u_lo", [P, 2, D], F32R)
        vh, vl = sb("v_hi", [P, 2, D], F32R), sb("v_lo", [P, 2, D], F32R)
        hg = t.big[:, 6 * D:6 * D + ROWS]
        hw = t.big[:, 6 * D + ROWS:6 * D + 2 * ROWS]
        hwh, hwl = sb("gated_hi", [P, 2, HWC], F32R), sb("gated_lo", [P, 2, SEQ], F32R)
        A = sb("onehot_i1", [P, 2, P, GT], BF16)
        E = sb("onehot_i2", [P, 2, SEGW, GT], BF16)
        B = sb("gated_i2", [P, 2, 3, SEGW, GT], BF16)
        o = 6 * D + 2 * ROWS
        iof = t.big[:, o:o + P]
        io = t.big[:, o + P:o + P + P * GT // 2].bitcast(BF16).rearrange("p (i r) -> p i r", r=GT)
        bn = sb("ln2_bn", [P, 12])
        mv = sb("ln2_mv", [P, 3])
        block = ctx.enter_context(nc.Block())
        bank = lambda i: t.psum[:, i]
        H, WP = bank(6), bank(7)
        x1h, x1l = t.x1h, t.x1l

        @block.sync
        def _(sp):
            with sp.Fori(0, NE // 2 - 1) as i:
                for m in range(2):
                    sp.wait_ge(s["u_lo"], i * 2 + (m + 1))
                    sp.dma_start(us[:, m], d.peer_u[bass.ds(i * 2 + (m + 2), 1)].rearrange("a p n -> p (a n)")).then_inc(s[f"ld_u{m}"], 16)
                    sp.wait_ge(s["v_lo"], i * 2 + (m + 1))
                    sp.dma_start(vs[:, m], d.peer_v[bass.ds(i * 2 + (m + 2), 1)].rearrange("a p n -> p (a n)")).then_inc(s[f"ld_v2{m}"], 16)
            for i in range(TILES):
                sp.wait_ge(s["l2_ln"], i + 1)
                sp.dma_start(d.o_y[P * i:P * i + RT[i], :], t.x1[0:RT[i], i, :]).then_inc(s["st_y"], 16)
            sp.wait_ge(s["st_y"], 48)

        def segments(eng, body, last):
            for g in range(SEGS):
                with eng.Fori(0, SEGW // UN - (g == SEGS - 1)) as i:
                    for k in range(UN):
                        body(g, i * UN + (SEGW * g + k), i * UN + k, k)
            for k in range(UN):
                last(NE - UN + k, SEGW - UN + k, k)

        @block.tensor
        def _(pe):
            pe.sem_inc(s["c_mm"], 2)
            pe.sem_inc(s["y_mm"], 1)

            def product1(n, q):
                pe.wait_ge(s["u_lo"], n + 1)
                pe.wait_ge(s["gelu"], n)
                for k in range(KD):
                    kc = slice(k * P, (k + 1) * P)
                    pe.matmul(H[:, 0:ROWS], uh[:, q, kc], x1h[:, k, :], start=(k == 0), stop=False)
                    pe.matmul(H[:, 0:ROWS], uh[:, q, kc], x1l[:, k, :], start=False, stop=False)
                    mm = pe.matmul(H[:, 0:ROWS], ul[:, q, kc], x1h[:, k, :], start=False, stop=(k == KD - 1))
                mm.then_inc(s["h_mm"], 1)

            def product2(n, q, stop):
                pe.wait_ge(s["hw_lo"], n + 2)
                pe.wait_ge(s["v_lo"], n + 1)
                for i in range(TILES):
                    r = slice(i * P, (i + 1) * P)
                    pairs = ((hwh, vh), (hwh, vl), (hwl, vh))[0:3 if i < 2 else 2]
                    for x, (a, b) in enumerate(pairs):
                        for h in range(2):
                            mm = pe.matmul(bank(2 * i + h), a[:, q, r], b[:, q, 512 * h:512 * (h + 1)], start=False,
                                           stop=stop and x == len(pairs) - 1, skip_group_check=True)
                mm.then_inc(s["y_mm"], 1)

            def gate_rows(c, q):
                pe.wait_ge(s["onehot"], c + 1)
                pe.wait_ge(s["W_out"], c + 1)
                for r in range(GT):
                    for x in range(3):
                        mm = pe.matmul(WP[:, r * SEGW:(r + 1) * SEGW], A[:, q, :, r], B[:, q, x, :, r], start=(x == 0), stop=(x == 2))
                mm.then_inc(s["c_mm"], 1)

            pe.wait_ge(s["zero"], 2)
            for i in range(2 * TILES):
                mm = pe.matmul(bank(i), hwh[:, 1, 0:P], vh[:, 1, 0:512], start=True, stop=False, skip_group_check=True)
            mm.then_inc(s["y_mm"], 1)
            with pe.Fori(0, SEGW // 2) as i:
                for q in range(2):
                    pe.wait_ge(s["onehot_12"], i * 2 + (q + 1))
                    gate_rows(i * 2 + q, q)
            product1(0, 0)

            def body(g, n, j, k):
                product1(n + 1, (k + 1) % 2)
                if g < SEGS - 1:
                    gate_rows(n + SEGW, k % 2)
                product2(n, k % 2, False)

            def last(n, j, k):
                if k < UN - 1:
                    product1(n + 1, (k + 1) % 2)
                product2(n, k % 2, k == UN - 1)

            segments(pe, body, last)

        @block.scalar
        def _(act):
            def u_hi(n, q, w):
                act.wait_ge(s[f"ld_u{q}"], w)
                act.activation(uh[:, q], us[:, q], ACT.Copy).then_inc(s["u_hi"], 1)

            def W_out(c, seg, g):
                act.wait_ge(s["c_mm"], c + 3)
                act.activation(W[:, seg % 2, :, bass.ds(g * GT, GT)].rearrange("p j r -> p r j"),
                               WP[:, 0:GT * SEGW].rearrange("p (r j) -> p r j", j=SEGW), ACT.Copy).then_inc(s["W_out"], 1)

            act.sem_inc(s["W_out"], 1)
            with act.Fori(0, SEGW // 2) as i:
                for q in range(2):
                    W_out(i * 2 + q, 0, i * 2 + q)
            u_hi(0, 0, 16)

            def loads(n, k):
                return (n - k % 2) * 8 + 16

            def hidden(n):
                act.wait_ge(s["h_mm"], n + 1)
                act.wait_ge(s["hw"], n + 1)
                act.activation(hg[:], H[:, 0:ROWS], ACT.Gelu_apprx_tanh).then_inc(s["gelu"], 1)

            def body(g, n, j, k, end=False):
                q = k % 2
                act.wait_ge(s["hw"], n + 2)
                act.wait_ge(s["y_mm"], n + 1)
                act.activation(hwh[:, q, 0:ROWS], hw[:], ACT.Copy).then_inc(s["hw_hi"], 1)
                if not end:
                    u_hi(n + 1, (k + 1) % 2, loads(n + 1, k + 1))
                act.wait_ge(s[f"ld_v2{q}"], loads(n, k))
                act.activation(vh[:, q], vs[:, q], ACT.Copy).then_inc(s["v_hi"], 1)
                if not end:
                    hidden(n + 1)
                if g < SEGS - 1:
                    W_out(n + SEGW, g + 1, j)

            hidden(0)
            segments(act, body, lambda n, j, k: body(SEGS - 1, n, j, k, end=(k == UN - 1)))
            for i in range(TILES):
                act.wait_ge(s["l2_var"], i + 1)
                act.activation(mv[0:RT[i], 2:3], mv[0:RT[i], 2:3], ACT.Sqrt).then_inc(s["l2_root"], 1)

        @block.vector
        def _(ve):
            for z in (hwh, vh):
                ve.memset(z[:].bitcast(F32), 0.0).then_inc(s["zero"], 1)
            ve.wait_ge(s["iota_in"], 16)
            ve.tensor_copy(io[:], iof[:].unsqueeze(2).broadcast_to([P, P, GT])).then_inc(s["iota"], 1)
            ve.wait_ge(s["iota"], 1)
            ve.sem_inc(s["hw"], 1)
            ve.sem_inc(s["hw_lo"], 1)

            def onehots(c, seg, g, q, parts=3):
                r = bass.ds(g * GT, GT)
                ve.wait_ge(s["c_mm"], c + 1)
                ve.tensor_tensor(E[:, q], io[:, 0:SEGW, :], t.i2[:, seg, r].unsqueeze(1).broadcast_to([P, SEGW, GT]), ALU.is_equal).then_inc(s["oh_e"], 1)
                ve.tensor_tensor(A[:, q], io[:], t.i1[:, r].unsqueeze(1).broadcast_to([P, P, GT]), ALU.is_equal)
                ve.wait_ge(s["oh_e"], c + 1)
                ve.tensor_tensor(B[:, q, 0:parts], E[:, q].unsqueeze(1).broadcast_to([P, parts, SEGW, GT]),
                                 t.gp[:, 0:parts, r].unsqueeze(2).broadcast_to([P, parts, SEGW, GT]), ALU.mult).then_inc(s["onehot"], 1)

            def u_lo(n, q):
                ve.wait_ge(s["u_hi"], n + 1)
                ve.tensor_tensor(ul[:, q], us[:, q], uh[:, q].bitcast(F32), ALU.subtract).then_inc(s["u_lo"], 1)

            with ve.Fori(0, SEGW // 2) as i:
                for q in range(2):
                    onehots(i * 2 + q, 0, i * 2 + q, q, 1)
            u_lo(0, 0)

            def body(g, n, j, k):
                q = k % 2
                if k == 0:
                    ve.wait_ge(s["W_out"], SEGW * (g + 1) + 1)
                ve.wait_ge(s["gelu"], n + 1)
                ve.wait_ge(s["hw_lo"], n + 1)
                ve.tensor_tensor(hw[:], hg[:], W[:, g % 2, bass.ds(j, 1), :].rearrange("p a r -> p (a r)"), ALU.mult).then_inc(s["hw"], 1)
                ve.wait_ge(s["hw_hi"], n + 1)
                ve.tensor_tensor(hwh[:, q, ROWS:HWC], hw[:, SEQ:ROWS], hwh[:, q, SEQ:ROWS].bitcast(F32), ALU.subtract)
                ve.tensor_tensor(hwl[:, q, :], hw[:, 0:SEQ], hwh[:, q, 0:SEQ].bitcast(F32), ALU.subtract).then_inc(s["hw_lo"], 1)
                if type(n) is not int or k < UN - 1:
                    u_lo(n + 1, (k + 1) % 2)
                ve.wait_ge(s["v_hi"], n + 1)
                ve.tensor_tensor(vl[:, q], vs[:, q], vh[:, q].bitcast(F32), ALU.subtract).then_inc(s["v_lo"], 1)
                if g < SEGS - 1:
                    onehots(n + SEGW, g + 1, j, q)

            segments(ve, body, lambda n, j, k: body(SEGS - 1, n, j, k))
            ve.wait_ge(s["y_mm"], NE + 2)
            ve.wait_ge(s["ld_ln2"], 32)
            for h in range(2):
                ve.tensor_copy(us[0:64, 0, 512 * h:512 * (h + 1)], bank(4 + h)[64:P, :]).then_inc(s["y_low"], 1)
            ve.wait_ge(s["y_low"], 2)
            ve.scalar_tensor_tensor(t.x1[0:64, 2, :], us[0:64, 0], 1.0 / ALPHA, t.x1[0:64, 2, :], ALU.mult, ALU.add).then_inc(s["y_low"], 1)
            ve.wait_ge(s["y_low"], 3)
            for i in range(TILES):
                r = RT[i]
                norm_rows(ve, s, "l2", i, r, t.x1[0:r, i, :], [bank(2 * i + h)[0:r, :] for h in range(2)], t.x1[0:r, i, :], ln, bn, mv)

        @block.gpsimd
        def _(gp):
            gp.dma_start(iof[:], d.iota).then_inc(s["iota_in"], 16)
            with gp.Fori(0, SEGW // 2) as i:
                for q in range(2):
                    r = bass.ds((i * 2 + q) * GT, GT)
                    gp.wait_ge(s["oh_e"], i * 2 + (q + 1))
                    gp.tensor_tensor(B[:, q, 1:3], E[:, q].unsqueeze(1).broadcast_to([P, 2, SEGW, GT]),
                                     t.gp[:, 1:3, r].unsqueeze(2).broadcast_to([P, 2, SEGW, GT]), ALU.mult).then_inc(s["onehot_12"], 1)
            with gp.Fori(0, NB) as b:
                one = lambda x: x[bass.ds(b, 1)].rearrange("a p n -> (a p) n")
                for x in range(4):
                    gp.wait_ge(s["v_lo"], b * 14 + (3 * x + 1))
                    r = slice(32 * x, 32 * (x + 1))
                    src = d.a_k[bass.ds(b, 1), r, :, NT:PAST].rearrange("a p c n -> (a p) c n")
                    gp.dma_start(d.keep_ak[bass.ds(b, 1), r].rearrange("a p c n -> (a p) c n"), src).then_inc(s["kept"], 16)
                    gp.wait_ge(s["v_lo"], b * 14 + (3 * x + 2))
                    r = slice(32 * x, min(32 * (x + 1), P - 1))
                    gp.dma_start(one(d.keep_av)[r], one(d.a_v)[32 * x + 1:r.stop + 1]).then_inc(s["kept"], 16)
                gp.wait_ge(s["v_lo"], b * 14 + 13)
                gp.dma_start(one(d.keep_wk), one(d.w_k)[:, NT:512]).then_inc(s["kept"], 16)
                gp.wait_ge(s["v_lo"], b * 14 + 14)
                gp.dma_start(one(d.keep_wv), one(d.w_v)[2:P]).then_inc(s["kept"], 16)
            gp.wait_ge(s["kept"], 16 * 10 * NB)


def constants():
    c0 = np.zeros((P, C0_W), np.float32)
    c0[:, 0:P] = np.eye(P, dtype=np.float32)
    inv = np.power(np.float32(500000.0), -np.arange(HALF, dtype=np.float32) / np.float32(HALF)).astype(np.float32)
    for i in range(TILES):
        pos = (np.arange(P) + P * i) if i < 2 else PAST + np.arange(P) % NT
        ang = pos.astype(np.float32)[:, None] * inv[None, :]
        c0[:, P + HALF * i:P + HALF * (i + 1)] = np.cos(ang)
        c0[:, P + HALF * (TILES + i):P + HALF * (TILES + i + 1)] = np.sin(ang)
    ca = np.zeros((P, CA_W), np.float32)
    many = lambda dist: sum(((dist >= 0) & (dist <= w) & (dist % dil == 0)) for w, dil in ((128, 1), (512, 4), (2048, 16)))
    log = lambda n: np.where(n > 0, np.log(np.maximum(n, 1)), NEG).astype(np.float32)
    mask = lambda ok: np.where(ok, 0.0, NEG).astype(np.float32)
    for i in range(2):
        n = P * (i + 1)
        dist = (np.arange(P) + P * i)[:, None] - np.arange(n)[None, :]
        ca[:, CA_PA + P * i:CA_PA + P * i + n] = log(many(dist))
        ca[:, CA_PC + P * i:CA_PC + P * i + n] = mask(dist >= 0)
        ca[:, CA_PB + NC_P * i:CA_PB + NC_P * (i + 1)] = mask(16 * np.arange(NC_P)[None, :] + 31 <= (np.arange(P) + P * i)[:, None])
    tt = (np.arange(P) % NT)[:, None]
    ca[:, CA_SA:CA_SA + NKA] = log(many(PAST + tt - np.arange(NKA)[None, :]))
    tt = tt[0:64]
    dist = 512 + tt - np.arange(NKW)[None, :]
    ca[0:64, CA_SW:CA_SW + NKW] = mask((dist >= 0) & (dist <= 512))
    ca[0:64, CA_SN:CA_SN + NT] = mask(np.arange(NT)[None, :] <= tt)
    c, j = 16 * np.arange(NC_S)[:, None], 64 * np.arange(NSEL)[None, :]
    ca[0:NC_S, CA_OV:CA_OV + NSEL] = (c < j + 64) & (c + 32 > j)
    r = np.arange(64)
    ca[0:64, CA_GS:CA_GS + 64] = (r[:, None] // 32 == r[None, :] // 32) & (r[:, None] % NT == r[None, :] % NT)
    ca[:, CA_RV:CA_RV + 14] = 13 - np.arange(14)
    return {"c0": c0, "ca": ca, "iota_pairs": np.tile(np.arange(NPAIR, dtype=np.float32), (P, 1)),
            "iota": np.tile(np.arange(P, dtype=np.float32), (P, 1))}


def layouts(x):
    a = {n: np.asarray(v) for n, v in x.items()}
    out = constants()
    rows = np.concatenate([a["x_prompt"].reshape(SEQ, D), a["x_sample"].reshape(NB * NT, D)])
    out["xT"] = rows.reshape(ROWS, KD, P).transpose(2, 1, 0)
    out["x_rows"] = rows
    w = a["w_in"][0]
    cut = np.cumsum([0, 512, 512, 512, 512] + [128] * 6 + [24])
    qa, ka, va, qb, kc, vc, ks, vs, kw, vw, gl = [w[:, cut[i]:cut[i + 1]] for i in range(11)]
    pair = [h for g in range(G) for h in (g, g + G)]
    qb = qb.reshape(D, HEADS, HD)[:, pair].reshape(D, 512)
    blocks = [qb, qa, ka, np.concatenate([ks, kw, gl], 1), va, np.concatenate([kc, vc, vs, vw], 1)]
    out["w_in"] = np.concatenate([b.reshape(KD, P, -1).transpose(1, 0, 2).reshape(P, -1) for b in blocks], 1)
    pool = lambda n: a[n][0]
    cp = [pool(n).reshape(80, 8, 8, 2, KVH, HD).transpose(0, 3, 5, 4, 2, 1) for n in ("cache_cmp_k", "cache_cmp_v")]
    out["cmp_pool"] = np.stack([c.reshape(80, P, P) for c in cp], 2).reshape(80, P, 2 * P)
    kp = pool("cache_sel_k").transpose(0, 2, 3, 1).reshape(80, P, P)
    out["sel_pool"] = np.stack([kp, pool("cache_sel_v").reshape(80, P, P)], 2).reshape(80, P, 2 * P)
    out["a_k"] = a["cache_a_k"][0].reshape(NB, PAST, 4, P).transpose(0, 3, 2, 1)
    out["a_v"] = a["cache_a_v"][0].reshape(NB, P, 8 * 512)
    out["w_k"] = a["cache_win_k"][0].reshape(NB, 512, P).transpose(0, 2, 1)
    out["w_v"] = a["cache_win_v"][0].reshape(NB, P, 4 * P)
    wo = a["w_o"][0]
    wo = np.concatenate([wo[0:512], wo[512:].reshape(HEADS, HD, D)[pair].reshape(512, D)])
    out["w_o"] = wo.reshape(KD, P, D).transpose(1, 0, 2)
    for n in ("ln1_g", "ln1_b", "ln2_g", "ln2_b"):
        out[n] = a[n][0]
    out["peer_wq"] = a["peer_wq"][0].reshape(KD, P, HH, P).transpose(2, 1, 0, 3)
    out["peer_keys"] = np.stack([a["peer_k1"][0], a["peer_k2"][0]], 1).reshape(HH, P, P).transpose(2, 0, 1)
    out["peer_u"] = a["peer_u"][0].reshape(P, NE, KD, P).transpose(1, 3, 2, 0).reshape(NE, P, D)
    out["peer_v"] = a["peer_v"][0].reshape(P, NE, D).transpose(1, 0, 2)
    out["page_table"] = a["page_table"].reshape(1, -1)
    for n in "kv":
        out[f"w1{n}"] = a[f"cmp_w1_{n}"][0].reshape(CMP_W1, P, 256).transpose(1, 0, 2)
        out[f"w2{n}"] = a[f"cmp_w2_{n}"][0].reshape(2, P, HD).transpose(1, 0, 2)
    out["pe"] = np.stack([a[f"cmp_pe_{n}"][0].reshape(CMP_W1, P).T for n in "kv"], 1)
    return {n: np.ascontiguousarray(v) for n, v in out.items()}


OUTS = {"o_ak": (ROWS, 512), "o_av": (ROWS, 512), "o_kv": (ROWS, 512), "o_ksw": (ROWS, 256), "o_y": (ROWS, D),
        "keep_ak": (NB, P, 4, PAST - NT), "keep_av": (NB, P - 1, 8 * 512),
        "keep_wk": (NB, P, 512 - NT), "keep_wv": (NB, P - 2, 4 * P)}
SEMS = """x_in0 x_in1 x_in2 x_in3 proj w_in0 w_in1 c0 w1 evac roped out0 out_kv gate gate_e gate_a gate_out turned turned_out rope_c
ptab c16 pe_in cmp_zero cmp_slot_free cmp_pg0 cmp_pg1 cmp_bias cmp_turn cmp_rp cmp_hid cmp_gelu cmp_second cmp_done
ca gs ld_ka0 ld_ka1 ld_pg0 ld_pg1 ld_v0 ld_v1 kept diag0 diag
p_scores p_masked p_max p_cmax p_csum p_exp p_rec p_fac p_turned p_turned_out p_pv p_zero p_q p_weighed p_OT
s_scores s_read s_max s_exp s_rec s_fac s_turned s_turned_out s_pv s_sel_used s_branch s_normed s_out_turned s_OT i_pc i_mm i_dve i_sel i_pen
ld_wo0 ld_wo1 ld_xr ld_ky ld_wq0 ld_wq1 ld_wq2 ld_wq3 o_mm x_turn x_out x_hi x_lo q_mm q_out sc_mm sc_out
l1_sum l1_st l1_var l1_root l1_g l1_ln top topr topb top2 ixf be ber beb bei pr128 pair pair_v bf g_max g_sub g_exp g_den g_fin
id_eq id_mul id_sum id_turn id_out split
l2_sum l2_st l2_var l2_root l2_g l2_ln ld_u0 ld_u1 ld_v20 ld_v21 ld_ln2 y_low u_hi u_lo v_hi v_lo h_mm gelu hw hw_hi hw_lo y_mm
c_mm W_out onehot onehot_12 oh_e zero iota iota_in st_y""".split()


def build(nc, d, upto=9):
    with ExitStack() as ctx:
        sb = lambda n, sh, dt=F32: ctx.enter_context(nc.sbuf_tensor(n, sh, dt))
        s = {n: ctx.enter_context(nc.semaphore(n)) for n in SEMS}
        t = Names()
        t.psum = ctx.enter_context(nc.psum_tensor("psum", [P, 8, 512], F32))
        t.c0 = sb("c0", [P, C0_W])
        t.OT = sb("OT", [P, KD, ROWS])
        t.big = sb("big", [P, KD * D])
        att = ctx.enter_context(ExitStack())
        ab = lambda n, sh, dt=F32: att.enter_context(nc.sbuf_tensor(n, sh, dt))
        t.hk = ab("h_keep", [P, TILES, HK_W])
        t.TT = ab("qk_turned", [P, NTT, ROWS])
        t.gates = ab("gates", [P, TILES, 24])
        t.kc = ab("kc", [P, NB + 1, NC_S])
        t.vc = ab("vc", [NC_S, NB + 1, P])
        t.ptab = ab("ptab", [1, NB * PAGES], I32)
        t.ca = ab("att_consts", [P, CA_W])
        t.gs = ab("gates_ht", [64, NB, 3])
        with ExitStack() as c1:
            cb = lambda n, sh, dt=F32: c1.enter_context(nc.sbuf_tensor(n, sh, dt))
            t.w1k, t.w1v = cb("w1k", [P, CMP_W1, 256]), cb("w1v", [P, CMP_W1, 256])
            w2 = t.big[:, BIG_W2:BIG_PE].rearrange("p (a h n) -> p a h n", a=2, h=2)
            t.w2k, t.w2v = w2[:, 0], w2[:, 1]
            t.pe = t.big[:, BIG_PE:BIG_END].rearrange("p (a c) -> p a c", a=2)
            t.cpg = cb("cmp_pages", [P, 2, PAGES + 3, 2, KVH, 8, 8])
            project_block(nc, d, t, s)
            compress_block(nc, d, t, s)
        attention_block(nc, d, t, s)
        att.close()
        t.x1 = sb("x1", [P, TILES, D])
        t.x1h, t.x1l = sb("x1_hi", [P, KD, ROWS], F32R), sb("x1_lo", [P, KD, ROWS], F32R)
        t.i1 = sb("i1", [P, ROWS], BF16)
        t.i2 = sb("i2", [P, SEGS, ROWS], BF16)
        t.gp = sb("gate_parts", [P, 3, ROWS], BF16)
        route_block(nc, d, t, s)
        expert_block(nc, d, t, s)


def kernel(**inputs):
    import concourse.bacc as bacc
    from concourse.bass_utils import run_bass_kernel_spmd

    nc = bacc.Bacc("TRN2", target_bir_lowering=False, num_devices=1)
    arrays = layouts(inputs)
    d = Names()
    for n, v in arrays.items():
        d.__dict__[n] = nc.dram_tensor("in_" + n, v.shape, mybir.dt.from_np(v.dtype), kind="ExternalInput").ap()
    for n, shape in OUTS.items():
        d.__dict__[n] = nc.dram_tensor(n, shape, F32, kind="ExternalOutput").ap()
    d.gate_rows = nc.dram_tensor("gate_rows", (NB * NT, 24), F32, kind="Internal").ap()
    build(nc, d)
    r = run_bass_kernel_spmd(nc, [{"in_" + n: v for n, v in arrays.items()}], core_ids=[0]).results[0]
    o = {n: r[n] for n in OUTS}
    new = lambda a: a[SEQ:].reshape(1, NB, NT, -1, HD)
    old = lambda a: a[:SEQ].reshape(1, 1, SEQ, -1, HD)
    kc, vc, vs, vw = [o["o_kv"][:, P * i:P * (i + 1)] for i in range(4)]
    ks, kw = o["o_ksw"][:, 0:P], o["o_ksw"][:, P:2 * P]
    join = lambda kept, fresh: np.concatenate([kept, new(fresh)], 2)
    a_k = o["keep_ak"].transpose(0, 3, 2, 1).reshape(1, NB, PAST - NT, HEADS, HD)
    a_v = o["keep_av"].reshape(1, NB, PAST - NT, HEADS, HD)
    w_k = o["keep_wk"].transpose(0, 2, 1).reshape(1, NB, 512 - NT, KVH, HD)
    w_v = o["keep_wv"].reshape(1, NB, 512 - NT, KVH, HD)
    y = o["o_y"]
    return (y[:SEQ].reshape(1, SEQ, D), y[SEQ:].reshape(NB, NT, D),
            old(o["o_ak"]), old(o["o_av"]), old(kc), old(vc), old(ks), old(vs), old(kw), old(vw),
            join(a_k, o["o_ak"]), join(a_v, o["o_av"]), new(kc), new(vc), new(ks), new(vs),
            join(w_k, kw), join(w_v, vw))
```

```python
from contextlib import ExitStack

import numpy as np
import concourse.bass as bass
from concourse import mybir

F32 = mybir.dt.float32
F32R = mybir.dt.float32r
BF16 = mybir.dt.bfloat16
I32 = mybir.dt.int32
U32 = mybir.dt.uint32
ALU = mybir.AluOpType
ACT = mybir.ActivationFunctionType
AX = mybir.AxisListType

class Names:
    pass


P = 128
D = 1024
KD = D // P
SEQ = 256
NB = 8
NT = 8
ROWS = SEQ + NB * NT
TILES = 3
RT = [P, P, NB * NT]
PAST = 1024
HD = 64
HEADS = 8
KVH = 2
G = HEADS // KVH
SCALE = HD ** -0.5
NEG = -1e30
ROT = HD // 4
HALF = ROT // 2
ALPHA = 2.0 ** 0.25
EPS = 1e-5
TINY = float(np.finfo(np.float32).tiny)

HK_VA, HK_KC, HK_VC, HK_VS, HK_VW, HK_GL, HK_W = 0, 512, 640, 768, 896, 1024, 1048
HR_QB, HR_QR, HR_QA, HR_KA, HR_KS, HR_W = 0, 512, 1024, 1536, 2048, 2304
ROPED = (HR_W - HR_QR) // HD
WCOLS = [512, 512, 512, 280, 512, 512]
WOFF = [KD * c for c in np.cumsum([0] + WCOLS).tolist()]
QB0, QR0, QA0, KA0, KS0, KW0, NTT = 0, 4, 8, 12, 16, 17, 18

PAGES = PAST // P
CMP_W1 = 16
NC_S = 63
NC_P = 15
NC_ALL = 64 + NC_P
PE_BLOCK = 80
NG_ALL = 8 * (PAGES + 3)
C0_W = P + 2 * TILES * HALF


BIG_LOW = 2 * KVH * 16 * HD
BIG_RT = BIG_LOW + 512
BIG_W2 = BIG_RT + 4 * ROPED * HALF
BIG_PE = BIG_W2 + 2 * 2 * HD
BIG_END = BIG_PE + 2 * CMP_W1


def project_block(nc, d, t, s):
    with ExitStack() as ctx:
        sb = lambda n, sh, dt=F32: ctx.enter_context(nc.sbuf_tensor(n, sh, dt))
        xT = t.big[:, 0:KD * ROWS].rearrange("p (k n) -> p k n", k=KD)
        xh, xl = sb("x_hi", [P, KD, HWC], F32R), sb("x_lo", [P, KD, SEQ], F32R)
        w = [x[:, 1024 * y:1024 * (y + 1)] for x in (t.ca, t.big[:, BIG_END:BIG_END + 2048]) for y in range(2)][0:3]
        wh, wl = sb("w_in_hi", [P, 2, 2 * 512], F32R), sb("w_in_lo", [P, 2, 2 * 512], F32R)
        low = t.big[0:64, BIG_LOW:BIG_LOW + 512]
        hr2 = sb("h_rope", [P, 2, HR_W])
        hr = [hr2[:, 0], hr2[:, 1], t.OT[:].rearrange("p k n -> p (k n)")[:, 0:HR_W]]
        rt = t.big[:, BIG_RT:BIG_W2].rearrange("p (x g n) -> p x g n", x=4, g=ROPED)
        ps = [t.psum[:, i] for i in range(6)]
        pt = [t.psum[:, 6 + i].rearrange("p (c n) -> p c n", n=P) for i in range(2)]
        block = ctx.enter_context(nc.Block())
        hk, TT, c0 = t.hk, t.TT, t.c0

        def places(n, i):
            r = RT[i]
            if n == 3:
                return [(hr[i][0:r, HR_KS:HR_W], 0, 256), (hk[0:r, i, HK_GL:HK_W], 256, 280)]
            dst = hr[i][0:r, 512 * (n + (n > 0)):512 * (n + (n > 0)) + 512] if n < 3 else hk[0:r, i, 512 * (5 - n):512 * (6 - n)]
            return [(dst, 0, 512)]

        ident = c0[:, 0:P]
        nblk = len(WCOLS)
        steps = [(n, x) for n in range(nblk) for x in range(4)]
        c16 = t.big[0:16, 0:BIG_LOW].rearrange("p (a k r n) -> p a k r n", a=2, k=KVH, r=16)
        pr = t.psum[:, 0].rearrange("p (x g) -> p x g", g=16)

        @block.sync
        def _(sp):
            for u, (n, x) in enumerate(steps):
                c = 2 * WCOLS[n]
                if n == 0:
                    sp.dma_start(xT[:, 2 * x:2 * x + 2], d.xT[:, 2 * x:2 * x + 2]).then_inc(s[f"x_in{x}"], 16)
                if u >= 3:
                    sp.wait_ge(s["w_lo"], u - 2)
                sp.dma_start(w[u % 3][:, 0:c], d.w_in[:, WOFF[n] + x * c:WOFF[n] + (x + 1) * c]).then_inc(s[f"w_in{u % 3}"], 16)
                if (n, x) == (1, 0):
                    sp.dma_start(c0[:], d.c0).then_inc(s["c0"], 16)
                    sp.dma_start(t.pe, d.pe).then_inc(s["c0"], 16)
                    sp.dma_start(t.ptab[:], d.page_table).then_inc(s["ptab"], 16)
                if (n, x) == (2, 0):
                    sp.dma_start(t.w1k[:], d.w1k).then_inc(s["w1"], 16)
                    sp.dma_start(t.w2k, d.w2k).then_inc(s["w1"], 16)
                if (n, x) == (3, 0):
                    sp.dma_start(t.w1v[:], d.w1v).then_inc(s["w1"], 16)
                    sp.dma_start(t.w2v, d.w2v).then_inc(s["w1"], 16)
            sp.wait_ge(s["evac"], 3 * (nblk - 1))
            for i in range(TILES):
                sp.dma_start(d.o_kv[P * i:P * i + RT[i], :], hk[0:RT[i], i, 512:1024]).then_inc(s["out_kv"], 16)
            sp.wait_ge(s["out_kv"], 48)
            for x in range(2 * KVH):
                sp.dma_start(c16[:, x // KVH, x % KVH], d.o_kv.rearrange("(j r) c -> j r c", r=16)[0:16, :, x * HD:(x + 1) * HD])\
                  .then_inc(s["c16"], 16)
            for i in range(TILES):
                r, o = RT[i], P * i
                sp.wait_ge(s["roped"], i + 1)
                sp.dma_start(d.o_ak[o:o + r, :], hr[i][0:r, HR_KA:HR_KS]).then_inc(s["out0"], 16)
                sp.dma_start(d.o_ksw[o:o + r, :], hr[i][0:r, HR_KS:HR_W]).then_inc(s["out0"], 16)
            sp.wait_ge(s["evac"], 3 * nblk)
            for i in range(TILES):
                sp.dma_start(d.o_av[P * i:P * i + RT[i], :], hk[0:RT[i], i, 0:512]).then_inc(s["out0"], 16)
            sp.wait_ge(s["gate"], 2)
            sp.dma_start(d.gate_rows, t.gates[0:RT[2], 2, :]).then_inc(s["out0"], 16)
            sp.wait_ge(s["out0"], 16 * 10)

        @block.tensor
        def _(pe):
            def turn(i):
                pe.wait_ge(s["c0"], 32)
                pe.wait_ge(s["roped"], i + 1)
                for g in range(5):
                    u = 5 * i + g
                    if u >= 2:
                        pe.wait_ge(s["turned_out"], u - 1)
                    for c in range(4 if g < 4 else 2):
                        mm = pe.transpose(pt[u % 2][:, c, 0:RT[i]], hr[i][0:RT[i], (4 * g + c) * P:(4 * g + c + 1) * P],
                                          ident[0:RT[i], 0:RT[i]])
                    mm.then_inc(s["turned"], 1)
                    if 8 <= u < 12:
                        turn_prompt((u - 8) // KVH, u % KVH)

            def turn_prompt(a, k):
                pe.wait_ge(s["c16"], 64)
                pe.wait_ge(s["evac"], 3 * (nblk - 1))
                for r in range(8):
                    mm = pe.transpose(pr[:, (a * KVH + k) * 8 + r, :], c16[0:16, a, k, 2 * r:2 * r + 2, :].rearrange("j r e -> j (r e)"), ident[0:16, 0:16])
                mm.then_inc(s["cmp_turn"], 1)

            for u, (n, x) in enumerate(steps):
                pe.wait_ge(s["w_lo"], u + 1)
                c = WCOLS[n]
                for i in range(TILES):
                    if n >= 2 and x == 0:
                        pe.wait_ge(s["evac"], 3 * (n - 2) + i + 1)
                    out = ps[3 * (n % 2) + i]
                    for k in range(2):
                        for y, (a, b) in enumerate(((xh, wh), (xh, wl), (xl, wh))[0:3 if i < 2 else 2]):
                            mm = pe.matmul(out[:, 0:c], a[:, 2 * x + k, P * i:P * i + P], b[:, u % 2, k * c:(k + 1) * c],
                                           start=(x + k + y == 0), stop=(x == 3 and k == 1 and y == (2 if i < 2 else 1)))
                    if x == 3 and i < 2:
                        mm.then_inc(s["proj"], 1)
                mm.then_inc(s["w_used"], 1)
            for i in range(TILES):
                turn(i)

        @block.scalar
        def _(act):
            def evac(n):
                if n:
                    act.wait_ge(s["evac"], 3 * n)
                for i in range(TILES):
                    if i < 2:
                        act.wait_ge(s["proj"], 2 * n + i + 1)
                    else:
                        act.wait_ge(s["w_used"], 4 * (n + 1))
                    if i == 2:
                        c = WCOLS[n]
                        act.activation(low[:, 0:c], ps[3 * (n % 2) + 2][64:P, 0:c], ACT.Copy).then_inc(s["h_low"], 1)
                        continue
                    src = ps[3 * (n % 2) + i]
                    for dst, a, b in places(n, i):
                        ins = act.activation(dst, src[:, a:b], ACT.Copy)
                    ins.then_inc(s["evac"], 1)

            for u, (n, x) in enumerate(steps):
                c = 2 * WCOLS[n]
                if n == 0:
                    k = slice(2 * x, 2 * x + 2)
                    act.wait_ge(s[f"x_in{x}"], 16)
                    act.activation(xh[:, k, 0:ROWS], xT[:, k], ACT.Copy)
                act.wait_ge(s[f"w_in{u % 3}"], 16 * (u // 3 + 1))
                if u >= 2:
                    act.wait_ge(s["w_used"], u - 1)
                act.activation(wh[:, u % 2, 0:c], w[u % 3][:, 0:c], ACT.Copy).then_inc(s["w_hi"], 1)
                if n and x == 1:
                    evac(n - 1)
                if u >= 8:
                    if u == 8:
                        act.wait_ge(s["ptab"], 16)
                    load_cmp_pages(act, t, d, s, (u - 8) // PAGES, 0, [u - 8])
            evac(nblk - 1)
            act.wait_ge(s["evac"], 12)
            act.activation(t.gates[:, 0:2, :], hk[:, 0:2, HK_GL:HK_W], ACT.Exp, scale=-1.0).then_inc(s["gate_e"], 1)
            act.activation(t.gates[0:RT[2], 2, :], hk[0:RT[2], 2, HK_GL:HK_W], ACT.Exp, scale=-1.0).then_inc(s["gate_e"], 1)

        @block.vector
        def _(ve):
            cos = lambda i: c0[:, P + HALF * i:P + HALF * (i + 1)]
            sin = lambda i: c0[:, P + HALF * (TILES + i):P + HALF * (TILES + i + 1)]
            def split(u):
                n, x = steps[u]
                c = 2 * WCOLS[n]
                ve.wait_ge(s["w_hi"], u + 1)
                if n == 0:
                    k = slice(2 * x, 2 * x + 2)
                    ve.tensor_tensor(xh[:, k, ROWS:HWC], xT[:, k, SEQ:ROWS], xh[:, k, SEQ:ROWS].bitcast(F32), ALU.subtract)
                    ve.tensor_tensor(xl[:, k], xT[:, k, 0:SEQ], xh[:, k, 0:SEQ].bitcast(F32), ALU.subtract)
                if u >= 2:
                    ve.wait_ge(s["w_used"], u - 1)
                ve.tensor_tensor(wl[:, u % 2, 0:c], w[u % 3][:, 0:c], wh[:, u % 2, 0:c].bitcast(F32), ALU.subtract).then_inc(s["w_lo"], 1)

            def turned_out(i):
                for g in range(5):
                    u, n = 5 * i + g, 4 if g < 4 else 2
                    ve.wait_ge(s["turned"], u + 1)
                    ve.tensor_copy(TT[:, 4 * g:4 * g + n, P * i:P * i + RT[i]], pt[u % 2][:, 0:n, 0:RT[i]]).then_inc(s["turned_out"], 1)

            def evac_last(n):
                ve.wait_ge(s["h_low"], n + 1)
                ve.wait_ge(s["evac"], 3 * n + 2)
                for dst, a, b in places(n, 2):
                    ins = ve.scalar_tensor_tensor(dst, ps[3 * (n % 2) + 2][0:64, a:b], 1.0, low[:, a:b], ALU.mult, ALU.add)
                ins.then_inc(s["evac"], 1)

            def turn_rope(i):
                r = RT[i]
                ve.wait_ge(s["evac"], 12)
                ve.tensor_copy(hr[i][0:r, HR_QR:HR_QA], hr[i][0:r, HR_QB:HR_QR]).then_inc(s["rope_c"], 1)
                ve.wait_ge(s["rope_c"], 3 * i + 1)
                z = hr[i][0:r, HR_QR:HR_W].rearrange("p (g d) -> p g d", d=HD)
                x1, x2 = z[:, :, 0:HALF], z[:, :, HALF:ROT]
                cb = cos(i)[0:r].unsqueeze(1).broadcast_to([r, ROPED, HALF])
                sn = sin(i)[0:r].unsqueeze(1).broadcast_to([r, ROPED, HALF])
                if i:
                    ve.wait_ge(s["roped"], i)
                for j, (a, b) in enumerate([(x1, cb), (x2, sn), (x2, cb), (x1, sn)]):
                    ins = ve.tensor_tensor(rt[0:r, j], a, b, ALU.mult)
                ins.then_inc(s["rope_c"], 1)
                ve.wait_ge(s["rope_c"], 3 * i + 2)
                ve.tensor_tensor(x1, rt[0:r, 0], rt[0:r, 1], ALU.subtract).then_inc(s["rope_c"], 1)
                ve.tensor_tensor(x2, rt[0:r, 2], rt[0:r, 3], ALU.add).then_inc(s["roped"], 1)
            for u, (n, x) in enumerate(steps):
                split(u)
                if n and x == 1:
                    evac_last(n - 1)
                if n == 4 and x >= 2:
                    if x == 2:
                        ve.wait_ge(s["c0"], 32)
                    turn_rope(x - 2)
                if n == 5 and x == 0:
                    turn_rope(2)
            evac_last(nblk - 1)
            for i in range(TILES):
                turned_out(i)
            ve.wait_ge(s["gate_e"], 2)
            g2 = [t.gates[:, 0:2, :], t.gates[0:RT[2], 2, :]]
            for a in g2:
                ve.tensor_scalar(a, a, 1.0, None, ALU.add).then_inc(s["gate_a"], 1)
            ve.wait_ge(s["gate_a"], 2)
            for a in g2:
                ve.reciprocal(a, a).then_inc(s["gate"], 1)
            own = t.cpg[:, 0, PAGES:PAGES + 2].rearrange("p w a k r g -> p (a k r) w g")
            ve.wait_ge(s["cmp_rp"], 1)
            for g in range(2):
                for k in range(KVH):
                    ve.tensor_copy(t.cpg[:, 0, PAGES + 2, :, k, :, g], t.pe[:, :, 8 * g:8 * g + 8])
            ve.wait_ge(s["cmp_turn"], 2 * KVH)
            ve.tensor_copy(own, pr.rearrange("p x (w g) -> p x w g", w=2)).then_inc(s["cmp_rp"], 1)

        @block.gpsimd
        def _(gp):
            gp.memset(t.cpg[:, 0, PAGES + 2], 0.0).then_inc(s["cmp_rp"], 1)


def load_cmp_pages(eng, t, d, s, slot, first, places=range(PAGES)):
    for p in places:
        r = eng.value_load(t.ptab[0:1, bass.ds(first + p, 1)], min_val=0, max_val=79)
        eng.dma_start(t.cpg[:, slot, p % PAGES].rearrange("p a k r g -> p (a k r g)"),
                      d.cmp_pool[bass.ds(r, 1)].rearrange("a p n -> p (a n)")).then_inc(s[f"cmp_pg{slot}"], 16)


def compress_block(nc, d, t, s):
    with ExitStack() as ctx:
        sb = lambda n, sh, dt=F32: ctx.enter_context(nc.sbuf_tensor(n, sh, dt))
        hid = sb("cmp_hidden", [P, 2, 2, KVH, NC_ALL])
        bias = sb("cmp_bias", [P, 2, 2])
        ph = [t.psum[:, i, 0:4 * (NG_ALL + 1)].rearrange("p (h k n) -> p h k n", h=2, k=KVH) for i in range(2)]
        po = [t.psum[:, 2 + i] for i in range(2)]
        block = ctx.enter_context(nc.Block())
        pages, w1, w2 = t.cpg, [t.w1k, t.w1v], [t.w2k, t.w2v]
        units = [(b, a) for b in range(NB) for a in range(2)]
        blocks = lambda b: NC_S if b else NC_ALL

        @block.sync
        def _(sp):
            sp.dma_start(t.ca[:], d.ca).then_inc(s["ca"], 16)
            for br in range(3):
                rows = d.gate_rows.rearrange("(b t) (r h) -> r h t b", t=NT, r=3)[br]
                for h in range(HEADS):
                    sp.dma_start(t.gs[h * NT:(h + 1) * NT, :, br], rows[h], allow_slow_non_contiguous=True).then_inc(s["gs"], 16)
            with sp.Fori(0, NB // 2 - 1) as i:
                for b in range(2):
                    sp.wait_ge(s["cmp_slot_free"], i * 4 + (2 * b + 2))
                    load_cmp_pages(sp, t, d, s, b, i * (2 * PAGES) + (b + 2) * PAGES)

        @block.tensor
        def _(pe):
            pe.wait_ge(s["w1"], 64)

            def hidden(u):
                b, a = units[u]
                pe.wait_ge(s[f"cmp_pg{b % 2}"], 16 * PAGES * (b // 2 + 1))
                if u >= 2:
                    pe.wait_ge(s["cmp_gelu"], 2 * (u - 1))
                pages_n = PAGES if b else PAGES + 3
                n = 8 * pages_n
                for h in range(2):
                    for c in range(CMP_W1):
                        rhs = pages[:, b % 2, 0:pages_n, a, :, c % 8, :].rearrange("p g k b -> p k g b")
                        o = ph[u % 2][:, h, :, 1:1 + n] if c < 8 else ph[u % 2][:, h, :, 0:n]
                        mm = pe.matmul(o.rearrange("p k (g b) -> p k g b", b=8), w1[a][:, c, h * P:(h + 1) * P], rhs,
                                       start=(c == 0), stop=(c == CMP_W1 - 1), skip_group_check=True)
                mm.then_inc(s["cmp_hid"], 1)

            def second(u):
                b, a = units[u]
                n = blocks(b)
                pe.wait_ge(s["cmp_gelu"], 2 * (u + 1))
                if u >= 2:
                    pe.wait_ge(s["cmp_done"], u - 1)
                if a == 0:
                    for k in range(KVH):
                        for h in range(2):
                            mm = pe.matmul(po[u % 2][k * HD:(k + 1) * HD, 0:n], w2[0][:, h, :], hid[:, u % 2, h, k, 0:n], start=(h == 0), stop=(h == 1))
                else:
                    for x, (c0, c1) in enumerate([(0, NC_S)] if b else [(0, NC_S), (64, NC_ALL)]):
                        for k in range(KVH):
                            for h in range(2):
                                mm = pe.matmul(po[u % 2][0:c1 - c0, x * P + k * HD:x * P + (k + 1) * HD], hid[:, u % 2, h, k, c0:c1], w2[1][:, h, :],
                                               start=(h == 0), stop=(h == 1))
                mm.then_inc(s["cmp_second"], 1)

            for u in range(len(units)):
                hidden(u)
                if u >= 1:
                    second(u - 1)
            second(len(units) - 1)

        @block.scalar
        def _(act):
            for u, (b, a) in enumerate(units):
                n = blocks(b)
                act.wait_ge(s["cmp_hid"], u + 1)
                if b == 0:
                    act.wait_ge(s["cmp_bias"], a + 1)
                if u >= 2:
                    act.wait_ge(s["cmp_second"], u - 1)
                for h in range(2):
                    act.activation(hid[:, u % 2, h, :, 0:n], ph[u % 2][:, h, :, 1:1 + n], ACT.Gelu_apprx_tanh,
                                   bias=bias[:, a, h:h + 1]).then_inc(s["cmp_gelu"], 1)

        @block.vector
        def _(ve):
            for u, (b, a) in enumerate(units):
                ve.wait_ge(s["cmp_hid"], u + 1)
                ve.sem_inc(s["cmp_slot_free"], 1)
                if b == 0:
                    ve.tensor_copy(bias[:, a, :], ph[u % 2][:, :, 0, 1 + PE_BLOCK]).then_inc(s["cmp_bias"], 1)
                ve.wait_ge(s["cmp_second"], u + 1)
                if a == 0:
                    if b == 0:
                        ve.tensor_copy(t.kc[:, NB, 0:NC_P], po[u % 2][:, 64:NC_ALL])
                    ve.tensor_copy(t.kc[:, b, :], po[u % 2][:, 0:NC_S]).then_inc(s["cmp_done"], 1)
                else:
                    if b == 0:
                        ve.tensor_copy(t.vc[0:NC_P, NB, :], po[u % 2][0:NC_P, P:2 * P])
                    ve.tensor_copy(t.vc[:, b, :], po[u % 2][0:NC_S, 0:P]).then_inc(s["cmp_done"], 1)


NKA, NKW = PAST + NT, 512 + NT
SS, SW = 0, NKA
SB_COLS = NKA + NKW
PR = 32
CA_PA = 0
CA_PC = CA_PA + 3 * P
CA_PB = CA_PC + 3 * P
CA_SA = CA_PB + 2 * NC_P
CA_SW = CA_SA + NKA
CA_SN = CA_SW + NKW
CA_OV = CA_SN + NT
CA_GS = CA_OV + 17
CA_RV = CA_GS + 64
CA_W = CA_RV + 14
NSEL = 17


def attention_block(nc, d, t, s):
    with ExitStack() as ctx:
        sb = lambda n, sh, dt=F32: ctx.enter_context(nc.sbuf_tensor(n, sh, dt))
        wk = sb("att_work", [P, 2 * (NKA + SB_COLS)])
        pp = wk[:, 0:2048].rearrange("p (s e n) -> p s e n", s=4, e=2)
        pT = wk[:, 2048:3072].rearrange("p (s x q) -> p s x q", s=2, x=4)
        nm = sb("att_negmax", [P, 64])
        sm = sb("att_sum", [P, 64])
        rs = sb("att_rsum", [P, 64])
        qd = wk[:, 3072:4096].rearrange("p (s e q) -> p s e q", s=4, e=2)
        ka = t.big[:].rearrange("p (s c n) -> p s c n", s=2, c=4)
        va = sb("a_vals", [P, 2, 8, 512])
        pg = sb("sel_pages", [P, 2, PAGES, 2, P])
        kw = sb("win_keys", [P, 2, 512])
        vw = sb("win_vals", [P, 2, 4, P])
        vn = sb("new_vals", [NT, 2, 768])
        qa = sb("qa_diag", [P, NB, 4, PR])
        qn = sb("qn_diag", [P, 2, NB, 64])
        sA = wk[:, 0:2 * NKA].rearrange("p (s n) -> p s n", s=2)
        sB = wk[0:64, 2 * NKA:2 * (NKA + SB_COLS)].rearrange("p (s n) -> p s n", s=2)
        zA = sb("smp_turned_a", [P, 2, 8, P])
        zAn = sb("smp_turned_a_new", [NT, 2, P])
        zB = sb("smp_turned_b", [P, 2, 14, 64])
        oA = sb("smp_out_a", [P, 2, P])
        oB = sb("smp_out_b", [64, 2, P])
        stA = sb("smp_stats_a", [P, NB, 3])
        stB = sb("smp_stats_b", [64, NB, 2, 4])
        pc = wk[0:64, 0:NB * NC_S].rearrange("p (b n) -> p b n", n=NC_S)
        pcT = sb("smp_cmp_turned", [NC_S, NB, 64])
        cst = sb("smp_cmp_stats", [64, 2, NB])
        x1 = wk[0:64, 512:512 + NB * NSEL]
        imp = wk[0:64, 704:704 + NB * 14].rearrange("p (b j) -> p b j", j=14)
        top = wk[0:64, 832:832 + NB * 8].rearrange("p (b j) -> p b j", j=8)
        tix = sb("smp_topi", [64, NB, 8], U32)
        tif = sb("smp_topf", [64, NB])
        pen = sb("smp_pen", [64, NB, 16])
        block = ctx.enter_context(nc.Block())
        hk, TT, OT, ident = t.hk, t.TT, t.OT, t.c0[:, 0:P]
        ca, gs = t.ca, t.gs
        bank = lambda i: t.psum[:, i]
        KINDS = ["A", "cmp", "sel", "win"]
        units = [(i, c, k) for i in range(2) for c in range(4) for k in KINDS]
        NU = len(units)

        def shape(u):
            i, _, k = units[u]
            return (NC_P, 1, NC_P) if k == "cmp" else (P * (i + 1), i + 1, P)

        def queries(u):
            return 3 * (u // 4) + min(u % 4, 2)

        last_reader = lambda x: 4 * (x // 3) + (0, 1, 3)[x % 3]

        chunk = lambda b, n: 6 * b + n

        @block.sync
        def _(sp):
            for b in range(NB):
                q = b % 2
                if b >= 2:
                    sp.wait_ge(s["s_scores"], chunk(b - 2, 3) + 1)
                sp.dma_start(ka[:, q], d.a_k[b]).then_inc(s[f"ld_ka{q}"], 16)
                sp.dma_start(kw[:, q], d.w_k[b]).then_inc(s[f"ld_ka{q}"], 16)
                if b >= 2:
                    sp.wait_ge(s["s_sel_used"], b - 1)
                for p in range(PAGES):
                    r = sp.value_load(t.ptab[0:1, b * PAGES + p:b * PAGES + p + 1], min_val=0, max_val=79)
                    sp.dma_start(pg[:, q, p].rearrange("p a n -> p (a n)"),
                                 d.sel_pool[bass.ds(r, 1)].rearrange("a p n -> p (a n)")).then_inc(s[f"ld_pg{q}"], 16)
                if b >= 2:
                    sp.wait_ge(s["s_pv"], b - 1)
                sp.dma_start(va[:, q].rearrange("p j n -> p (j n)"), d.a_v[b]).then_inc(s[f"ld_v{q}"], 16)
                sp.dma_start(vw[:, q].rearrange("p j n -> p (j n)"), d.w_v[b]).then_inc(s[f"ld_v{q}"], 16)
                o = SEQ + NT * b
                sp.dma_start(vn[:, q, 0:512], d.o_av[o:o + NT, :]).then_inc(s[f"ld_v{q}"], 16)
                sp.dma_start(vn[:, q, 512:768], d.o_kv[o:o + NT, 256:512]).then_inc(s[f"ld_v{q}"], 16)
            wo = t.big[:].rearrange("p (k n) -> p k n", k=KD)
            for k in range(0, KD, 2):
                if k == 0 or k == 4:
                    sp.wait_ge(s["s_scores"], chunk(NB - 2 + k // 4, 3) + 1)
                sp.dma_start(wo[:, k:k + 2], d.w_o[:, k:k + 2]).then_inc(s[f"ld_wo{k // 4}"], 16)

        @block.gpsimd
        def _(gp):
            gp.memset(qd, 0.0).then_inc(s["diag_zero"], 1)
            gp.memset(qa[:], 0.0).then_inc(s["diag_zero"], 1)
            gp.memset(qn[:], 0.0).then_inc(s["diag_zero"], 1)
            gp.memset(pen[:], 0.0).then_inc(s["diag_zero"], 1)
            gp.wait_ge(s["diag_zero"], 4)
            for x in range(3 * NU // 4):
                i, c, k = units[last_reader(x)]
                q = {"A": QA0, "cmp": QB0, "win": QR0}[k] + c
                if x >= 4:
                    gp.wait_ge(s["p_scores"], last_reader(x - 4) + 1)
                for e in range(2):
                    h = slice(e * HD, (e + 1) * HD)
                    ins = gp.tensor_copy(qd[h, x % 4, e, :], TT[h, q, P * i:P * i + P])
                ins.then_inc(s["p_q"], 1)

        @block.tensor
        def _(pe):
            def p_scores(u):
                i, c, k = units[u]
                n = shape(u)[0]
                if u >= 2:
                    pe.wait_ge(s["p_masked"], u - 1)
                pe.wait_ge(s["p_q"], queries(u) + 1)
                keys = {"A": TT[:, KA0 + c, 0:n], "cmp": t.kc[:, NB, 0:min(n, NC_P)], "sel": TT[:, KS0, 0:n], "win": TT[:, KW0, 0:n]}[k]
                for e in range(2):
                    mm = pe.matmul(bank(2 * (u % 2) + e)[:, 0:n], qd[:, queries(u) % 4, e, :], keys, start=True, stop=True)
                mm.then_inc(s["p_scores"], 1)

            def p_turn(u):
                n, nk, kr = shape(u)
                pe.wait_ge(s["p_weighed"], u + 1)
                if u >= 2:
                    pe.wait_ge(s["p_turned_out"], u - 1)
                for e in range(2):
                    for x in range(nk):
                        mm = pe.transpose(bank(4 + u % 2)[0:kr, (2 * e + x) * P:(2 * e + x + 1) * P], pp[:, u % 4, e, x * P:x * P + kr], ident)
                mm.then_inc(s["p_turned"], 1)

            def p_pv(u):
                i, c, k = units[u]
                n, nk, kr = shape(u)
                pe.wait_ge(s["p_turned_out"], u + 1)
                g = u // 4
                if g and k in ("A", "cmp"):
                    pe.wait_ge(s["p_OT"], 2 * g - (k == "A"))
                for x in range(nk):
                    for e in range(2):
                        v = {"A": hk[:, x, (2 * c + e) * HD:(2 * c + e + 1) * HD], "cmp": t.vc[0:min(kr, NC_P), NB, e * HD:(e + 1) * HD],
                             "sel": hk[:, x, HK_VS + e * HD:HK_VS + (e + 1) * HD],
                             "win": hk[:, x, HK_VW + e * HD:HK_VW + (e + 1) * HD]}[k]
                        mm = pe.matmul(bank(6 + (k != "A"))[e * HD:(e + 1) * HD, 0:P], v, pT[0:kr, u % 2, 2 * e + x, :],
                                       start=(x == 0 and k in ("A", "cmp")), stop=(x == nk - 1 and k in ("A", "win")), skip_group_check=True)
                mm.then_inc(s["p_pv"], 1)

            for u in range(NU + 3):
                if u < NU:
                    p_scores(u)
                if 2 <= u < NU + 2:
                    p_turn(u - 2)
                if u >= 3:
                    p_pv(u - 3)
            pe.wait_ge(s["diag"], 12)
            for b in range(NB):
                mm = pe.matmul(bank(0)[0:64, b * NC_S:(b + 1) * NC_S], qn[:, 0, b, :], t.kc[:, b, :], start=True, stop=True)
            mm.then_inc(s["i_mm"], 1)
            pe.wait_ge(s["i_pc"], 4)
            for b in range(NB):
                mm = pe.transpose(bank(1)[0:NC_S, b * 64:(b + 1) * 64], pc[:, b, :], ident[0:64, 0:64])
            mm.then_inc(s["i_mm"], 1)
            pe.wait_ge(s["i_pc"], 5)
            for b in range(NB):
                mm = pe.matmul(bank(2)[0:64, b * NSEL:(b + 1) * NSEL], pcT[:, b, :], ca[0:NC_S, CA_OV:CA_OV + NSEL], start=True, stop=True)
            mm.then_inc(s["i_mm"], 1)
            pe.wait_ge(s["i_pc"], 6)
            pe.matmul(bank(7)[0:64, 0:NB * NSEL], ca[0:64, CA_GS:CA_GS + 64], x1[:], start=True, stop=True).then_inc(s["i_mm"], 1)

            def chunk_begin(b, n):
                q = chunk(b, n)
                if q >= 3:
                    pe.wait_ge(s["s_read"], q - 2)
                return bank(q % 3)

            def scores(b):
                q = b % 2
                o = chunk_begin(b, 0)
                r = slice(SEQ + NT * b, SEQ + NT * (b + 1))
                for c in range(4):
                    pe.matmul(o[c * PR:(c + 1) * PR, 0:NT], qa[:, b, c, :], TT[:, KA0 + c, r], start=True, stop=True)
                pe.matmul(o[0:64, 8:16], qn[:, 1, b, :], TT[:, KS0, r], start=True, stop=True)
                pe.matmul(o[0:64, 16:24], qn[:, 1, b, :], TT[:, KW0, r], start=True, stop=True).then_inc(s["s_scores"], 1)
                pe.wait_ge(s[f"ld_ka{q}"], 32 * (b // 2 + 1))
                for x in range(2):
                    o = chunk_begin(b, 1 + x)
                    for c in range(4):
                        mm = pe.matmul(o[c * PR:(c + 1) * PR, :], qa[:, b, c, :], ka[:, q, c, x * 512:(x + 1) * 512], start=True, stop=True)
                    mm.then_inc(s["s_scores"], 1)
                o = chunk_begin(b, 3)
                pe.matmul(o[0:64, :], qn[:, 1, b, :], kw[:, q, :], start=True, stop=True).then_inc(s["s_scores"], 1)

            def sel_scores(b):
                q = b % 2
                pe.wait_ge(s[f"ld_pg{q}"], 16 * PAGES * (b // 2 + 1))
                for x in range(2):
                    o = chunk_begin(b, 4 + x)
                    pe.matmul(o[0:64, :], qn[:, 1, b, :], pg[:, q, 4 * x:4 * x + 4, 0, :], start=True, stop=True).then_inc(s["s_scores"], 1)

            def turn(b, n):
                w = 4 * b + n
                pe.wait_ge(s["s_exp"], 3 * b + (1 if n < 2 else 3))
                if w >= 2:
                    pe.wait_ge(s["s_turned_out"], w - 1)
                o = bank(3 + w % 2)
                a, z = sA[:, b % 2, :], sB[:, b % 2, :]
                id64 = ident[0:64, 0:64]
                if n < 2:
                    for j in range(4):
                        mm = pe.transpose(o[:, j * P:(j + 1) * P], a[:, 4 * n + j:PAST:8], ident)
                elif n == 2:
                    for j in range(8):
                        mm = pe.transpose(o[:, j * 64:(j + 1) * 64], z[:, SS + j * P:SS + (j + 1) * P], id64)
                else:
                    for j in range(4):
                        pe.transpose(o[:, j * 64:(j + 1) * 64], z[:, SW + j:SW + 512:4], id64)
                    pe.transpose(o[0:NT, 256:320], z[:, SS + PAST:SS + NKA], id64)
                    pe.transpose(o[0:NT, 320:384], z[:, SW + 512:SW + NKW], id64)
                    mm = pe.transpose(o[0:NT, 384:512], a[:, PAST:NKA], ident)
                mm.then_inc(s["s_turned"], 1)

            def values(b):
                q = b % 2
                pe.wait_ge(s["s_turned_out"], 4 * b + 4)
                pe.wait_ge(s[f"ld_v{q}"], 64 * (b // 2 + 1))
                if b >= 2:
                    pe.wait_ge(s["s_normed"], b - 1)
                o = bank(5 + q)
                for j in range(8):
                    mm = pe.matmul(o[0:64, 2 * P:3 * P], zB[:, q, j, :], pg[:, q, j, 1, :], start=(j == 0), stop=False)
                mm.then_inc(s["s_sel_used"], 1)
                pe.matmul(o[0:64, 2 * P:3 * P], zB[0:NT, q, 12, :], vn[:, q, 512:640], start=False, stop=True)
                pe.matmul(o[0:64, P:2 * P], pcT[:, b, :], t.vc[:, b, :], start=True, stop=True)
                for j in range(4):
                    pe.matmul(o[0:64, 3 * P:4 * P], zB[:, q, 8 + j, :], vw[:, q, j, :], start=(j == 0), stop=False)
                pe.matmul(o[0:64, 3 * P:4 * P], zB[0:NT, q, 13, :], vn[:, q, 640:768], start=False, stop=True)
                for j in range(9):
                    for c in range(4):
                        w, v = (zA[:, q, j, :], va[:, q, j, :]) if j < 8 else (zAn[:, q, :], vn[:, q, 0:512])
                        mm = pe.matmul(o[c * PR:(c + 1) * PR, 0:P], w[:, c * PR:(c + 1) * PR], v[:, c * P:(c + 1) * P], start=(j == 0), stop=(j == 8))
                mm.then_inc(s["s_pv"], 1)

            def turn_out(b):
                pe.wait_ge(s["s_normed"], b + 1)
                if b:
                    pe.wait_ge(s["s_OT"], b)
                pe.transpose(bank(7)[:, 0:P], oA[:, b % 2, :], ident)
                pe.transpose(bank(7)[:, P:P + 64], oB[:, b % 2, :], ident[0:64, 0:64]).then_inc(s["s_out_turned"], 1)

            pe.wait_ge(s["i_sel"], 1)
            for b in range(NB + 2):
                if b < NB:
                    scores(b)
                if 1 <= b <= NB:
                    for n in range(4):
                        turn(b - 1, n)
                if b >= 2:
                    turn_out(b - 2)
                if b < NB:
                    sel_scores(b)
                if 1 <= b <= NB:
                    values(b - 1)

        @block.scalar
        def _(act):
            def p_exp(u):
                n = shape(u)[0]
                act.wait_ge(s["p_max"], u + 1)
                for e in range(2):
                    v = pp[:, u % 4, e, 0:n]
                    ins = act.activation(v, v, ACT.Exp, bias=nm[:, 2 * u + e:2 * u + e + 1], accum_out=sm[:, 2 * u + e:2 * u + e + 1])
                ins.then_inc(s["p_exp"], 1)

            def p_out(u):
                n, nk, kr = shape(u)
                act.wait_ge(s["p_turned"], u + 1)
                if u >= 2:
                    act.wait_ge(s["p_pv"], u - 1)
                src = bank(4 + u % 2)[0:kr, :].rearrange("p (e x q) -> p e x q", e=2, x=2)[:, :, 0:nk, :]
                dst = pT[0:kr, u % 2].rearrange("p (e x) q -> p e x q", e=2)[:, :, 0:nk, :]
                act.activation(dst, src, ACT.Copy).then_inc(s["p_turned_out"], 1)

            def p_OT(u):
                i, c, k = units[u]
                act.wait_ge(s["p_pv"], u + 1)
                act.activation(OT[:, c + (0 if k == "A" else 4), P * i:P * i + P], bank(6 + (k != "A"))[:, 0:P], ACT.Copy).then_inc(s["p_OT"], 1)

            for u in range(NU + 4):
                if u < NU:
                    p_exp(u)
                if 2 <= u < NU + 2:
                    p_out(u - 2)
                if u >= 4 and units[u - 4][2] in ("A", "win"):
                    p_OT(u - 4)
            act.wait_ge(s["i_pc"], 2)
            act.activation(pc[:], pc[:], ACT.Exp).then_inc(s["i_pc"], 1)
            act.wait_ge(s["i_mm"], 2)
            act.activation(pcT[:].rearrange("p b r -> p (b r)"), bank(1)[0:NC_S, :], ACT.Copy).then_inc(s["i_pc"], 1)

            def s_exp(b, n):
                act.wait_ge(s["s_max"], 3 * b + n + 1)
                if n == 0:
                    v, z = sA[:, b % 2, :], stA[:, b, :]
                elif n == 1:
                    v, z = sB[:, b % 2, SW:SW + NKW], stB[:, b, 1, :]
                else:
                    v, z = sB[:, b % 2, SS:SS + NKA], stB[:, b, 0, :]
                act.activation(v, v, ACT.Exp, bias=z[:, 0:1], accum_out=z[:, 1:2]).then_inc(s["s_exp"], 1)

            def s_out(b, n):
                w, q = 4 * b + n, b % 2
                act.wait_ge(s["s_turned"], w + 1)
                if n == 0 and b >= 2:
                    act.wait_ge(s["s_pv"], b - 1)
                o = bank(3 + w % 2)
                if n < 2:
                    ins = act.activation(zA[:, q, 4 * n:4 * n + 4, :].rearrange("p j r -> p (j r)"), o, ACT.Copy)
                elif n == 2:
                    ins = act.activation(zB[:, q, 0:8, :].rearrange("p j r -> p (j r)"), o, ACT.Copy)
                else:
                    act.activation(zB[:, q, 8:12, :].rearrange("p j r -> p (j r)"), o[:, 0:256], ACT.Copy)
                    act.activation(zB[0:NT, q, 12:14, :].rearrange("p j r -> p (j r)"), o[0:NT, 256:384], ACT.Copy)
                    ins = act.activation(zAn[:, q, :], o[0:NT, 384:512], ACT.Copy)
                ins.then_inc(s["s_turned_out"], 1)

            def s_OT(b):
                act.wait_ge(s["s_out_turned"], b + 1)
                r = slice(SEQ + NT * b, SEQ + NT * (b + 1))
                o = bank(7)
                for e in range(2):
                    h = slice(e * HD, (e + 1) * HD)
                    act.activation(OT[h, 0:4, r], o[h, 0:P].rearrange("p (c q) -> p c q", c=4)[:, :, e * NT:(e + 1) * NT], ACT.Copy)
                    ins = act.activation(OT[h, 4:8, r], o[h, P:P + 64].rearrange("p (k g q) -> p k g q", k=KVH, g=G)[:, e], ACT.Copy)
                ins.then_inc(s["s_OT"], 1)

            for b in range(NB + 2):
                if b < NB:
                    s_exp(b, 0)
                if 1 <= b <= NB:
                    for n in range(3):
                        s_out(b - 1, n)
                if b < NB:
                    s_exp(b, 1)
                if 1 <= b <= NB:
                    s_out(b - 1, 3)
                if b >= 2:
                    s_OT(b - 2)
                if b < NB:
                    s_exp(b, 2)

        @block.vector
        def _(ve):
            def sample_queries():
                ve.wait_ge(s["diag_zero"], 4)
                for c in range(4):
                    for e in range(2):
                        h = slice(e * HD, (e + 1) * HD)
                        n = e * NT
                        ve.tensor_copy(qa[h, :, c, n:n + NT], TT[h, QA0 + c, SEQ:ROWS].rearrange("p (b t) -> p b t", t=NT)).then_inc(s["diag"], 1)
                for x, q0 in enumerate((QB0, QR0)):
                    for e in range(2):
                        h = slice(e * HD, (e + 1) * HD)
                        ve.tensor_copy(qn[h, x, :, e * 32:(e + 1) * 32].rearrange("p b (g t) -> p b g t", t=NT),
                                       TT[h, q0:q0 + G, SEQ:ROWS].rearrange("p g (b t) -> p b g t", t=NT)).then_inc(s["diag"], 1)

            ve.wait_ge(s["ca"], 16)
            ve.wait_ge(s["gs"], 16 * 3 * HEADS)

            def p_mask(u):
                i, c, k = units[u]
                n = shape(u)[0]
                ve.wait_ge(s["p_scores"], u + 1)
                if u >= 4:
                    ve.wait_ge(s["p_turned"], u - 3)
                base, w = {"A": (CA_PA, P), "cmp": (CA_PB, NC_P)}.get(k, (CA_PC, P))
                mask = ca[:, base + w * i:base + w * i + n].unsqueeze(1).broadcast_to([P, 2, n])
                v = pp[:, u % 4, :, 0:n]
                ve.scalar_tensor_tensor(v, t.psum[:, 2 * (u % 2):2 * (u % 2) + 2, 0:n], SCALE, mask, ALU.mult, ALU.add)\
                  .then_inc(s["p_masked"], 1)
                ve.wait_ge(s["p_masked"], u + 1)
                z = nm[:, 2 * u:2 * u + 2]
                if k != "cmp":
                    ve.tensor_reduce(z, v, AX.X, ALU.max, negate=True).then_inc(s["p_max"], 1)
                else:
                    j = (u // 4) + 1
                    ve.tensor_reduce(z, v, AX.X, ALU.max, negate=True).then_inc(s["p_cmax"], 1)
                    ve.wait_ge(s["p_cmax"], j)
                    ve.tensor_scalar(z, z, -NEG * 0.1, None, ALU.min).then_inc(s["p_max"], 1)

            def p_weigh(u):
                i, c, k = units[u]
                n = shape(u)[0]
                ve.wait_ge(s["p_exp"], u + 1)
                zs, z = sm[:, 2 * u:2 * u + 2], rs[:, 2 * u:2 * u + 2]
                if k == "cmp":
                    ve.tensor_scalar(zs, zs, TINY, None, ALU.max).then_inc(s["p_csum"], 1)
                    ve.wait_ge(s["p_csum"], u // 4 + 1)
                ve.reciprocal(z, zs).then_inc(s["p_rec"], 1)
                if k != "A":
                    br = KINDS.index(k) - 1
                    gate = t.gates[:, i, br * HEADS:(br + 1) * HEADS].rearrange("p (k g) -> p k g", k=KVH)[:, :, c]
                    ve.wait_ge(s["p_rec"], u + 1)
                    ve.tensor_tensor(z, z, gate, ALU.mult).then_inc(s["p_fac"], 1)
                    ve.wait_ge(s["p_fac"], u - u // 4)
                else:
                    ve.wait_ge(s["p_rec"], u + 1)
                for e in range(2):
                    v = pp[:, u % 4, e, 0:n]
                    ins = ve.tensor_scalar(v, v, rs[:, 2 * u + e:2 * u + e + 1], None, ALU.mult)
                ins.then_inc(s["p_weighed"], 1)

            for u in range(NU + 1):
                if u < NU:
                    p_mask(u)
                if u == 8:
                    sample_queries()
                if u >= 1:
                    p_weigh(u - 1)
            ve.wait_ge(s["p_pv"], NU)
            over = lambda z: z.unsqueeze(2).broadcast_to([64, NB, NC_S])
            ve.wait_ge(s["i_mm"], 1)
            ve.tensor_scalar(pc[:].rearrange("p b n -> p (b n)"), bank(0)[0:64, 0:NB * NC_S], SCALE, None, ALU.mult).then_inc(s["i_dve"], 1)
            ve.wait_ge(s["i_dve"], 1)
            ve.tensor_reduce(cst[:, 0], pc[:], AX.X, ALU.max, negate=True).then_inc(s["i_pc"], 1)
            ve.wait_ge(s["i_pc"], 1)
            ve.tensor_tensor(pc[:], pc[:], over(cst[:, 0]), ALU.add).then_inc(s["i_pc"], 1)
            ve.wait_ge(s["i_pc"], 3)
            ve.tensor_reduce(cst[:, 1], pc[:], AX.X, ALU.add).then_inc(s["i_dve"], 1)
            ve.wait_ge(s["i_dve"], 2)
            ve.reciprocal(cst[:, 1], cst[:, 1]).then_inc(s["i_dve"], 1)
            ve.wait_ge(s["i_dve"], 3)
            ve.tensor_tensor(pc[:], pc[:], over(cst[:, 1]), ALU.mult).then_inc(s["i_pc"], 1)
            ve.wait_ge(s["i_mm"], 3)
            ve.tensor_copy(x1[:], bank(2)[0:64, 0:NB * NSEL]).then_inc(s["i_pc"], 1)
            ve.wait_ge(s["i_mm"], 4)
            ve.tensor_scalar(imp[:], bank(7)[0:64, 0:NB * NSEL].rearrange("p (b j) -> p b j", j=NSEL)[:, :, 14:0:-1], -1.0, None, ALU.mult).then_inc(s["i_sel"], 1)
            ve.wait_ge(s["i_sel"], 1)
            for b in range(NB):
                ve.max(top[:, b], imp[:, b]).then_inc(s["i_sel"], 1)
            ve.wait_ge(s["i_sel"], 1 + NB)
            for b in range(NB):
                ve.max_index(tix[:, b], top[:, b], imp[:, b]).then_inc(s["i_sel"], 1)
            ve.wait_ge(s["i_sel"], 1 + 2 * NB)
            ve.tensor_copy(tif[:], tix[:, :, 0]).then_inc(s["i_sel"], 1)
            ve.wait_ge(s["i_sel"], 2 + 2 * NB)
            ve.tensor_tensor(pen[:, :, 1:15], ca[0:64, CA_RV:CA_RV + 14].unsqueeze(1).broadcast_to([64, NB, 14]),
                             tif[:].unsqueeze(2).broadcast_to([64, NB, 14]), ALU.is_equal).then_inc(s["i_sel"], 1)
            ve.wait_ge(s["i_sel"], 3 + 2 * NB)
            ve.tensor_scalar(pen[:, :, 1:15], pen[:, :, 1:15], NEG, None, ALU.mult).then_inc(s["i_pen"], 1)
            ve.wait_ge(s["i_pen"], 1)

            read = lambda ins: ins.then_inc(s["s_read"], 1)

            def masked(b, n, dst, bk0, w, mask):
                r = dst.shape[0]
                return ve.scalar_tensor_tensor(dst, bank(chunk(b, n) % 3)[0:r, bk0:bk0 + w], SCALE, mask, ALU.mult, ALU.add)

            def negmax(b, n):
                ve.wait_ge(s["s_read"], chunk(b, [2, 3, 5][n]) + 1)
                v, z = [(sA[:, b % 2, :], stA[:, b, 0:1]), (sB[:, b % 2, SW:SW + NKW], stB[:, b, 1, 0:1]),
                        (sB[:, b % 2, SS:SS + NKA], stB[:, b, 0, 0:1])][n]
                ve.tensor_reduce(z, v, AX.X, ALU.max, negate=True).then_inc(s["s_max"], 1)

            def normed(b):
                q = b % 2
                ve.wait_ge(s["s_exp"], 3 * b + 3)
                ve.reciprocal(stA[:, b, 2:3], stA[:, b, 1:2])
                ve.reciprocal(stB[:, b, :, 2], stB[:, b, :, 1]).then_inc(s["s_rec"], 1)
                ve.wait_ge(s["s_rec"], b + 1)
                ve.tensor_tensor(stB[:, b, :, 3], stB[:, b, :, 2], gs[:, b, 1:3], ALU.mult).then_inc(s["s_fac"], 1)
                ve.wait_ge(s["s_fac"], b + 1)
                ve.wait_ge(s["s_pv"], b + 1)
                if b >= 2:
                    ve.wait_ge(s["s_out_turned"], b - 1)
                o, z = bank(5 + q), oB[:, q, :]
                ve.tensor_scalar(z, o[0:64, P:2 * P], gs[:, b, 0:1], None, ALU.mult).then_inc(s["s_branch"], 1)
                ve.tensor_scalar(oA[:, q, :], o[:, 0:P], stA[:, b, 2:3], None, ALU.mult)
                ve.wait_ge(s["s_branch"], 2 * b + 1)
                ve.scalar_tensor_tensor(z, o[0:64, 2 * P:3 * P], stB[:, b, 0, 3:4], z, ALU.mult, ALU.add).then_inc(s["s_branch"], 1)
                ve.wait_ge(s["s_branch"], 2 * b + 2)
                ve.scalar_tensor_tensor(z, o[0:64, 3 * P:4 * P], stB[:, b, 1, 3:4], z, ALU.mult, ALU.add).then_inc(s["s_normed"], 1)

            for b in range(NB):
                a, z = sA[:, b % 2, :], sB[:, b % 2, :]
                ve.wait_ge(s["s_scores"], chunk(b, 0) + 1)
                if b >= 2:
                    ve.wait_ge(s["s_turned"], 4 * (b - 1))
                masked(b, 0, a[:, PAST:NKA], 0, NT, ca[:, CA_SA + PAST:CA_SA + NKA])
                masked(b, 0, z[:, SS + PAST:SS + NKA], 8, NT, ca[0:64, CA_SN:CA_SN + NT])
                read(masked(b, 0, z[:, SW + 512:SW + NKW], 16, NT, ca[0:64, CA_SW + 512:CA_SW + NKW]))
                for x in range(2):
                    ve.wait_ge(s["s_scores"], chunk(b, 1 + x) + 1)
                    c = slice(512 * x, 512 * (x + 1))
                    read(masked(b, 1 + x, a[:, c], 0, 512, ca[:, CA_SA + 512 * x:CA_SA + 512 * (x + 1)]))
                negmax(b, 0)
                ve.wait_ge(s["s_scores"], chunk(b, 3) + 1)
                read(masked(b, 3, z[:, SW:SW + 512], 0, 512, ca[0:64, CA_SW:CA_SW + 512]))
                negmax(b, 1)
                if b >= 2:
                    normed(b - 2)
                for x in range(2):
                    ve.wait_ge(s["s_scores"], chunk(b, 4 + x) + 1)
                    m = pen[:, b, 8 * x:8 * x + 8].unsqueeze(2).broadcast_to([64, 8, 64])
                    read(ve.scalar_tensor_tensor(z[:, SS + 512 * x:SS + 512 * (x + 1)].rearrange("p (j n) -> p j n", n=64),
                                                 bank(chunk(b, 4 + x) % 3)[0:64].rearrange("p (j n) -> p j n", n=64), SCALE, m, ALU.mult, ALU.add))
                negmax(b, 2)
            normed(NB - 2)
            normed(NB - 1)


NH = 8
HH = 2 * NH
TOPK = 16
PAIRS = [TOPK // (a + 1) for a in range(8)]
POFF = [sum(PAIRS[:a]) for a in range(9)]
NPAIR = POFF[8] + 8
HU = 2 * NH + NH // 2
LOW = -3e38


class Norm:

    def __init__(self, s, first, x, psum, y, lnp, bn, mv):
        self.s, self.first, self.x, self.psum, self.y, self.lnp, self.bn, self.mv = s, first, x, psum, y, lnp, bn, mv

    def moments(self, ve, i):
        s, T, r = self.s, self.first + i, RT[i]
        x, y, bn, mv = self.x(i), self.y(i), self.bn, self.mv
        for h in range(2):
            c = slice(512 * h, 512 * (h + 1))
            ve.scalar_tensor_tensor(y[:, c], x[:, c], ALPHA, self.psum(i, h), ALU.mult, ALU.add).then_inc(s["ln_sum"], 1)
        for h in range(2):
            ve.wait_ge(s["ln_sum"], 2 * T + h + 1)
            if h == 0 and T:
                ve.wait_ge(s["ln_mean"], T)
            ve.bn_stats(bn[0:r, 6 * h:6 * h + 6], y[:, 512 * h:512 * (h + 1)]).then_inc(s["ln_st"], 1)
        ve.wait_ge(s["ln_st"], 2 * T + 2)
        ve.bn_aggr(mv[0:r, i, 0:2], bn[0:r, :]).then_inc(s["ln_mean"], 1)
        ve.wait_ge(s["ln_mean"], T + 1)
        ve.tensor_scalar(mv[0:r, i, 2:3], mv[0:r, i, 1:2], EPS, None, ALU.add).then_inc(s["ln_var"], 1)

    def root(self, act, i):
        act.wait_ge(self.s["ln_var"], self.first + i + 1)
        z = self.mv[0:RT[i], i, 2:3]
        act.activation(z, z, ACT.Sqrt).then_inc(self.s["ln_root"], 1)

    def factors(self, ve, i):
        s, T, mv = self.s, self.first + i, self.mv[0:RT[i], i, :]
        ve.wait_ge(s["ln_root"], T + 1)
        ve.reciprocal(mv[:, 2:3], mv[:, 2:3]).then_inc(s["ln_fac"], 1)
        ve.wait_ge(s["ln_fac"], 2 * T + 1)
        ve.scalar_tensor_tensor(mv[:, 3:4], mv[:, 0:1], -1.0, mv[:, 2:3], ALU.mult, ALU.mult).then_inc(s["ln_fac"], 1)

    def scale(self, act, i):
        act.wait_ge(self.s["ln_fac"], 2 * (self.first + i + 1))
        mv = self.mv[0:RT[i], i, :]
        act.activation(self.y(i), self.y(i), ACT.Identity, scale=mv[:, 2:3], bias=mv[:, 3:4]).then_inc(self.s["ln_scaled"], 1)

    def gain(self, eng, i, h):
        s, T, r, c = self.s, self.first + i, RT[i], slice(512 * h, 512 * (h + 1))
        mid, end = [("ln_lg", "ln_l"), ("ln_rg", "ln_r")][h]
        y = self.y(i)[:, c]
        eng.wait_ge(s["ln_scaled"], T + 1)
        if T and h:
            eng.wait_ge(s[end], T)
        eng.tensor_tensor(y, y, self.lnp[0:r, 0, c], ALU.mult).then_inc(s[mid], 1)
        eng.wait_ge(s[mid], T + 1)
        eng.tensor_tensor(y, y, self.lnp[0:r, 1, c], ALU.add).then_inc(s[end], 1)


def route_block(nc, d, t, s):
    with ExitStack() as ctx:
        sb = lambda n, sh, dt=F32: ctx.enter_context(nc.sbuf_tensor(n, sh, dt))
        wo = t.big[:].rearrange("p (k n) -> p k n", k=KD)
        xr = sb("x_rows", [P, TILES, D])
        ln = sb("ln1", [P, 2, D])
        wq = sb("wq_ring", [P, 4, KD, P])
        ky = sb("peer_keys", [P, HH, P])
        qT = sb("peer_q", [P, HH, ROWS])
        xT = sb("x1T", [P, KD, ROWS])
        sc = sb("peer_scores", [P, 3, 4, P])
        sc2 = sb("peer_scores2", [P, 4, P])
        v = sb("top_vals", [P, 2, 4, TOPK])
        ix = sb("top_idx", [P, 2, 4, TOPK], U32)
        ixf = sb("top_idxf", [P, 2, 4, TOPK])
        i128 = sb("top_idx128", [P, 2, 2, TOPK])
        cv = sb("pair_vals", [P, 2, NPAIR])
        cv2 = sb("pair_vals2", [P, 2, NPAIR])
        ci = sb("pair_ids", [P, 2, 2, NPAIR])
        bi = sb("best_idx", [P, 2, TOPK], U32)
        bf = sb("best_idxf", [P, 2, TOPK], BF16)
        eq = sb("best_onehot", [P, 2, 2, NPAIR, TOPK], BF16)
        pi = sb("onehot_ids", [P, 2, 2, NPAIR, TOPK])
        iop = sb("iota_wide", [P, NPAIR, TOPK], BF16)
        bv = sb("best_vals", [P, HU, TOPK])
        ids = sb("expert_ids", [P, HU, TOPK])
        den = sb("gate_sum", [P, 2, HU])
        cT = sb("ids_turned", [P, ROWS])
        gT = sb("gates_turned", [P, ROWS])
        ii = sb("ids_int", [P, 2, ROWS], I32)
        gr = sb("gate_rest", [P, 2, ROWS])
        bn = sb("ln1_bn", [P, 12])
        mv = sb("ln1_mv", [P, TILES, 4])
        io = sb("iota_pairs", [P, NPAIR])
        block = ctx.enter_context(nc.Block())
        OT, x1, ident = t.OT, t.x1, t.c0[:, 0:P]
        bank = lambda i: t.psum[:, i]
        norm = Norm(s, 0, lambda i: xr[0:RT[i], i, :], lambda i, h: bank(2 * i + h)[0:RT[i], :], lambda i: x1[0:RT[i], i, :], ln, bn, mv)
        by_group = [[(0, 0), (1, 0)], [(0, 1), (1, 1)], [(0, 2), (1, 2), (2, 0)], [(0, 3), (1, 3), (2, 1)]]
        units = [x for g in by_group for x in g]
        head = lambda u: 8 * units[u][0] + 2 * units[u][1]

        @block.sync
        def _(sp):
            for i in range(TILES):
                sp.dma_start(xr[0:RT[i], i, :], d.x_rows[P * i:P * i + RT[i], :]).then_inc(s["ld_xr"], 16)
            sp.dma_start(ln[:, 0, :], d.ln1_g.partition_broadcast(P)).then_inc(s["ld_xr"], 16)
            sp.dma_start(ln[:, 1, :], d.ln1_b.partition_broadcast(P)).then_inc(s["ld_xr"], 16)
            sp.dma_start(io[:], d.iota_pairs).then_inc(s["ld_ky"], 16)
            sp.dma_start(ky[:], d.peer_keys).then_inc(s["ld_ky"], 16)
            for j in range(HH):
                if j >= 4:
                    sp.wait_ge(s["q_mm"], j - 3)
                sp.dma_start(wq[:, j % 4], d.peer_wq[j]).then_inc(s[f"ld_wq{j % 4}"], 16)
            for m in range(2):
                sp.dma_start(t.big[:, m * D:(m + 1) * D], d.peer_u[m]).then_inc(s[f"ld_u{m}"], 16)
                sp.dma_start(t.big[:, (2 + m) * D:(3 + m) * D], d.peer_v[m]).then_inc(s[f"ld_v2{m}"], 16)
            sp.dma_start(t.big[:, BIG_IOTA:BIG_IOTA + P], d.iota).then_inc(s["iota_in"], 16)
            sp.dma_start(t.big[:, 4 * D:5 * D], d.ln2_g.partition_broadcast(P)).then_inc(s["ld_ln2"], 16)
            sp.dma_start(t.big[:, 5 * D:6 * D], d.ln2_b.partition_broadcast(P)).then_inc(s["ld_ln2"], 16)

        @block.tensor
        def _(pe):
            for i in range(TILES):
                r = slice(P * i, P * i + RT[i])
                for h in range(2):
                    for k in range(KD):
                        if i == 0 and h == 0 and k % 4 == 0:
                            pe.wait_ge(s[f"ld_wo{k // 4}"], 32)
                        mm = pe.matmul(bank(2 * i + h)[0:RT[i], :], OT[:, k, r], wo[:, k, 512 * h:512 * (h + 1)],
                                       start=(k == 0), stop=(k == KD - 1))
                mm.then_inc(s["o_mm"], 1)
            for x in range(2 * TILES):
                i = x // 2
                pe.wait_ge(s["ln_r" if x % 2 else "ln_l"], i + 1)
                if x >= 2:
                    pe.wait_ge(s["x_out"], x - 1)
                for y in range(4):
                    k = 4 * (x % 2) + y
                    mm = pe.transpose(bank(6 + x % 2)[:, y * P:y * P + RT[i]], x1[0:RT[i], i, k * P:(k + 1) * P], ident[0:RT[i], 0:RT[i]])
                mm.then_inc(s["x_turn"], 1)
            pe.wait_ge(s["x_out"], 6)
            pe.wait_ge(s["ld_ky"], 32)
            for g in range(4):
                for j in range(4 * g, 4 * g + 4):
                    pe.wait_ge(s[f"ld_wq{j % 4}"], 16 * (j // 4 + 1))
                    if j >= 2:
                        pe.wait_ge(s["q_out"], j - 1)
                    for k in range(KD):
                        mm = pe.matmul(bank(j % 2)[:, 0:ROWS], wq[:, j % 4, k, :], xT[:, k, :], start=(k == 0), stop=(k == KD - 1))
                    mm.then_inc(s["q_mm"], 1)
                pe.wait_ge(s["q_out"], 4 * g + 4)
                for i, l in by_group[g]:
                    u = units.index((i, l))
                    if u >= 2:
                        pe.wait_ge(s["sc_out"], u - 1)
                    for j in range(4):
                        for r0, q in ([(0, 4 * l + j)] if i < 2 else [(0, 4 * l + j), (64, 4 * l + 8 + j)]):
                            mm = pe.matmul(bank(2 + u % 2)[r0:r0 + RT[i], j * P:(j + 1) * P], qT[:, q, P * i:P * i + RT[i]], ky[:, q, :],
                                           start=True, stop=True)
                    mm.then_inc(s["sc_mm"], 1)
            pe.wait_ge(s["id_sum"], len(units))
            pe.wait_ge(s["g_fin"], 1)
            for i in range(TILES):
                h = slice(8 * i, min(8 * i + 8, HU))
                n = 16 * (h.stop - h.start)
                pe.transpose(bank(4 + i)[0:n, 0:P], ids[:, h].rearrange("p h k -> p (h k)"), ident)
                pe.transpose(bank(4 + i)[0:n, P:2 * P], bv[:, h].rearrange("p h k -> p (h k)"), ident).then_inc(s["id_turn"], 1)

        @block.scalar
        def _(act):
            for i in range(TILES):
                norm.root(act, i)
                norm.scale(act, i)
            for x in range(2 * TILES):
                i, c = x // 2, 4 * (x % 2)
                act.wait_ge(s["x_turn"], x + 1)
                act.activation(xT[:, c:c + 4, P * i:P * i + RT[i]], bank(6 + x % 2).rearrange("p (c q) -> p c q", q=P)[:, :, 0:RT[i]],
                               ACT.Copy).then_inc(s["x_out"], 1)
            act.wait_ge(s["x_out"], 6)
            for g in range(4):
                for j in range(4 * g, 4 * g + 4):
                    act.wait_ge(s["q_mm"], j + 1)
                    act.activation(qT[:, j, :], bank(j % 2)[:, 0:ROWS], ACT.Copy).then_inc(s["q_out"], 1)
                for x in by_group[g]:
                    u = units.index(x)
                    act.wait_ge(s["sc_mm"], u + 1)
                    if u >= 3:
                        act.wait_ge(s["top2"], 4 * (u - 2))
                    act.activation(sc[:, u % 3], bank(2 + u % 2).rearrange("p (j n) -> p j n", n=P), ACT.Copy).then_inc(s["sc_out"], 1)
                if g == 0:
                    act.activation(t.x1h[:], xT[:], ACT.Copy).then_inc(s["x_hi"], 1)
            act.wait_ge(s["g_sub"], 1)
            act.activation(bv[:], bv[:], ACT.Exp).then_inc(s["g_exp"], 1)

        @block.gpsimd
        def _(gp):
            gp.wait_ge(s["ld_xr"], 80)
            for i in range(TILES):
                norm.gain(gp, i, 1)
            gp.wait_ge(s["ln_r"], TILES)
            for u in range(len(units)):
                q = u % 2
                y = v[:, q].rearrange("p (h e) k -> p h e k", e=2)
                gp.wait_ge(s["top2"], 4 * (u + 1))
                if u:
                    gp.wait_ge(s["bei"], 2 * u)
                for a in range(8):
                    n, o = PAIRS[a], POFF[a]
                    gp.tensor_tensor(cv[:, :, o:o + n], y[:, :, 1, 0:n], y[:, :, 0, a].unsqueeze(2).broadcast_to([P, 2, n]), ALU.add)
                gp.tensor_tensor(cv[:, :, POFF[8]:NPAIR], y[:, :, 0, 8:16], y[:, :, 1, 0].unsqueeze(2).broadcast_to([P, 2, 8]), ALU.add)\
                  .then_inc(s["pair_v"], 1)
                z = ixf[:, q].rearrange("p (h e) k -> p h e k", e=2)
                gp.wait_ge(s["ixf"], u + 1)
                if u >= 2:
                    gp.wait_ge(s["id_mul"], u - 1)
                gp.tensor_scalar(i128[:, q], z[:, :, 0, :], float(P), None, ALU.mult).then_inc(s["pr128"], 1)
                gp.wait_ge(s["pr128"], u + 1)
                for a in range(8):
                    n, o = PAIRS[a], POFF[a]
                    gp.tensor_tensor(ci[:, q, :, o:o + n], z[:, :, 1, 0:n], i128[:, q, :, a].unsqueeze(2).broadcast_to([P, 2, n]), ALU.add)
                gp.tensor_tensor(ci[:, q, :, POFF[8]:NPAIR], i128[:, q, :, 8:16], z[:, :, 1, 0].unsqueeze(2).broadcast_to([P, 2, 8]), ALU.add)\
                  .then_inc(s["pair"], 1)
                gp.wait_ge(s["pair"], u + 1)
                gp.wait_ge(s["id_eq"], u + 1)
                if u >= 2:
                    gp.wait_ge(s["id_sum"], u - 1)
                gp.tensor_tensor(pi[:, q], eq[:, q], ci[:, q].unsqueeze(3).broadcast_to([P, 2, NPAIR, TOPK]), ALU.mult).then_inc(s["id_mul"], 1)
                if u == 0:
                    gp.wait_ge(s["x_hi"], 1)
                    gp.tensor_tensor(t.x1l[:], xT[:], t.x1h[:].bitcast(F32), ALU.subtract).then_inc(s["x_lo"], 1)

        @block.vector
        def _(ve):
            ve.wait_ge(s["ld_ky"], 32)
            ve.tensor_copy(iop[:], io[:].unsqueeze(2).broadcast_to([P, NPAIR, TOPK])).then_inc(s["g_den"], 1)
            ve.wait_ge(s["g_den"], 1)
            ve.wait_ge(s["ld_xr"], 80)
            for i in range(TILES):
                r = RT[i]
                ve.wait_ge(s["o_mm"], i + 1)
                norm.moments(ve, i)
                norm.factors(ve, i)
                norm.gain(ve, i, 0)
            def top16(n, base, src, src2, vals, idxs, names):
                a, b, c = names
                for j in range(n):
                    ve.max(vals(j)[:, 0:8], src(j)).then_inc(s[a], 1)
                ve.wait_ge(s[a], base + n)
                for j in range(n):
                    ve.max_index(idxs(j)[:, 0:8], vals(j)[:, 0:8], src(j))
                    ve.match_replace(src2(j), vals(j)[:, 0:8], src(j), LOW).then_inc(s[b], 1)
                ve.wait_ge(s[b], base + n)
                for j in range(n):
                    ve.max(vals(j)[:, 8:16], src2(j)).then_inc(s[a + "b"], 1)
                ve.wait_ge(s[a + "b"], base + n)
                for j in range(n):
                    ve.max_index(idxs(j)[:, 8:16], vals(j)[:, 8:16], src2(j)).then_inc(s[c], 1)

            def ids_of(u):
                ve.wait_ge(s["id_mul"], u + 1)
                ve.tensor_reduce(ids[:, head(u):head(u) + 2], pi[:, u % 2].rearrange("p h n k -> p h k n"), AX.X, ALU.add).then_inc(s["id_sum"], 1)

            for u in range(len(units)):
                q = u % 2
                ve.wait_ge(s["sc_out"], u + 1)
                if u >= 2:
                    ve.wait_ge(s["pair_v"], u - 1)
                    ve.wait_ge(s["pair"], u - 1)
                top16(4, 4 * u, lambda j: sc[:, u % 3, j], lambda j: sc2[:, j], lambda j: v[:, q, j], lambda j: ix[:, q, j],
                      ("top", "topr", "top2"))
                ve.wait_ge(s["top2"], 4 * (u + 1))
                ve.tensor_copy(ixf[:, q], ix[:, q]).then_inc(s["ixf"], 1)
                if u:
                    ids_of(u - 1)
                ve.wait_ge(s["pair_v"], u + 1)
                top16(2, 2 * u, lambda j: cv[:, j], lambda j: cv2[:, j], lambda j: bv[:, head(u) + j], lambda j: bi[:, j], ("be", "ber", "bei"))
                ve.wait_ge(s["bei"], 2 * (u + 1))
                if u:
                    ve.wait_ge(s["id_eq"], u)
                ve.tensor_copy(bf[:], bi[:]).then_inc(s["bf"], 1)
                ve.wait_ge(s["bf"], u + 1)
                if u >= 2:
                    ve.wait_ge(s["id_mul"], u - 1)
                ve.tensor_tensor(eq[:, q], iop[:].unsqueeze(1).broadcast_to([P, 2, NPAIR, TOPK]),
                                 bf[:].unsqueeze(2).broadcast_to([P, 2, NPAIR, TOPK]), ALU.is_equal).then_inc(s["id_eq"], 1)
            over = lambda z: z.unsqueeze(2).broadcast_to([P, HU, TOPK])
            ve.tensor_copy(den[:, 1], bv[:, :, 0]).then_inc(s["g_den"], 1)
            ve.wait_ge(s["g_den"], 2)
            ve.tensor_tensor(bv[:], bv[:], over(den[:, 1]), ALU.subtract).then_inc(s["g_sub"], 1)
            ve.wait_ge(s["g_exp"], 1)
            ve.tensor_reduce(den[:, 0], bv[:], AX.X, ALU.add).then_inc(s["g_den"], 1)
            ve.wait_ge(s["g_den"], 3)
            ve.reciprocal(den[:, 0], den[:, 0]).then_inc(s["g_den"], 1)
            ve.wait_ge(s["g_den"], 4)
            ve.tensor_tensor(bv[:], bv[:], over(den[:, 0]), ALU.mult).then_inc(s["g_fin"], 1)
            ids_of(len(units) - 1)
            for i in range(TILES):
                r = slice(P * i, P * i + RT[i])
                ve.wait_ge(s["id_turn"], i + 1)
                for x, dst in enumerate((cT, gT)):
                    o = bank(4 + i)[:, x * P:(x + 1) * P]
                    if i < 2:
                        ins = ve.tensor_copy(dst[:, r], o)
                    else:
                        ve.tensor_copy(dst[0:64, r], o[0:64, 0:64])
                        ins = ve.tensor_copy(dst[64:P, r], o[0:64, 64:P])
                ins.then_inc(s["id_out"], 1)
            step = [0]

            def after(ins):
                step[0] += 1
                ins.then_inc(s["split"], 1)
                ve.wait_ge(s["split"], step[0])

            ve.wait_ge(s["id_out"], 3)
            after(ve.tensor_copy(ii[:, 0, :], cT[:]))
            after(ve.tensor_scalar(ii[:, 1, :], ii[:, 0, :], 7, None, ALU.logical_shift_right))
            after(ve.tensor_copy(t.i1[:], ii[:, 1, :]))
            after(ve.tensor_scalar(ii[:, 1, :], ii[:, 0, :], P - 1, None, ALU.bitwise_and))
            for g in range(SEGS):
                ve.tensor_scalar(t.i2[:, g, :], ii[:, 1, :], float(-g * SEGW), None, ALU.add)
            after(ve.tensor_copy(t.gp[:, 0, :], gT[:]))
            after(ve.tensor_tensor(gr[:, 0, :], gT[:], t.gp[:, 0, :], ALU.subtract))
            after(ve.tensor_copy(t.gp[:, 1, :], gr[:, 0, :]))
            after(ve.tensor_tensor(gr[:, 1, :], gr[:, 0, :], t.gp[:, 1, :], ALU.subtract))
            after(ve.tensor_copy(t.gp[:, 2, :], gr[:, 1, :]))


SEGS, SEGW = 4, 32
NE = 128
GT = ROWS // SEGW
HWC = TILES * P
assert ROWS + RT[2] == HWC
BIG_IOTA = 6 * D + 2 * ROWS
UN = 4


def expert_block(nc, d, t, s):
    with ExitStack() as ctx:
        sb = lambda n, sh, dt=F32: ctx.enter_context(nc.sbuf_tensor(n, sh, dt))
        W = sb("gate_matrix", [P, 2, SEGW, ROWS])
        us = t.big[:, 0:2 * D].rearrange("p (s n) -> p s n", s=2)
        vs = t.big[:, 2 * D:4 * D].rearrange("p (s n) -> p s n", s=2)
        ln = t.big[:, 4 * D:6 * D].rearrange("p (s n) -> p s n", s=2)
        uh, ul = sb("u_hi", [P, 2, D], F32R), sb("u_lo", [P, 2, D], F32R)
        vh, vl = sb("v_hi", [P, 2, D], F32R), sb("v_lo", [P, 2, D], F32R)
        hg = t.big[:, 6 * D:6 * D + ROWS]
        hw = t.big[:, 6 * D + ROWS:6 * D + 2 * ROWS]
        hwh, hwl = sb("gated_hi", [P, 2, HWC], F32R), sb("gated_lo", [P, 2, SEQ], F32R)
        A = sb("onehot_i1", [P, 2, P, GT], BF16)
        E = sb("onehot_i2", [P, 2, SEGW, GT], BF16)
        B = sb("gated_i2", [P, 2, 3, SEGW, GT], BF16)
        o = BIG_IOTA
        iof = t.big[:, o:o + P]
        io = t.big[:, o + P:o + P + P * GT // 2].bitcast(BF16).rearrange("p (i r) -> p i r", r=GT)
        bn = sb("ln2_bn", [P, 12])
        mv = sb("ln2_mv", [P, TILES, 4])
        block = ctx.enter_context(nc.Block())
        bank = lambda i: t.psum[:, i]
        H, WP = bank(6), bank(7)
        x1 = lambda i: t.x1[0:RT[i], i, :]
        norm = Norm(s, TILES, x1, lambda i, h: bank(2 * i + h)[0:RT[i], :], x1, ln, bn, mv)
        x1h, x1l = t.x1h, t.x1l

        @block.sync
        def _(sp):
            with sp.Fori(0, NE // 2 - 1) as i:
                for m in range(2):
                    sp.wait_ge(s["u_lo"], i * 2 + (m + 1))
                    sp.dma_start(us[:, m], d.peer_u[bass.ds(i * 2 + (m + 2), 1)].rearrange("a p n -> p (a n)")).then_inc(s[f"ld_u{m}"], 16)
                    sp.wait_ge(s["v_lo"], i * 2 + (m + 1))
                    sp.dma_start(vs[:, m], d.peer_v[bass.ds(i * 2 + (m + 2), 1)].rearrange("a p n -> p (a n)")).then_inc(s[f"ld_v2{m}"], 16)
            for i in range(TILES):
                for h, done in enumerate(("ln_l", "ln_r")):
                    c = slice(512 * h, 512 * (h + 1))
                    sp.wait_ge(s[done], TILES + i + 1)
                    sp.dma_start(d.o_y[P * i:P * i + RT[i], c], x1(i)[:, c]).then_inc(s["st_y"], 16)
            sp.wait_ge(s["st_y"], 96)

        def segments(eng, body, last):
            for g in range(SEGS):
                with eng.Fori(0, SEGW // UN - (g == SEGS - 1)) as i:
                    for k in range(UN):
                        body(g, i * UN + (SEGW * g + k), i * UN + k, k)
            for k in range(UN):
                last(NE - UN + k, SEGW - UN + k, k)

        @block.tensor
        def _(pe):
            pe.sem_inc(s["c_mm"], 2)
            pe.sem_inc(s["y_mm"], 1)

            def product1(n, q):
                pe.wait_ge(s["u_lo"], n + 1)
                pe.wait_ge(s["gelu"], n)
                for k in range(KD):
                    kc = slice(k * P, (k + 1) * P)
                    pe.matmul(H[:, 0:ROWS], uh[:, q, kc], x1h[:, k, :], start=(k == 0), stop=False)
                    pe.matmul(H[:, 0:ROWS], uh[:, q, kc], x1l[:, k, :], start=False, stop=False)
                    mm = pe.matmul(H[:, 0:ROWS], ul[:, q, kc], x1h[:, k, :], start=False, stop=(k == KD - 1))
                mm.then_inc(s["h_mm"], 1)

            def product2(n, q, stop):
                pe.wait_ge(s["hw_lo"], n + 2)
                pe.wait_ge(s["v_lo"], n + 1)
                for i in range(TILES):
                    r = slice(i * P, (i + 1) * P)
                    pairs = ((hwh, vh), (hwh, vl), (hwl, vh))[0:3 if i < 2 else 2]
                    for x, (a, b) in enumerate(pairs):
                        for h in range(2):
                            mm = pe.matmul(bank(2 * i + h), a[:, q, r], b[:, q, 512 * h:512 * (h + 1)], start=False,
                                           stop=stop and x == len(pairs) - 1, skip_group_check=True)
                    if stop:
                        mm.then_inc(s["y_done"], 1)
                if not stop:
                    mm.then_inc(s["y_mm"], 1)

            def gate_rows(c, q):
                pe.wait_ge(s["onehot"], c + 1)
                pe.wait_ge(s["W_out"], c + 1)
                for r in range(GT):
                    for x in range(3):
                        mm = pe.matmul(WP[:, r * SEGW:(r + 1) * SEGW], A[:, q, :, r], B[:, q, x, :, r], start=(x == 0), stop=(x == 2))
                mm.then_inc(s["c_mm"], 1)

            pe.wait_ge(s["zero"], 2)
            for i in range(2 * TILES):
                mm = pe.matmul(bank(i), hwh[:, 1, 0:P], vh[:, 1, 0:512], start=True, stop=False, skip_group_check=True)
            mm.then_inc(s["y_mm"], 1)
            with pe.Fori(0, SEGW // 2) as i:
                for q in range(2):
                    pe.wait_ge(s["onehot_12"], i * 2 + (q + 1))
                    gate_rows(i * 2 + q, q)
            product1(0, 0)

            def body(g, n, j, k):
                product1(n + 1, (k + 1) % 2)
                if g < SEGS - 1:
                    gate_rows(n + SEGW, k % 2)
                product2(n, k % 2, False)

            def last(n, j, k):
                if k < UN - 1:
                    product1(n + 1, (k + 1) % 2)
                product2(n, k % 2, k == UN - 1)

            segments(pe, body, last)

        @block.scalar
        def _(act):
            def u_hi(n, q, w):
                act.wait_ge(s[f"ld_u{q}"], w)
                act.activation(uh[:, q], us[:, q], ACT.Copy).then_inc(s["u_hi"], 1)

            def W_out(c, seg, g):
                act.wait_ge(s["c_mm"], c + 3)
                act.activation(W[:, seg % 2, :, bass.ds(g * GT, GT)].rearrange("p j r -> p r j"),
                               WP[:, 0:GT * SEGW].rearrange("p (r j) -> p r j", j=SEGW), ACT.Copy).then_inc(s["W_out"], 1)

            act.sem_inc(s["W_out"], 1)
            with act.Fori(0, SEGW // 2) as i:
                for q in range(2):
                    W_out(i * 2 + q, 0, i * 2 + q)
            u_hi(0, 0, 16)

            def loads(n, k):
                return (n - k % 2) * 8 + 16

            def hidden(n):
                act.wait_ge(s["h_mm"], n + 1)
                act.wait_ge(s["hw"], n + 1)
                act.activation(hg[:], H[:, 0:ROWS], ACT.Gelu_apprx_tanh).then_inc(s["gelu"], 1)

            def body(g, n, j, k, end=False):
                q = k % 2
                act.wait_ge(s["hw"], n + 2)
                act.wait_ge(s["y_mm"], n + 1)
                act.activation(hwh[:, q, 0:ROWS], hw[:], ACT.Copy).then_inc(s["hw_hi"], 1)
                if not end:
                    u_hi(n + 1, (k + 1) % 2, loads(n + 1, k + 1))
                act.wait_ge(s[f"ld_v2{q}"], loads(n, k))
                act.activation(vh[:, q], vs[:, q], ACT.Copy).then_inc(s["v_hi"], 1)
                if not end:
                    hidden(n + 1)
                if g < SEGS - 1:
                    W_out(n + SEGW, g + 1, j)

            hidden(0)
            segments(act, body, lambda n, j, k: body(SEGS - 1, n, j, k, end=(k == UN - 1)))
            for i in range(TILES):
                norm.root(act, i)
                norm.scale(act, i)

        @block.vector
        def _(ve):
            for z in (hwh[:, 1, 0:P], vh[:, 1, 0:512]):
                ve.memset(z.bitcast(F32), 0.0).then_inc(s["zero"], 1)
            ve.wait_ge(s["iota_in"], 16)
            ve.tensor_copy(io[:], iof[:].unsqueeze(2).broadcast_to([P, P, GT])).then_inc(s["iota"], 1)
            ve.wait_ge(s["iota"], 1)
            ve.sem_inc(s["hw"], 1)
            ve.sem_inc(s["hw_lo"], 1)

            def onehots(c, seg, g, q, parts=3):
                r = bass.ds(g * GT, GT)
                ve.wait_ge(s["c_mm"], c + 1)
                ve.tensor_tensor(E[:, q], io[:, 0:SEGW, :], t.i2[:, seg, r].unsqueeze(1).broadcast_to([P, SEGW, GT]), ALU.is_equal).then_inc(s["oh_e"], 1)
                ve.tensor_tensor(A[:, q], io[:], t.i1[:, r].unsqueeze(1).broadcast_to([P, P, GT]), ALU.is_equal)
                ve.wait_ge(s["oh_e"], c + 1)
                ve.tensor_tensor(B[:, q, 0:parts], E[:, q].unsqueeze(1).broadcast_to([P, parts, SEGW, GT]),
                                 t.gp[:, 0:parts, r].unsqueeze(2).broadcast_to([P, parts, SEGW, GT]), ALU.mult).then_inc(s["onehot"], 1)

            def u_lo(n, q):
                ve.wait_ge(s["u_hi"], n + 1)
                ve.tensor_tensor(ul[:, q], us[:, q], uh[:, q].bitcast(F32), ALU.subtract).then_inc(s["u_lo"], 1)

            with ve.Fori(0, SEGW // 2) as i:
                for q in range(2):
                    onehots(i * 2 + q, 0, i * 2 + q, q, 1)
            u_lo(0, 0)

            def body(g, n, j, k, end=False):
                q = k % 2
                if k == 0:
                    ve.wait_ge(s["W_out"], SEGW * (g + 1) + 1)
                ve.wait_ge(s["gelu"], n + 1)
                ve.wait_ge(s["hw_lo"], n + 1)
                ve.tensor_tensor(hw[:], hg[:], W[:, g % 2, bass.ds(j, 1), :].rearrange("p a r -> p (a r)"), ALU.mult).then_inc(s["hw"], 1)
                ve.wait_ge(s["hw_hi"], n + 1)
                ve.tensor_tensor(hwh[:, q, ROWS:HWC], hw[:, SEQ:ROWS], hwh[:, q, SEQ:ROWS].bitcast(F32), ALU.subtract)
                ve.tensor_tensor(hwl[:, q, :], hw[:, 0:SEQ], hwh[:, q, 0:SEQ].bitcast(F32), ALU.subtract).then_inc(s["hw_lo"], 1)
                if not end:
                    u_lo(n + 1, (k + 1) % 2)
                ve.wait_ge(s["v_hi"], n + 1)
                ve.tensor_tensor(vl[:, q], vs[:, q], vh[:, q].bitcast(F32), ALU.subtract).then_inc(s["v_lo"], 1)
                if g < SEGS - 1:
                    onehots(n + SEGW, g + 1, j, q)

            segments(ve, body, lambda n, j, k: body(SEGS - 1, n, j, k, end=(k == UN - 1)))
            ve.wait_ge(s["ld_ln2"], 32)
            for i in range(2):
                ve.wait_ge(s["y_done"], i + 1)
                norm.moments(ve, i)
            norm.factors(ve, 0)
            ve.wait_ge(s["y_done"], 3)
            for h in range(2):
                ve.tensor_copy(us[0:64, 0, 512 * h:512 * (h + 1)], bank(4 + h)[64:P, :]).then_inc(s["y_low"], 1)
            ve.wait_ge(s["y_low"], 2)
            ve.scalar_tensor_tensor(x1(2), us[0:64, 0], 1.0 / ALPHA, x1(2), ALU.mult, ALU.add).then_inc(s["y_low"], 1)
            norm.factors(ve, 1)
            ve.wait_ge(s["y_low"], 3)
            norm.moments(ve, 2)
            norm.gain(ve, 0, 0)
            norm.factors(ve, 2)
            norm.gain(ve, 1, 0)
            norm.gain(ve, 2, 0)

        @block.gpsimd
        def _(gp):
            with gp.Fori(0, SEGW // 2) as i:
                for q in range(2):
                    r = bass.ds((i * 2 + q) * GT, GT)
                    gp.wait_ge(s["oh_e"], i * 2 + (q + 1))
                    gp.tensor_tensor(B[:, q, 1:3], E[:, q].unsqueeze(1).broadcast_to([P, 2, SEGW, GT]),
                                     t.gp[:, 1:3, r].unsqueeze(2).broadcast_to([P, 2, SEGW, GT]), ALU.mult).then_inc(s["onehot_12"], 1)
            with gp.Fori(0, NB) as b:
                one = lambda x: x[bass.ds(b, 1)].rearrange("a p n -> (a p) n")
                for x in range(4):
                    gp.wait_ge(s["v_lo"], b * 14 + (3 * x + 1))
                    r = slice(32 * x, 32 * (x + 1))
                    src = d.a_k[bass.ds(b, 1), r, :, NT:PAST].rearrange("a p c n -> (a p) c n")
                    gp.dma_start(d.keep_ak[bass.ds(b, 1), r].rearrange("a p c n -> (a p) c n"), src).then_inc(s["kept"], 16)
                    gp.wait_ge(s["v_lo"], b * 14 + (3 * x + 2))
                    r = slice(32 * x, min(32 * (x + 1), P - 1))
                    gp.dma_start(one(d.keep_av)[r], one(d.a_v)[32 * x + 1:r.stop + 1]).then_inc(s["kept"], 16)
                gp.wait_ge(s["v_lo"], b * 14 + 13)
                gp.dma_start(one(d.keep_wk), one(d.w_k)[:, NT:512]).then_inc(s["kept"], 16)
                gp.wait_ge(s["v_lo"], b * 14 + 14)
                gp.dma_start(one(d.keep_wv), one(d.w_v)[2:P]).then_inc(s["kept"], 16)
            gp.wait_ge(s["kept"], 16 * 10 * NB)
            for i in range(TILES):
                norm.gain(gp, i, 1)


def constants():
    c0 = np.zeros((P, C0_W), np.float32)
    c0[:, 0:P] = np.eye(P, dtype=np.float32)
    inv = np.power(np.float32(500000.0), -np.arange(HALF, dtype=np.float32) / np.float32(HALF)).astype(np.float32)
    for i in range(TILES):
        pos = (np.arange(P) + P * i) if i < 2 else PAST + np.arange(P) % NT
        ang = pos.astype(np.float32)[:, None] * inv[None, :]
        c0[:, P + HALF * i:P + HALF * (i + 1)] = np.cos(ang)
        c0[:, P + HALF * (TILES + i):P + HALF * (TILES + i + 1)] = np.sin(ang)
    ca = np.zeros((P, CA_W), np.float32)
    many = lambda dist: sum(((dist >= 0) & (dist <= w) & (dist % dil == 0)) for w, dil in ((128, 1), (512, 4), (2048, 16)))
    log = lambda n: np.where(n > 0, np.log(np.maximum(n, 1)), NEG).astype(np.float32)
    mask = lambda ok: np.where(ok, 0.0, NEG).astype(np.float32)
    for i in range(2):
        n = P * (i + 1)
        dist = (np.arange(P) + P * i)[:, None] - np.arange(n)[None, :]
        ca[:, CA_PA + P * i:CA_PA + P * i + n] = log(many(dist))
        ca[:, CA_PC + P * i:CA_PC + P * i + n] = mask(dist >= 0)
        ca[:, CA_PB + NC_P * i:CA_PB + NC_P * (i + 1)] = mask(16 * np.arange(NC_P)[None, :] + 31 <= (np.arange(P) + P * i)[:, None])
    tt = (np.arange(P) % NT)[:, None]
    ca[:, CA_SA:CA_SA + NKA] = log(many(PAST + tt - np.arange(NKA)[None, :]))
    tt = tt[0:64]
    dist = 512 + tt - np.arange(NKW)[None, :]
    ca[0:64, CA_SW:CA_SW + NKW] = mask((dist >= 0) & (dist <= 512))
    ca[0:64, CA_SN:CA_SN + NT] = mask(np.arange(NT)[None, :] <= tt)
    c, j = 16 * np.arange(NC_S)[:, None], 64 * np.arange(NSEL)[None, :]
    ca[0:NC_S, CA_OV:CA_OV + NSEL] = (c < j + 64) & (c + 32 > j)
    r = np.arange(64)
    ca[0:64, CA_GS:CA_GS + 64] = (r[:, None] // 32 == r[None, :] // 32) & (r[:, None] % NT == r[None, :] % NT)
    ca[:, CA_RV:CA_RV + 14] = 13 - np.arange(14)
    return {"c0": c0, "ca": ca, "iota_pairs": np.tile(np.arange(NPAIR, dtype=np.float32), (P, 1)),
            "iota": np.tile(np.arange(P, dtype=np.float32), (P, 1))}


def layouts(x):
    a = {n: np.asarray(v) for n, v in x.items()}
    out = constants()
    rows = np.concatenate([a["x_prompt"].reshape(SEQ, D), a["x_sample"].reshape(NB * NT, D)])
    out["xT"] = rows.reshape(ROWS, KD, P).transpose(2, 1, 0)
    out["x_rows"] = rows
    w = a["w_in"][0]
    cut = np.cumsum([0, 512, 512, 512, 512] + [128] * 6 + [24])
    qa, ka, va, qb, kc, vc, ks, vs, kw, vw, gl = [w[:, cut[i]:cut[i + 1]] for i in range(11)]
    pair = [h for g in range(G) for h in (g, g + G)]
    qb = qb.reshape(D, HEADS, HD)[:, pair].reshape(D, 512)
    blocks = [qb, qa, ka, np.concatenate([ks, kw, gl], 1), np.concatenate([kc, vc, vs, vw], 1), va]
    out["w_in"] = np.concatenate([b.reshape(KD, P, -1).transpose(1, 0, 2).reshape(P, -1) for b in blocks], 1)
    pool = lambda n: a[n][0]
    cp = [pool(n).reshape(80, 8, 8, 2, KVH, HD).transpose(0, 3, 5, 4, 2, 1) for n in ("cache_cmp_k", "cache_cmp_v")]
    out["cmp_pool"] = np.stack([c.reshape(80, P, P) for c in cp], 2).reshape(80, P, 2 * P)
    kp = pool("cache_sel_k").transpose(0, 2, 3, 1).reshape(80, P, P)
    out["sel_pool"] = np.stack([kp, pool("cache_sel_v").reshape(80, P, P)], 2).reshape(80, P, 2 * P)
    out["a_k"] = a["cache_a_k"][0].reshape(NB, PAST, 4, P).transpose(0, 3, 2, 1)
    out["a_v"] = a["cache_a_v"][0].reshape(NB, P, 8 * 512)
    out["w_k"] = a["cache_win_k"][0].reshape(NB, 512, P).transpose(0, 2, 1)
    out["w_v"] = a["cache_win_v"][0].reshape(NB, P, 4 * P)
    wo = a["w_o"][0]
    wo = np.concatenate([wo[0:512], wo[512:].reshape(HEADS, HD, D)[pair].reshape(512, D)])
    out["w_o"] = wo.reshape(KD, P, D).transpose(1, 0, 2)
    for n in ("ln1_g", "ln1_b", "ln2_g", "ln2_b"):
        out[n] = a[n][0]
    out["peer_wq"] = a["peer_wq"][0].reshape(KD, P, HH, P).transpose(2, 1, 0, 3)
    out["peer_keys"] = np.stack([a["peer_k1"][0], a["peer_k2"][0]], 1).reshape(HH, P, P).transpose(2, 0, 1)
    out["peer_u"] = a["peer_u"][0].reshape(P, NE, KD, P).transpose(1, 3, 2, 0).reshape(NE, P, D)
    out["peer_v"] = a["peer_v"][0].reshape(P, NE, D).transpose(1, 0, 2)
    out["page_table"] = a["page_table"].reshape(1, -1)
    for n in "kv":
        out[f"w1{n}"] = a[f"cmp_w1_{n}"][0].reshape(CMP_W1, P, 256).transpose(1, 0, 2)
        out[f"w2{n}"] = a[f"cmp_w2_{n}"][0].reshape(2, P, HD).transpose(1, 0, 2)
    out["pe"] = np.stack([a[f"cmp_pe_{n}"][0].reshape(CMP_W1, P).T for n in "kv"], 1)
    return {n: np.ascontiguousarray(v) for n, v in out.items()}


OUTS = {"o_ak": (ROWS, 512), "o_av": (ROWS, 512), "o_kv": (ROWS, 512), "o_ksw": (ROWS, 256), "o_y": (ROWS, D),
        "keep_ak": (NB, P, 4, PAST - NT), "keep_av": (NB, P - 1, 8 * 512),
        "keep_wk": (NB, P, 512 - NT), "keep_wv": (NB, P - 2, 4 * P)}
SEMS = """x_in0 x_in1 x_in2 x_in3 w_hi w_lo w_used h_low proj w_in0 w_in1 w_in2 c0 w1 evac roped out0 out_kv gate gate_e gate_a turned turned_out rope_c
ptab c16 cmp_slot_free cmp_pg0 cmp_pg1 cmp_bias cmp_turn cmp_rp cmp_hid cmp_gelu cmp_second cmp_done
ca gs ld_ka0 ld_ka1 ld_pg0 ld_pg1 ld_v0 ld_v1 kept diag
p_scores p_masked p_max p_cmax p_csum p_exp p_rec p_fac p_turned p_turned_out p_pv diag_zero p_q p_weighed p_OT
s_scores s_read s_max s_exp s_rec s_fac s_turned s_turned_out s_pv s_sel_used s_branch s_normed s_out_turned s_OT i_pc i_mm i_dve i_sel i_pen
ld_wo0 ld_wo1 ld_xr ld_ky ld_wq0 ld_wq1 ld_wq2 ld_wq3 o_mm x_turn x_out x_hi x_lo q_mm q_out sc_mm sc_out
ln_sum ln_st ln_mean ln_var ln_root ln_fac ln_scaled ln_lg ln_l ln_rg ln_r top topr topb top2 ixf be ber beb bei pr128 pair pair_v bf g_sub g_exp g_den g_fin
id_eq id_mul id_sum id_turn id_out split
y_done ld_u0 ld_u1 ld_v20 ld_v21 ld_ln2 y_low u_hi u_lo v_hi v_lo h_mm gelu hw hw_hi hw_lo y_mm
c_mm W_out onehot onehot_12 oh_e zero iota iota_in st_y""".split()


def build(nc, d, upto=9):
    with ExitStack() as ctx:
        sb = lambda n, sh, dt=F32: ctx.enter_context(nc.sbuf_tensor(n, sh, dt))
        s = {n: ctx.enter_context(nc.semaphore(n)) for n in SEMS}
        t = Names()
        t.psum = ctx.enter_context(nc.psum_tensor("psum", [P, 8, 512], F32))
        t.c0 = sb("c0", [P, C0_W])
        t.OT = sb("OT", [P, KD, ROWS])
        t.big = sb("big", [P, KD * D])
        att = ctx.enter_context(ExitStack())
        ab = lambda n, sh, dt=F32: att.enter_context(nc.sbuf_tensor(n, sh, dt))
        t.hk = ab("h_keep", [P, TILES, HK_W])
        t.TT = ab("qk_turned", [P, NTT, ROWS])
        t.gates = ab("gates", [P, TILES, 24])
        t.kc = ab("kc", [P, NB + 1, NC_S])
        t.vc = ab("vc", [NC_S, NB + 1, P])
        t.ptab = ab("ptab", [1, NB * PAGES], I32)
        t.ca = ab("att_consts", [P, CA_W])
        t.gs = ab("gates_ht", [64, NB, 3])
        with ExitStack() as c1:
            cb = lambda n, sh, dt=F32: c1.enter_context(nc.sbuf_tensor(n, sh, dt))
            t.w1k, t.w1v = cb("w1k", [P, CMP_W1, 256]), cb("w1v", [P, CMP_W1, 256])
            w2 = t.big[:, BIG_W2:BIG_PE].rearrange("p (a h n) -> p a h n", a=2, h=2)
            t.w2k, t.w2v = w2[:, 0], w2[:, 1]
            t.pe = t.big[:, BIG_PE:BIG_END].rearrange("p (a c) -> p a c", a=2)
            t.cpg = cb("cmp_pages", [P, 2, PAGES + 3, 2, KVH, 8, 8])
            project_block(nc, d, t, s)
            compress_block(nc, d, t, s)
        attention_block(nc, d, t, s)
        att.close()
        t.x1 = sb("x1", [P, TILES, D])
        t.x1h, t.x1l = sb("x1_hi", [P, KD, ROWS], F32R), sb("x1_lo", [P, KD, ROWS], F32R)
        t.i1 = sb("i1", [P, ROWS], BF16)
        t.i2 = sb("i2", [P, SEGS, ROWS], BF16)
        t.gp = sb("gate_parts", [P, 3, ROWS], BF16)
        route_block(nc, d, t, s)
        expert_block(nc, d, t, s)


def kernel(**inputs):
    import concourse.bacc as bacc
    from concourse.bass_utils import run_bass_kernel_spmd

    nc = bacc.Bacc("TRN2", target_bir_lowering=False, num_devices=1)
    arrays = layouts(inputs)
    d = Names()
    for n, v in arrays.items():
        d.__dict__[n] = nc.dram_tensor("in_" + n, v.shape, mybir.dt.from_np(v.dtype), kind="ExternalInput").ap()
    for n, shape in OUTS.items():
        d.__dict__[n] = nc.dram_tensor(n, shape, F32, kind="ExternalOutput").ap()
    d.gate_rows = nc.dram_tensor("gate_rows", (NB * NT, 24), F32, kind="Internal").ap()
    build(nc, d)
    r = run_bass_kernel_spmd(nc, [{"in_" + n: v for n, v in arrays.items()}], core_ids=[0]).results[0]
    o = {n: r[n] for n in OUTS}
    new = lambda a: a[SEQ:].reshape(1, NB, NT, -1, HD)
    old = lambda a: a[:SEQ].reshape(1, 1, SEQ, -1, HD)
    kc, vc, vs, vw = [o["o_kv"][:, P * i:P * (i + 1)] for i in range(4)]
    ks, kw = o["o_ksw"][:, 0:P], o["o_ksw"][:, P:2 * P]
    join = lambda kept, fresh: np.concatenate([kept, new(fresh)], 2)
    a_k = o["keep_ak"].transpose(0, 3, 2, 1).reshape(1, NB, PAST - NT, HEADS, HD)
    a_v = o["keep_av"].reshape(1, NB, PAST - NT, HEADS, HD)
    w_k = o["keep_wk"].transpose(0, 2, 1).reshape(1, NB, 512 - NT, KVH, HD)
    w_v = o["keep_wv"].reshape(1, NB, 512 - NT, KVH, HD)
    y = o["o_y"]
    return (y[:SEQ].reshape(1, SEQ, D), y[SEQ:].reshape(NB, NT, D),
            old(o["o_ak"]), old(o["o_av"]), old(kc), old(vc), old(ks), old(vs), old(kw), old(vw),
            join(a_k, o["o_ak"]), join(a_v, o["o_av"]), new(kc), new(vc), new(ks), new(vs),
            join(w_k, kw), join(w_v, vw))
```
